# Optimizing a Trainium2 kernel written in Bass

```python
import math
import numpy as np
import jax
import jax.numpy as jnp
from jax import lax

D_MODEL = 1024
BATCH = 1
SEQ = 1024
DEPTH = 1
DEC_BATCH = 8
DEC_SEQ = 1
PAST_LEN = 8192
PAGE_SIZE = 128

NSA_HEADS = 8
NSA_KV_HEADS = 2
NSA_HPG = NSA_HEADS // NSA_KV_HEADS
HEAD_DIM = 64
NSA_WIDTH = NSA_HEADS * HEAD_DIM
CMP_BLOCK = 32
CMP_STRIDE = 16
CMP_HID = 256
SEL_BLOCK = 64
SEL_TOPN = 16
WINDOW = 512
Q_BLOCK = 64
MLSTM_HEADS = 4
MLSTM_DK = 128
MLSTM_DV = 128
MLSTM_WIDTH = MLSTM_HEADS * MLSTM_DV
MLSTM_CHUNK = 64
FFN_HIDDEN = ((8 * D_MODEL + 3 * 256 - 1) // (3 * 256)) * 256
REL_BUCKETS = 32
REL_MAX_DIST = 1024
N_KV_GROUPS = 6
OFF_QA = 0
OFF_KVA = OFF_QA + NSA_WIDTH
OFF_GA = OFF_KVA + N_KV_GROUPS * NSA_KV_HEADS * HEAD_DIM
OFF_QB = OFF_GA + 3 * NSA_HEADS
OFF_KB = OFF_QB + MLSTM_HEADS * MLSTM_DK
OFF_VB = OFF_KB + MLSTM_HEADS * MLSTM_DK
OFF_IFB = OFF_VB + MLSTM_WIDTH
OFF_OB = OFF_IFB + 2 * MLSTM_HEADS
OFF_MG = OFF_OB + MLSTM_WIDTH
N_IN = OFF_MG + 2 * D_MODEL
NEG = -1e30
BIG = 1e9
EPS = 1e-6

kernel_name = 'nsa_mlstm_gated_hybrid_step'

def rmsnorm(x, g):
    xf = x.astype(jnp.float32)
    y = xf * lax.rsqrt(jnp.mean(xf * xf, axis=-1, keepdims=True) + EPS)
    return (y * g.astype(jnp.float32)).astype(x.dtype)

def modulate(h, shift, scale):
    return h * (1.0 + scale[:, None, :]) + shift[:, None, :]

def head_norm(h, g):
    hf = h.astype(jnp.float32)
    mu = jnp.mean(hf, axis=-1, keepdims=True)
    var = jnp.mean(jnp.square(hf - mu), axis=-1, keepdims=True)
    y = (hf - mu) * lax.rsqrt(var + EPS)
    return y.reshape(h.shape[:2] + (-1,)) * g.astype(jnp.float32)

def rel_bucket(dist):
    exact = REL_BUCKETS // 2
    d = jnp.maximum(dist, 0)
    df = jnp.maximum(d, exact).astype(jnp.float32)
    large = exact + (jnp.log(df / exact) / math.log(REL_MAX_DIST / exact) * (REL_BUCKETS - exact)).astype(jnp.int32)
    large = jnp.minimum(large, REL_BUCKETS - 1)
    return jnp.where(d < exact, d, large)

def masked_softmax(s, mask):
    s = jnp.where(mask, s.astype(jnp.float32), NEG)
    m = jnp.max(s, axis=-1, keepdims=True)
    e = jnp.where(mask, jnp.exp(s - m), 0.0)
    return e / jnp.maximum(jnp.sum(e, axis=-1, keepdims=True), 1e-30)

def compress(kv, pe, w1, w2):
    b, t = kv.shape[:2]
    r = CMP_BLOCK // CMP_STRIDE
    n_c = (t - CMP_BLOCK) // CMP_STRIDE + 1
    pieces = kv[:, :(n_c + r - 1) * CMP_STRIDE].reshape(b, n_c + r - 1, CMP_STRIDE, NSA_KV_HEADS, HEAD_DIM)
    pe_r = pe.reshape(r, CMP_STRIDE, HEAD_DIM)
    w1_r = w1.reshape(r, CMP_STRIDE, HEAD_DIM, CMP_HID)
    hid = sum(jnp.einsum('bncgd,cdf->bngf', pieces[:, p:p + n_c] + pe_r[p][:, None, :], w1_r[p]) for p in range(r))
    return jnp.einsum('bngf,fd->bngd', jax.nn.gelu(hid), w2)

def compress_kv(k, v, p):
    kc = compress(k, p['cmp_pe'][0], p['cmp_w1'][0], p['cmp_w2'][0])
    vc = compress(v, p['cmp_pe'][1], p['cmp_w1'][1], p['cmp_w2'][1])
    cend = jnp.arange(kc.shape[1]) * CMP_STRIDE + CMP_BLOCK - 1
    return kc, vc, cend

def block_cover(n_c, n_sel):
    i = np.arange(n_c)[:, None]
    j = np.arange(n_sel)[None, :]
    start = i * CMP_STRIDE
    end = start + CMP_BLOCK - 1
    return ((start <= j * SEL_BLOCK + SEL_BLOCK - 1) & (end >= j * SEL_BLOCK)).astype(np.float32)

def sel_blocks(k):
    b, t = k.shape[:2]
    n_sel = -(-t // SEL_BLOCK)
    k = jnp.pad(k, ((0, 0), (0, n_sel * SEL_BLOCK - t), (0, 0), (0, 0)))
    return jnp.transpose(k.reshape(b, n_sel, SEL_BLOCK, NSA_KV_HEADS, HEAD_DIM), (0, 3, 1, 2, 4))

def nsa_core(q, qpos, gates, kc, vc, cend, ks_blk, vs_blk, kw, vw, wpos, rel_bias):
    b, tq = q.shape[:2]
    n_c = kc.shape[1]
    n_sel = ks_blk.shape[2]
    qg = q.reshape(b, tq, NSA_KV_HEADS, NSA_HPG, HEAD_DIM)
    table = rel_bias.reshape(REL_BUCKETS, NSA_KV_HEADS, NSA_HPG)
    dist_c = qpos[:, None] - cend[None, :]
    bias_c = jnp.transpose(table[rel_bucket(dist_c)], (0, 2, 3, 1))
    s_c = jnp.einsum('btghd,bngd->btghn', qg, kc) + bias_c
    p_c = masked_softmax(s_c, (dist_c >= 0)[:, None, None, :])
    o_c = jnp.einsum('btghn,bngd->btghd', p_c.astype(vc.dtype), vc)
    imp = jnp.einsum('btgn,nj->btgj', jnp.sum(p_c, axis=3), jnp.asarray(block_cover(n_c, n_sel)))
    jblk = jnp.arange(n_sel)
    cur = (qpos // SEL_BLOCK)[:, None]
    forced = ((jblk == 0) | (jblk == cur) | (jblk == cur - 1))[:, None, :]
    valid = (jblk * SEL_BLOCK <= qpos[:, None])[:, None, :]
    score = jnp.where(valid, jnp.where(forced, BIG, imp), NEG)
    _, idx = lax.top_k(score, min(SEL_TOPN, n_sel))
    bi = jnp.arange(b)[:, None, None, None]
    gi = jnp.arange(NSA_KV_HEADS)[None, None, :, None]
    k_sel = ks_blk[bi, gi, idx].reshape(b, tq, NSA_KV_HEADS, -1, HEAD_DIM)
    v_sel = vs_blk[bi, gi, idx].reshape(b, tq, NSA_KV_HEADS, -1, HEAD_DIM)
    kpos = (idx[..., None] * SEL_BLOCK + jnp.arange(SEL_BLOCK)).reshape(b, tq, NSA_KV_HEADS, -1)
    dist_s = qpos[None, :, None, None] - kpos
    bias_s = jnp.swapaxes(jnp.transpose(table, (1, 0, 2))[gi, rel_bucket(dist_s)], -1, -2)
    s_s = jnp.einsum('btghd,btgkd->btghk', qg, k_sel) + bias_s
    p_s = masked_softmax(s_s, (dist_s >= 0)[:, :, :, None, :])
    o_s = jnp.einsum('btghk,btgkd->btghd', p_s.astype(v_sel.dtype), v_sel)
    dist_w = qpos[:, None] - wpos[None, :]
    mask_w = ((dist_w >= 0) & (dist_w < WINDOW) & (wpos >= 0)[None, :])[:, None, None, :]
    bias_w = jnp.transpose(table[rel_bucket(dist_w)], (0, 2, 3, 1))
    s_w = jnp.einsum('btghd,bsgd->btghs', qg, kw) + bias_w
    p_w = masked_softmax(s_w, mask_w)
    o_w = jnp.einsum('btghs,bsgd->btghd', p_w.astype(vw.dtype), vw)
    shp = (b, tq, NSA_HEADS, HEAD_DIM)
    return gates[..., 0:1] * o_c.reshape(shp) + gates[..., 1:2] * o_s.reshape(shp) + gates[..., 2:3] * o_w.reshape(shp)

def mlstm_chunkwise(q, k, v, i_pre, f_pre, c0, n0, m0):
    b, t, h, dk = q.shape
    L = MLSTM_CHUNK if t % MLSTM_CHUNK == 0 else t
    nc = t // L

    def chunks(a):
        a = a.astype(jnp.float32).reshape((b, nc, L) + a.shape[2:])
        return jnp.moveaxis(jnp.moveaxis(a, 1, 0), 3, 2)

    causal = jnp.tril(jnp.ones((L, L), dtype=bool))

    def step(carry, inp):
        c_st, n_st, m_st = carry
        qc, kc, vc, ic, fc = inp
        bcum = jnp.cumsum(jax.nn.log_sigmoid(fc), axis=-1)
        a_inter = bcum + m_st[..., None]
        dmat = jnp.where(causal, bcum[..., :, None] - bcum[..., None, :] + ic[..., None, :], NEG)
        m_t = jnp.maximum(a_inter, jnp.max(dmat, axis=-1))
        w_inter = jnp.exp(a_inter - m_t)
        sw = jnp.einsum('bhld,bhsd->bhls', qc, kc) * jnp.exp(dmat - m_t[..., None])
        num = w_inter[..., None] * jnp.einsum('bhld,bhde->bhle', qc, c_st) + jnp.einsum('bhls,bhse->bhle', sw, vc)
        den = w_inter * jnp.einsum('bhld,bhd->bhl', qc, n_st) + jnp.sum(sw, axis=-1)
        h_out = num / jnp.maximum(jnp.abs(den), jnp.exp(-m_t))[..., None]
        b_last = bcum[..., -1]
        g_s = b_last[..., None] - bcum + ic
        m_new = jnp.maximum(b_last + m_st, jnp.max(g_s, axis=-1))
        w_c = jnp.exp(b_last + m_st - m_new)
        w_s = jnp.exp(g_s - m_new[..., None])
        c_new = w_c[..., None, None] * c_st + jnp.einsum('bhl,bhld,bhle->bhde', w_s, kc, vc)
        n_new = w_c[..., None] * n_st + jnp.einsum('bhl,bhld->bhd', w_s, kc)
        return (c_new, n_new, m_new), h_out

    xs = (chunks(q), chunks(k) * (dk ** -0.5), chunks(v), chunks(i_pre), chunks(f_pre))
    init = (c0.astype(jnp.float32), n0.astype(jnp.float32), m0.astype(jnp.float32))
    (c_f, n_f, m_f), hs = lax.scan(step, init, xs)
    return jnp.transpose(hs, (1, 0, 3, 2, 4)).reshape(b, t, h, -1), c_f, n_f, m_f

def mixer_input(x, c, p):
    b, t = x.shape[:2]
    mod = (c @ p['w_ada'] + p['b_ada']).reshape(b, 6, D_MODEL)
    u = modulate(rmsnorm(x, p['norm_mix_g']), mod[:, 0], mod[:, 1])
    z = u @ p['w_in']
    q_a = z[..., OFF_QA:OFF_KVA].reshape(b, t, NSA_HEADS, HEAD_DIM) * (HEAD_DIM ** -0.5)
    kv_a = z[..., OFF_KVA:OFF_GA].reshape(b, t, N_KV_GROUPS, NSA_KV_HEADS, HEAD_DIM)
    g_a = jax.nn.sigmoid(z[..., OFF_GA:OFF_QB].reshape(b, t, NSA_HEADS, 3))
    q_b = z[..., OFF_QB:OFF_KB].reshape(b, t, MLSTM_HEADS, MLSTM_DK)
    k_b = z[..., OFF_KB:OFF_VB].reshape(b, t, MLSTM_HEADS, MLSTM_DK)
    v_b = z[..., OFF_VB:OFF_IFB].reshape(b, t, MLSTM_HEADS, MLSTM_DV)
    if_b = (z[..., OFF_IFB:OFF_OB] + p['mlstm_gate_b']).reshape(b, t, 2, MLSTM_HEADS)
    o_b = jax.nn.sigmoid(z[..., OFF_OB:OFF_MG])
    g_m = jax.nn.sigmoid(z[..., OFF_MG:N_IN]).reshape(b, t, 2, D_MODEL)
    return mod, q_a, kv_a, g_a, q_b, k_b, v_b, if_b, o_b, g_m

def mixer_output_and_ffn(x, mod, o_a, h_b, o_b, g_m, p):
    b, t = x.shape[:2]
    br_a = o_a.reshape(b, t, NSA_WIDTH).astype(x.dtype) @ p['w_branch_a']
    br_b = (o_b.astype(jnp.float32) * head_norm(h_b, p['mlstm_norm_g'])).astype(x.dtype) @ p['w_branch_b']
    mixed = g_m[:, :, 0] * br_a + g_m[:, :, 1] * br_b
    x = x + mod[:, 2][:, None, :] * (mixed @ p['w_out'])
    u = modulate(rmsnorm(x, p['norm_ffn_g']), mod[:, 3], mod[:, 4])
    gate, up = jnp.split(u @ p['w_ffn_in'], 2, axis=-1)
    return x + mod[:, 5][:, None, :] * ((jax.nn.silu(gate) * up) @ p['w_ffn_out'])

def prompt_layer(x, c, rel_bias, p):
    b, t = x.shape[:2]
    mod, q_a, kv_a, g_a, q_b, k_b, v_b, if_b, o_b, g_m = mixer_input(x, c, p)
    kc, vc, cend = compress_kv(kv_a[:, :, 0], kv_a[:, :, 1], p)
    ks_blk = sel_blocks(kv_a[:, :, 2])
    vs_blk = sel_blocks(kv_a[:, :, 3])
    pad = ((0, 0), (WINDOW, 0), (0, 0), (0, 0))
    kw_pad = jnp.pad(kv_a[:, :, 4], pad)
    vw_pad = jnp.pad(kv_a[:, :, 5], pad)
    band = WINDOW + Q_BLOCK

    def query_block(j):
        q0 = j * Q_BLOCK
        return nsa_core(lax.dynamic_slice_in_dim(q_a, q0, Q_BLOCK, axis=1), q0 + jnp.arange(Q_BLOCK),
                        lax.dynamic_slice_in_dim(g_a, q0, Q_BLOCK, axis=1), kc, vc, cend, ks_blk, vs_blk,
                        lax.dynamic_slice_in_dim(kw_pad, q0, band, axis=1),
                        lax.dynamic_slice_in_dim(vw_pad, q0, band, axis=1),
                        q0 - WINDOW + jnp.arange(band), rel_bias)

    o_a = lax.map(query_block, jnp.arange(t // Q_BLOCK))
    o_a = jnp.moveaxis(o_a, 0, 1).reshape(b, t, NSA_HEADS, HEAD_DIM)
    c0 = jnp.zeros((b, MLSTM_HEADS, MLSTM_DK, MLSTM_DV), jnp.float32)
    n0 = jnp.zeros((b, MLSTM_HEADS, MLSTM_DK), jnp.float32)
    m0 = jnp.zeros((b, MLSTM_HEADS), jnp.float32)
    h_b, c_new, n_new, m_new = mlstm_chunkwise(q_b, k_b, v_b, if_b[:, :, 0], if_b[:, :, 1], c0, n0, m0)
    y = mixer_output_and_ffn(x, mod, o_a, h_b, o_b, g_m, p)
    keep = min(WINDOW, t)
    return y, kv_a[:, :, :4], kv_a[:, t - keep:, 4:], c_new, n_new, m_new

def sample_layer(x, c, kv_pages, page_table, win_buf, c0, n0, m0, rel_bias, p):
    b, t = x.shape[:2]
    mod, q_a, kv_a, g_a, q_b, k_b, v_b, if_b, o_b, g_m = mixer_input(x, c, p)
    past = kv_pages[page_table]
    past = past.reshape((b, -1) + past.shape[3:])
    past_len = past.shape[1]
    full = jnp.concatenate([past, kv_a[:, :, :4].astype(past.dtype)], axis=1)
    kc, vc, cend = compress_kv(full[:, :, 0], full[:, :, 1], p)
    win = jnp.concatenate([win_buf, kv_a[:, :, 4:].astype(win_buf.dtype)], axis=1)
    wpos = past_len - win_buf.shape[1] + jnp.arange(win.shape[1])
    qpos = past_len + jnp.arange(t)
    o_a = nsa_core(q_a, qpos, g_a, kc, vc, cend, sel_blocks(full[:, :, 2]), sel_blocks(full[:, :, 3]),
                   win[:, :, 0], win[:, :, 1], wpos, rel_bias)
    h_b, c_new, n_new, m_new = mlstm_chunkwise(q_b, k_b, v_b, if_b[:, :, 0], if_b[:, :, 1], c0, n0, m0)
    y = mixer_output_and_ffn(x, mod, o_a, h_b, o_b, g_m, p)
    keep = min(WINDOW, win.shape[1])
    return y, kv_a[:, :, :4], win[:, win.shape[1] - keep:], c_new, n_new, m_new

def final_norm(x, c, w, bvec, g):
    mod = (c @ w + bvec).reshape(c.shape[0], 2, D_MODEL)
    return modulate(rmsnorm(x, g), mod[:, 0], mod[:, 1])

def setup_inputs(seed: int = 0) -> dict:
    key = jax.random.key(seed)
    k = jax.random.split(key, 30)
    f32 = jnp.float32

    def nrm(kk, shape, scale):
        return scale * jax.random.normal(kk, shape, f32)

    d = D_MODEL
    n_pages = PAST_LEN // PAGE_SIZE
    n_used = DEC_BATCH * n_pages
    n_pool = n_used + (n_used + 3) // 4
    wb = min(WINDOW, PAST_LEN)
    page_table = jax.random.permutation(k[0], n_pool)[:n_used].reshape(DEC_BATCH, n_pages).astype(jnp.int32)
    gate_b = jnp.concatenate([nrm(k[1], (DEPTH, MLSTM_HEADS), 0.1),
                              jnp.linspace(3.0, 6.0, MLSTM_HEADS, dtype=f32)[None, :] + nrm(k[2], (DEPTH, MLSTM_HEADS), 0.1)], axis=-1)
    return {
        'x_prompt': nrm(k[3], (BATCH, SEQ, d), 1.0),
        'x_sample': nrm(k[4], (DEC_BATCH, DEC_SEQ, d), 1.0),
        'c_prompt': nrm(k[5], (BATCH, d), 1.0),
        'c_sample': nrm(k[6], (DEC_BATCH, d), 1.0),
        'cache_nsa_kv': nrm(k[7], (DEPTH, n_pool, PAGE_SIZE, 4, NSA_KV_HEADS, HEAD_DIM), 1.0),
        'cache_nsa_win': nrm(k[8], (DEPTH, DEC_BATCH, wb, 2, NSA_KV_HEADS, HEAD_DIM), 1.0),
        'state_mlstm_C': nrm(k[9], (DEPTH, DEC_BATCH, MLSTM_HEADS, MLSTM_DK, MLSTM_DV), 0.1),
        'state_mlstm_n': nrm(k[10], (DEPTH, DEC_BATCH, MLSTM_HEADS, MLSTM_DK), 0.1),
        'state_mlstm_m': nrm(k[11], (DEPTH, DEC_BATCH, MLSTM_HEADS), 1.0),
        'page_table': page_table,
        'rel_bias': nrm(k[12], (REL_BUCKETS, NSA_HEADS), 0.5),
        'w_ada': nrm(k[13], (DEPTH, d, 6 * d), 0.3 * d ** -0.5),
        'b_ada': nrm(k[14], (DEPTH, 6 * d), 0.02),
        'norm_mix_g': 1.0 + nrm(k[15], (DEPTH, d), 0.02),
        'norm_ffn_g': 1.0 + nrm(k[16], (DEPTH, d), 0.02),
        'w_in': nrm(k[17], (DEPTH, d, N_IN), d ** -0.5),
        'mlstm_gate_b': gate_b,
        'cmp_pe': nrm(k[18], (DEPTH, 2, CMP_BLOCK, HEAD_DIM), 0.1),
        'cmp_w1': nrm(k[19], (DEPTH, 2, CMP_BLOCK, HEAD_DIM, CMP_HID), (CMP_BLOCK * HEAD_DIM) ** -0.5),
        'cmp_w2': nrm(k[20], (DEPTH, 2, CMP_HID, HEAD_DIM), CMP_HID ** -0.5),
        'mlstm_norm_g': 1.0 + nrm(k[21], (DEPTH, MLSTM_WIDTH), 0.02),
        'w_branch_a': nrm(k[22], (DEPTH, NSA_WIDTH, d), NSA_WIDTH ** -0.5),
        'w_branch_b': nrm(k[23], (DEPTH, MLSTM_WIDTH, d), MLSTM_WIDTH ** -0.5),
        'w_out': nrm(k[24], (DEPTH, d, d), d ** -0.5),
        'w_ffn_in': nrm(k[25], (DEPTH, d, 2 * FFN_HIDDEN), d ** -0.5),
        'w_ffn_out': nrm(k[26], (DEPTH, FFN_HIDDEN, d), FFN_HIDDEN ** -0.5),
        'w_ada_final': nrm(k[27], (d, 2 * d), 0.3 * d ** -0.5),
        'b_ada_final': nrm(k[28], (2 * d,), 0.02),
        'norm_final_g': 1.0 + nrm(k[29], (d,), 0.02),
    }

def reference(x_prompt, x_sample, c_prompt, c_sample, cache_nsa_kv, cache_nsa_win, state_mlstm_C, state_mlstm_n,
              state_mlstm_m, page_table, rel_bias, w_ada, b_ada, norm_mix_g, norm_ffn_g, w_in, mlstm_gate_b,
              cmp_pe, cmp_w1, cmp_w2, mlstm_norm_g, w_branch_a, w_branch_b, w_out, w_ffn_in, w_ffn_out,
              w_ada_final, b_ada_final, norm_final_g):
    xp = x_prompt
    xs = x_sample
    st_p = []
    st_s = []
    for l in range(DEPTH):
        p = {'w_ada': w_ada[l], 'b_ada': b_ada[l], 'norm_mix_g': norm_mix_g[l], 'norm_ffn_g': norm_ffn_g[l],
             'w_in': w_in[l], 'mlstm_gate_b': mlstm_gate_b[l], 'cmp_pe': cmp_pe[l], 'cmp_w1': cmp_w1[l],
             'cmp_w2': cmp_w2[l], 'mlstm_norm_g': mlstm_norm_g[l], 'w_branch_a': w_branch_a[l],
             'w_branch_b': w_branch_b[l], 'w_out': w_out[l], 'w_ffn_in': w_ffn_in[l], 'w_ffn_out': w_ffn_out[l]}
        xp, kv_pl, win_pl, c_pl, n_pl, m_pl = prompt_layer(xp, c_prompt, rel_bias, p)
        xs, kv_sl, win_sl, c_sl, n_sl, m_sl = sample_layer(xs, c_sample, cache_nsa_kv[l], page_table, cache_nsa_win[l],
                                                          state_mlstm_C[l], state_mlstm_n[l], state_mlstm_m[l], rel_bias, p)
        st_p.append((kv_pl, win_pl, c_pl, n_pl, m_pl))
        st_s.append((kv_sl, win_sl, c_sl, n_sl, m_sl))
    kv_p, win_p, c_p, n_p, m_p = [jnp.stack(a) for a in zip(*st_p)]
    kv_s, win_s, c_s, n_s, m_s = [jnp.stack(a) for a in zip(*st_s)]
    y_prompt = final_norm(xp, c_prompt, w_ada_final, b_ada_final, norm_final_g)
    y_sample = final_norm(xs, c_sample, w_ada_final, b_ada_final, norm_final_g)
    return (y_prompt, y_sample, kv_p, kv_s, win_p, win_s, c_p, n_p, m_p, c_s, n_s, m_s)


_drawn_inputs = setup_inputs


def setup_inputs(seed=0):
    import zlib

    import numpy as np

    out = dict(_drawn_inputs(seed))
    spreads = {}
    factors = {'cache_nsa_kv': 8.0,
     'rel_bias': 5.357,
     'norm_ffn_g': 8.0,
     'cmp_pe': 8.0,
     'mlstm_norm_g': 28.418,
     'norm_final_g': 24.582,
     'b_ada_final': 2.731}
    for name, (base, spread) in spreads.items():
        noise = np.random.default_rng([zlib.crc32(name.encode()), seed]).standard_normal(out[name].shape)
        drawn = base * np.exp(spread * noise) if base else spread * noise
        out[name] = jnp.asarray(drawn.astype(out[name].dtype))
    for name, factor in factors.items():
        out[name] = (out[name] * factor).astype(out[name].dtype)
    return out
```

```python
from contextlib import ExitStack

import numpy as np
import concourse.bass as bass
from concourse import mybir

F32 = mybir.dt.float32
I32 = mybir.dt.int32
U32 = mybir.dt.uint32
ALU = mybir.AluOpType
ACT = mybir.ActivationFunctionType
AX = mybir.AxisListType

P = 128
D = 1024
T = 1024
B = 8
TT = T + B
DK = D // P
NTI = T // P
GT = TT // 3
NG = 3
H = 8
G = 2
HPG = 4
HD = 64
PAST = 8192
PAGE = 128
NPAGES = PAST // PAGE
POOL = 640
STRIDE = 16
NPIECE = PAST // STRIDE
NCMP = NPIECE - 1
NCP = T // STRIDE - 1
CH = 256
SEL = 64
TOPN = 16
WIN = 512
MH = 4
MD = 128
FF = 2816
NBUCKET = 32
OFF_QA, OFF_KVA = 0, 512
OFF_GA = OFF_KVA + 768
OFF_QB = OFF_GA + 24
OFF_KB = OFF_QB + 512
OFF_VB = OFF_KB + 512
OFF_IFB = OFF_VB + 512
OFF_OB = OFF_IFB + 8
OFF_MG = OFF_OB + 512
NIN = OFF_MG + 2 * D
NEG = -1e30
FLOOR = -1e20
EPS = 1e-6
BUCKET_START = [*range(16), 16, 21, 27, 35, 46, 59, 77, 99, 128, 166, 216, 280, 363, 470, 609, 790]
NREV = 8320
NFWD = 1152

VEC = {"b_ada": (0, 48), "b_ada_final": (48, 16), "norm_mix_g": (64, 8), "norm_ffn_g": (72, 8),
       "norm_final_g": (80, 8), "mlstm_norm_g": (88, 4)}
NVEC = 92


class Chain:

    def __init__(self, eng, sem, base=0):
        self.eng, self.sem, self.base, self.n, self.per = eng, sem, base, 0, None

    def start(self, i, per):
        self.i, self.per, self.n = i, per, 0

    def step(self, ins):
        ins.then_inc(self.sem, 1)
        self.n += 1

    def link(self, ins):
        self.step(ins)
        if self.per is None:
            self.eng.wait_ge(self.sem, self.base + self.n)
        else:
            self.eng.wait_ge(self.sem, self.i * self.per + self.base + self.n)

    def done(self):
        assert self.per == self.n, (self.per, self.n)


class Core:

    def __init__(self, nc, ins, outs):
        self.nc, self.i, self.o = nc, ins, outs
        self.ctx = ExitStack()
        self.stage_sems = []

    def sem(self, name):
        self.stage_sems.append(self.nc.alloc_semaphore(name=name))
        return self.stage_sems[-1]

    def stage_done(self):
        self.nc.clear_and_free_semaphores(self.stage_sems)
        self.nc.all_engine_barrier()
        self.stage_sems = []

    def sb(self, name, shape, dt=F32, ctx=None):
        return (ctx or self.ctx).enter_context(self.nc.sbuf_tensor(name, shape, dt))

    def ps(self, name, shape):
        return self.ctx.enter_context(self.nc.psum_tensor(name, shape, F32))

    def dram(self, name, shape, dt=F32):
        return self.nc.dram_tensor(name, shape, dt).ap()


def shared_buffers(k):
    k.bank = [k.ps(f"bank{n}", [P, 512]) for n in range(8)]
    k.ident = k.sb("ident", [P, P])
    k.ones = k.sb("ones", [P, P])
    k.vecT = k.sb("vecT", [P, NVEC])
    k.modT = k.sb("modT", [P, 64, 9])
    k.modA = k.sb("modA", [P, 3, DK, 9])
    k.biasfwd_d = k.dram("biasfwd_d", (H, NFWD))
    k.biasrev_d = k.dram("biasrev_d", (B * H, NREV))
    k.smalltok_d = k.dram("smalltok_d", (B, 32))


def conditioning(k):
    nc = k.nc
    s_const, s_rows, s_vec = k.sem("s_const"), k.sem("s_rows"), k.sem("s_vec")
    s_cT, s_cTs, s_mod, s_modrow = k.sem("s_cT"), k.sem("s_cTs"), k.sem("s_mod"), k.sem("s_modrow")
    s_w = [k.sem(f"s_wada{j}") for j in range(4)]
    s_modT, s_modA = k.sem("s_modT"), k.sem("s_modA")
    with ExitStack() as ctx:
        crow = k.sb("crow", [9, D], ctx=ctx)
        vrow = k.sb("vrow", [NVEC, P], ctx=ctx)
        cT = k.sb("cT", [P, DK, 9], ctx=ctx)
        modrow = k.sb("modrow", [9, 8 * D], ctx=ctx)
        wada = k.sb("wada", [P, 4, DK, 512], ctx=ctx)
        w_v = k.i["w_ada"][0].rearrange("(k p) n -> p k n", p=P)
        wf_v = k.i["w_ada_final"].rearrange("(k p) n -> p k n", p=P)
        block = ctx.enter_context(nc.Block())

        @block.sync
        def _(sp):
            sp.dma_start(crow[0:1, :], k.i["c_prompt"]).then_inc(s_rows, 16)
            sp.dma_start(crow[1:9, :], k.i["c_sample"]).then_inc(s_rows, 16)
            for j in range(4):
                sp.dma_start(wada[:, j], w_v[:, :, 512 * j:512 * j + 512]).then_inc(s_w[j], 16)
            for name, (r, n) in VEC.items():
                a = k.i[name]
                a = a[0] if len(a.shape) == 2 else a
                sp.dma_start(vrow[r:r + n, :], a.rearrange("(r p) -> r p", p=P)).then_inc(s_vec, 16)
            with sp.Fori(1, 3) as i:
                for j in range(4):
                    sp.wait_ge(s_mod, i * 4 + (j - 3))
                    sp.dma_start(wada[:, j], w_v[:, :, bass.ds(i * 2048 + 512 * j, 512)]).then_inc(s_w[j], 16)
            for j in range(4):
                sp.wait_ge(s_mod, 9 + j)
                sp.dma_start(wada[:, j], wf_v[:, :, 512 * j:512 * j + 512]).then_inc(s_w[j], 16)

        @block.gpsimd
        def _(pool):
            pool.memset(k.ident[:, :], 0.0).then_inc(s_const, 1)
            pool.memset(k.ones[:, :], 1.0).then_inc(s_const, 1)
            pool.wait_ge(s_const, 2)
            pool.affine_select(out=k.ident[:, :], in_=k.ident[:, :], compare_op=ALU.not_equal, fill=1.0,
                               base=0, pattern=[[-1, P]], channel_multiplier=1).then_inc(s_const, 1)

        @block.tensor
        def _(pe):
            pe.wait_ge(s_const, 3)
            pe.wait_ge(s_rows, 32)
            for c in range(DK):
                mm = pe.transpose(k.bank[7][:, 9 * c:9 * c + 9], crow[:, P * c:P * c + P], k.ident[0:9, 0:9])
            mm.then_inc(s_cT, 1)
            pe.wait_ge(s_vec, 16 * len(VEC))
            pe.transpose(k.bank[6][:, 0:NVEC], vrow[:, :], k.ident[0:NVEC, 0:NVEC]).then_inc(s_cT, 1)
            pe.wait_ge(s_cTs, 1)
            with pe.Fori(0, 4) as i:
                for j in range(4):
                    pe.wait_ge(s_w[j], i * 16 + 16)
                    if j < 4:
                        pe.wait_ge(s_modrow, i * 4)
                    for c in range(DK):
                        mm = pe.matmul(k.bank[j][0:9, :], cT[:, c, :], wada[:, j, c, :],
                                       start=(c == 0), stop=(c == DK - 1))
                    mm.then_inc(s_mod, 1)
            pe.wait_ge(s_modrow, 16)
            for c in range(64):
                bank, col = (4, 9 * c) if c < 48 else (5, 9 * (c - 48))
                mm = pe.transpose(k.bank[bank][:, col:col + 9], modrow[:, P * c:P * c + P], k.ident[0:9, 0:9])
            mm.then_inc(s_cT, 1)

        @block.scalar
        def _(act):
            with act.Fori(0, 4) as i:
                for j in range(4):
                    act.wait_ge(s_mod, i * 4 + (j + 1))
                    act.activation(modrow[:, bass.ds(i * 2048 + 512 * j, 512)], k.bank[j][0:9, :],
                                   ACT.Copy).then_inc(s_modrow, 1)

        @block.vector
        def _(dve):
            dve.wait_ge(s_cT, 1)
            dve.tensor_copy(cT[:, :, :], k.bank[7][:, 0:72].rearrange("p (c r) -> p c r", r=9)).then_inc(s_cTs, 1)
            dve.wait_ge(s_cT, 2)
            dve.tensor_copy(k.vecT[:, :], k.bank[6][:, 0:NVEC]).then_inc(s_cTs, 1)
            dve.wait_ge(s_cTs, 2)
            dve.wait_ge(s_cT, 3)
            for bank, lo, n in ((4, 0, 48), (5, 48, 16)):
                dve.tensor_tensor(k.modT[:, lo:lo + n, :],
                                  k.bank[bank][:, 0:9 * n].rearrange("p (c r) -> p c r", r=9),
                                  k.vecT[:, lo:lo + n].unsqueeze(2).to_broadcast([P, n, 9]), ALU.add).then_inc(s_modT, 1)
            dve.wait_ge(s_modT, 2)
            for n, (lo, g) in enumerate(((8, 64), (32, 72), (56, 80))):
                dve.scalar_tensor_tensor(out=k.modA[:, n], in0=k.modT[:, lo:lo + 8, :], scalar=1.0,
                                         in1=k.vecT[:, g:g + 8].unsqueeze(2).to_broadcast([P, 8, 9]),
                                         op0=ALU.add, op1=ALU.mult).then_inc(s_modA, 1)


def bias_tables(k):
    nc = k.nc
    s_tab, s_rev, s_neg, s_fwd, s_store = k.sem("s_tab"), k.sem("s_rev"), k.sem("s_neg"), k.sem("s_fwd"), k.sem("s_bstore")
    k.bias_cmp = k.sb("bias_cmp", [64, 512])
    k.bias_win = k.sb("bias_win", [64, 512])
    with ExitStack() as ctx:
        tab = k.sb("tab", [64, NBUCKET], ctx=ctx)
        rev = k.sb("rev", [64, NREV], ctx=ctx)
        fwd = k.sb("fwd", [H, NFWD], ctx=ctx)
        block = ctx.enter_context(nc.Block())
        ends = BUCKET_START[1:] + [PAST + 1]

        @block.sync
        def _(sp):
            with nc.allow_non_contiguous_dma(reason="a 32 x 8 table, transposed"):
                for b in range(B):
                    sp.dma_start(tab[8 * b:8 * b + 8, :], k.i["rel_bias"].rearrange("n h -> h n")).then_inc(s_tab, 16)
            sp.wait_ge(s_rev, NBUCKET)
            sp.wait_ge(s_neg, 1)
            sp.dma_start(k.biasrev_d, rev[:, :]).then_inc(s_store, 16)
            sp.wait_ge(s_fwd, 3)
            sp.dma_start(k.biasfwd_d, fwd[:, :]).then_inc(s_store, 16)
            sp.wait_ge(s_store, 32)

        @block.vector
        def _(dve):
            dve.memset(rev[:, PAST + 1:NREV], NEG).then_inc(s_neg, 1)
            dve.wait_ge(s_tab, 16 * B)
            for n, (lo, hi) in enumerate(zip(BUCKET_START, ends)):
                dve.tensor_copy(rev[:, PAST - hi + 1:PAST - lo + 1],
                                tab[:, n:n + 1].to_broadcast([64, hi - lo])).then_inc(s_rev, 1)
            dve.wait_ge(s_rev, NBUCKET)
            dve.wait_ge(s_neg, 1)
            dve.tensor_copy(fwd[:, :], rev[0:H, PAST + 127:PAST + 127 - NFWD:-1]).then_inc(s_fwd, 1)
            dve.tensor_copy(k.bias_cmp[:, :], rev[:, 31:31 + 512 * STRIDE:STRIDE]).then_inc(s_fwd, 1)
            dve.tensor_copy(k.bias_win[:, :], rev[:, PAST - 511:PAST + 1]).then_inc(s_fwd, 1)


def load_cmp_weights(k, sp, w1, w2, perow, sems):
    for kv in range(2):
        sp.dma_start(w1[:, kv].rearrange("p r s f -> p (r s) f"),
                     k.i["cmp_w1"][0, kv].rearrange("(j s) d f -> (s d) j f", s=2)).then_inc(sems[0], 16)
        sp.dma_start(w2[:, kv], k.i["cmp_w2"][0, kv].rearrange("(c f) d -> f c d", f=P)).then_inc(sems[1], 16)
    sp.dma_start(perow[:, :], k.i["cmp_pe"][0].rearrange("v (j s) d -> (v j) (s d)", s=2)).then_inc(sems[2], 16)


def cache_compress(k):
    nc = k.nc
    k.kcT_d = k.dram("kcT_d", (P, B, NPIECE))
    k.vc_d = k.dram("vc_d", (P, B, 4, P))
    k.peb = k.sb("peb", [P, 2, 2])
    s_pt, s_page = k.sem("s_pt"), [[k.sem(f"s_page{kv}{nt}") for nt in range(4)] for kv in range(2)]
    s_w1, s_w2, s_pe = k.sem("s_cw1"), k.sem("s_cw2"), k.sem("s_cpe")
    s_peT, s_peTs, s_peb = k.sem("s_peT"), k.sem("s_peTs"), k.sem("s_peb")
    s_kst = [k.sem(f"s_kst{kv}") for kv in range(2)]
    s_tr, s_xtv, s_xta = k.sem("s_tr"), k.sem("s_xtv"), k.sem("s_xta")
    s_hid, s_gelu, s_kc, s_kcs, s_zero = k.sem("s_hid"), k.sem("s_gelu"), k.sem("s_kc"), k.sem("s_kcs"), k.sem("s_hzero")
    with ExitStack() as ctx:
        kc_vc = k.sb("kc_vc", [P, 2, NPIECE], ctx=ctx)
        w1 = k.sb("cw1", [P, 2, 2, 8, CH], ctx=ctx)
        w2 = k.sb("cw2", [P, 2, 2, HD], ctx=ctx)
        perow = k.sb("perow", [32, P], ctx=ctx)
        peT = k.sb("peT", [P, 32], ctx=ctx)
        pt = k.sb("pt", [1, B * NPAGES], I32, ctx=ctx)
        raw = k.sb("raw", [P, 2, 4, STRIDE, P], ctx=ctx)
        xt = k.sb("xt", [P, 2, G, 8, NPIECE], ctx=ctx)
        hid = k.sb("hid", [P, 2, 2, NPIECE], ctx=ctx)
        pages = k.i["cache_nsa_kv"][0].rearrange("q (n s) v g d -> q n s (v g d)", s=STRIDE)
        block = ctx.enter_context(nc.Block())

        @block.sync
        def _(sp):
            sp.dma_start(pt[:, :], k.i["page_table"].rearrange("b n -> (b n)").rearrange("(o n) -> o n", o=1)).then_inc(s_pt, 16)
            load_cmp_weights(k, sp, w1, w2, perow, (s_w1, s_w2, s_pe))
            sp.wait_ge(s_pt, 16)

            def item(i, kv):
                for nt in range(4):
                    for q in range(16):
                        page = sp.value_load(pt[0:1, bass.ds(i * NPAGES + 16 * nt + q, 1)], min_val=0, max_val=POOL - 1)
                        sp.dma_start(raw[8 * q:8 * q + 8, kv, nt], pages[bass.ds(page, 1), :, :, P * kv:P * kv + P]
                                     .rearrange("o n s c -> (o n) s c")).then_inc(s_page[kv][nt], 16)

            nc.disable_value_cache = True
            item(0, 0)
            item(0, 1)
            with sp.Fori(1, B) as i:
                for kv in range(2):
                    sp.wait_ge(s_tr, i * 32 + (16 * kv + 16 - 32))
                    item(i, kv)
            nc.disable_value_cache = False

        @block.gpsimd
        def _(pool):
            for i in range(B):
                pool.wait_ge(s_kcs, i * 2 + 1)
                pool.dma_start(k.kcT_d[:, i, :], kc_vc[:, 0, :]).then_inc(s_kst[0], 16)
                pool.wait_ge(s_kcs, i * 2 + 2)
                pool.dma_start(k.vc_d[:, i].rearrange("p t d -> p (t d)"), kc_vc[:, 1, :]).then_inc(s_kst[1], 16)
            for kv in range(2):
                pool.wait_ge(s_kst[kv], 16 * B)

        @block.tensor
        def _(pe):
            pe.wait_ge(s_pe, 16)
            pe.transpose(k.bank[0][:, 0:32], perow[:, :], k.ident[0:32, 0:32]).then_inc(s_peT, 1)
            pe.wait_ge(s_peTs, 1)
            pe.wait_ge(s_w1, 32)
            pe.wait_ge(s_w2, 32)
            for kv in range(2):
                for c in range(2):
                    for j in range(16):
                        mm = pe.matmul(k.bank[1][:, 2 * kv + c:2 * kv + c + 1], w1[:, kv, j // 8, j % 8, P * c:P * c + P],
                                       peT[:, 16 * kv + j:16 * kv + j + 1], start=(j == 0), stop=(j == 15))
            mm.then_inc(s_peT, 1)
            pe.wait_ge(s_peb, 1)

            def turn(i, kv, tokens, start=False):
                for s in tokens:
                    if s == 0:
                        for nt in range(4):
                            pe.wait_ge(s_page[kv][nt], i * 256 + 256)
                    if not (start and s < 4):
                        pe.wait_ge(s_xta if s % 2 else s_xtv, i * 16 + (8 * kv + s // 2 - 1))
                    for nt in range(4):
                        mm = pe.transpose(k.bank[s % 4][:, P * nt:P * nt + P], raw[:, kv, nt, s, :], k.ident[:, :])
                    mm.then_inc(s_tr, 1)

            def first(i, kv, n):
                g, c = n // 2, n % 2
                pe.wait_ge(s_gelu, i * 8 + max(4 * kv + n - 1, 0))
                for j in range(16):
                    mm = pe.matmul(k.bank[4 + c][:, 0:NCMP], w1[:, kv, j // 8, j % 8, P * c:P * c + P],
                                   xt[:, kv, g, j % 8, j // 8:j // 8 + NCMP], start=(j == 0), stop=(j == 15))
                mm.then_inc(s_hid, 1)

            def second(i, kv, g):
                if g == 0:
                    pe.wait_ge(s_kcs, i * 2 + kv)
                pe.wait_ge(s_gelu, i * 8 + (4 * kv + 2 * g + 2))
                for nt in range(1 if kv == 0 else 4):
                    for c in range(2):
                        if kv == 0:
                            mm = pe.matmul(k.bank[7][HD * g:HD * g + HD, :], w2[:, 0, c, :], hid[:, g, c, :],
                                           start=(c == 0), stop=(c == 1))
                        else:
                            mm = pe.matmul(k.bank[7][:, P * nt + HD * g:P * nt + HD * g + HD],
                                           hid[:, g, c, P * nt:P * nt + P], w2[:, 1, c, :],
                                           start=(c == 0), stop=(c == 1))
                mm.then_inc(s_kc, 1)

            def item(i, kv, following):
                pe.wait_ge(s_xtv, i * 16 + (8 * kv + 8))
                pe.wait_ge(s_xta, i * 16 + (8 * kv + 8))
                for n in range(4):
                    first(i, kv, n)
                    if n == 2:
                        second(i, kv, 0)
                    if following:
                        turn(*following, range(4 * n, 4 * n + 4))
                second(i, kv, 1)

            turn(0, 0, range(STRIDE), True)
            with pe.Fori(0, B - 1) as i:
                item(i, 0, (i, 1))
                item(i, 1, (i + 1, 0))
            item(B - 1, 0, (B - 1, 1))
            item(B - 1, 1, None)

        def copy(eng, i, kv, s, first=False):
            odd = s % 2
            if s < 2 and not first:
                eng.wait_ge(s_hid, i * 8 + (4 * kv - 4))
            eng.wait_ge(s_tr, i * 32 + (16 * kv + s + 1))
            for g in range(G):
                dst = xt[HD * odd:HD * odd + HD, kv, g, s // 2, :]
                src = k.bank[s % 4][HD * g:HD * g + HD, :]
                ins = eng.activation(dst, src, ACT.Copy) if odd else eng.tensor_copy(dst, src)
            ins.then_inc(s_xta if odd else s_xtv, 1)

        @block.vector
        def _(dve):
            def item(i, kv, following):
                if following:
                    for s in range(0, STRIDE, 2):
                        copy(dve, *following, s)
                dve.wait_ge(s_kst[kv], i * 16)
                dve.wait_ge(s_kc, i * 4 + (2 * kv + 2))
                dve.tensor_copy(kc_vc[:, kv, :], k.bank[7][:, :]).then_inc(s_kcs, 1)

            dve.memset(hid[:, :, :, NCMP:NPIECE], 0.0).then_inc(s_zero, 1)
            dve.wait_ge(s_peT, 1)
            dve.tensor_copy(peT[:, :], k.bank[0][:, 0:32]).then_inc(s_peTs, 1)
            dve.wait_ge(s_peT, 2)
            dve.tensor_copy(k.peb[:, :, :], k.bank[1][:, 0:4].rearrange("p (v c) -> p v c", v=2)).then_inc(s_peb, 1)
            for s in range(0, STRIDE, 2):
                copy(dve, 0, 0, s, True)
            with dve.Fori(0, B - 1) as i:
                item(i, 0, (i, 1))
                item(i, 1, (i + 1, 0))
            item(B - 1, 0, (B - 1, 1))
            item(B - 1, 1, None)

        @block.scalar
        def _(act):
            def item(i, kv, following):
                for n in range(4):
                    g, c = n // 2, n % 2
                    act.wait_ge(s_hid, i * 8 + (4 * kv + n + 1))
                    act.wait_ge(s_kc, i * 4 + max(2 * kv + g - 1, 0))
                    act.activation(hid[:, g, c, 0:NCMP], k.bank[4 + c][:, 0:NCMP],
                                   ACT.Gelu_apprx_tanh, bias=k.peb[:, kv, c:c + 1]).then_inc(s_gelu, 1)
                    if following:
                        for s in range(4 * n + 1, 4 * n + 4, 2):
                            copy(act, *following, s)

            act.wait_ge(s_peb, 1)
            act.wait_ge(s_zero, 1)
            for s in range(1, STRIDE, 2):
                copy(act, 0, 0, s, True)
            with act.Fori(0, B - 1) as i:
                item(i, 0, (i, 1))
                item(i, 1, (i + 1, 0))
            item(B - 1, 0, (B - 1, 1))
            item(B - 1, 1, None)


def load_x(k, xT):
    nc = k.nc
    s_x, s_xt, s_xc = [k.sem(f"s_x{j}") for j in range(4)], k.sem("s_xt"), k.sem("s_xc")
    s_xs = k.sem("s_xs")
    with ExitStack() as ctx:
        xrow = k.sb("xrow", [P, 4, D], ctx=ctx)
        xsrow = k.sb("xsrow", [B, D], ctx=ctx)
        block = ctx.enter_context(nc.Block())

        @block.sync
        def _(sp):
            for ti in range(NTI):
                if ti >= 4:
                    sp.wait_ge(s_xt, 2 * (ti - 3))
                sp.dma_start(xrow[:, ti % 4], k.i["x_prompt"][0, P * ti:P * ti + P, :]).then_inc(s_x[ti % 4], 16)
                if ti == 0:
                    sp.dma_start(xsrow[:, :], k.i["x_sample"].rearrange("b o d -> (b o) d")).then_inc(s_xs, 16)

        @block.tensor
        def _(pe):
            for f in range(2 * NTI):
                ti, half = f // 2, f % 2
                pe.wait_ge(s_x[ti % 4], 16 * (ti // 4 + 1))
                if f >= 4:
                    pe.wait_ge(s_xc, f - 3)
                for q in range(4):
                    c = 4 * half + q
                    mm = pe.transpose(k.bank[f % 4][:, P * q:P * q + P], xrow[:, ti % 4, P * c:P * c + P], k.ident[:, :])
                mm.then_inc(s_xt, 1)
            pe.wait_ge(s_xs, 16)
            for c in range(DK):
                mm = pe.transpose(k.bank[4][:, B * c:B * c + B], xsrow[:, P * c:P * c + P], k.ident[0:B, 0:B])
            mm.then_inc(s_xt, 1)

        @block.vector
        def _(dve):
            for f in range(2 * NTI):
                ti, half = f // 2, f % 2
                dve.wait_ge(s_xt, f + 1)
                dve.tensor_copy(xT[:, 4 * half:4 * half + 4, P * ti:P * ti + P],
                                k.bank[f % 4][:, :].rearrange("p (q t) -> p q t", q=4)).then_inc(s_xc, 1)
            dve.wait_ge(s_xt, 2 * NTI + 1)
            dve.tensor_copy(xT[:, :, T:TT], k.bank[4][:, 0:B * DK].rearrange("p (c t) -> p c t", c=DK)).then_inc(s_xc, 1)


def norm(k, tag, src, n, dst, keep=None, keep_dst=None):
    nc = k.nc
    shift = (0, 24, 48)[n]
    s_sq, s_sum, s_ms, s_rt, s_rstd = (k.sem(f"{x}_{tag}") for x in ("s_sq", "s_sum", "s_ms", "s_rt", "s_rstd"))
    s_mul, s_out, s_smp = (k.sem(f"{x}_{tag}") for x in ("s_mul", "s_nout", "s_smp"))
    s_keep = k.sem(f"s_keep_{tag}")
    with ExitStack() as ctx:
        sq = k.sb(f"sq_{tag}", [P, 4, GT], ctx=ctx)
        rs = k.sb(f"rs_{tag}", [P, NG, GT], ctx=ctx)
        tmp = k.sb(f"tmp_{tag}", [P, 4, GT], ctx=ctx)
        block = ctx.enter_context(nc.Block())

        if keep is not None:
            @block.sync
            def _(sp):
                sp.dma_start(keep, src[:, :, :]).then_inc(s_keep, 16)
                sp.wait_ge(s_out, NG * DK)
                sp.wait_ge(s_smp, DK + 1)
                sp.dma_start(keep_dst, dst[:, :, :]).then_inc(s_keep, 16)
                sp.wait_ge(s_keep, 32)

        @block.scalar
        def _(act):
            for g in range(NG):
                for c in range(DK):
                    f = g * DK + c
                    if f >= 4:
                        act.wait_ge(s_sum, f - 3)
                    act.activation(sq[:, f % 4, :], src[:, c, GT * g:GT * g + GT], ACT.Square).then_inc(s_sq, 1)
            for g in range(NG):
                act.wait_ge(s_ms, g + 1)
                act.activation(rs[:, g, :], rs[:, g, :], ACT.Sqrt).then_inc(s_rt, 1)

        @block.tensor
        def _(pe):
            for g in range(NG):
                for c in range(DK):
                    pe.wait_ge(s_sq, g * DK + c + 1)
                    pe.matmul(k.bank[g][:, 0:GT], k.ones[:, :], sq[:, (g * DK + c) % 4, :],
                              start=(c == 0), stop=(c == DK - 1)).then_inc(s_sum, 1)

        @block.vector
        def _(dve):
            for g in range(NG):
                dve.wait_ge(s_sum, DK * (g + 1))
                dve.tensor_scalar(rs[:, g, :], k.bank[g][:, 0:GT], 1.0 / D, EPS, ALU.mult, ALU.add).then_inc(s_ms, 1)
            for g in range(NG):
                dve.wait_ge(s_rt, g + 1)
                dve.reciprocal(rs[:, g, :], rs[:, g, :]).then_inc(s_rstd, 1)
            for g in range(NG):
                dve.wait_ge(s_rstd, g + 1)
                for c in range(DK):
                    f = g * DK + c
                    if f >= 4:
                        dve.wait_ge(s_out, f - 3)
                    dve.tensor_tensor(tmp[:, f % 4, :], src[:, c, GT * g:GT * g + GT], rs[:, g, :], ALU.mult).then_inc(s_mul, 1)
                    dve.wait_ge(s_mul, f + 1)
                    w = GT if g < NG - 1 else T - GT * (NG - 1)
                    if w < GT:
                        dve.tensor_tensor(dst[:, c, T:TT], tmp[:, f % 4, w:GT], k.modA[:, n, c, 1:9], ALU.mult).then_inc(s_smp, 1)
                    dve.tensor_scalar(dst[:, c, GT * g:GT * g + w], tmp[:, f % 4, 0:w], k.modA[:, n, c, 0:1],
                                      k.modT[:, shift + c, 0:1], ALU.mult, ALU.add).then_inc(s_out, 1)
            dve.wait_ge(s_smp, DK)
            dve.tensor_tensor(dst[:, :, T:TT], dst[:, :, T:TT], k.modT[:, shift:shift + DK, 1:9], ALU.add).then_inc(s_smp, 1)


def mlstm_project(k):
    nc = k.nc
    w_v = k.i["w_in"][0].rearrange("(k p) n -> p k n", p=P)
    units = ((OFF_QB, k.qbT, 1.0), (OFF_KB, k.kbT, float(MD) ** -0.5))
    s_w, s_ws, s_gb = [k.sem(f"s_mw{j}") for j in range(2)], k.sem("s_mws"), k.sem("s_gb")
    s_fill, s_evT, s_evK, s_one = k.sem("s_mfill"), k.sem("s_mevT"), k.sem("s_mevK"), k.sem("s_mone")
    s_sm, s_gbb = k.sem("s_smallst"), k.sem("s_gbb")
    s_add = k.sem("s_madd")
    with ExitStack() as ctx:
        w = k.sb("mw", [P, 2, DK, 512], ctx=ctx)
        wsm = k.sb("mwsm", [P, DK, 32], ctx=ctx)
        gb = k.sb("gb", [1, 8], ctx=ctx)
        gbb = k.sb("gbb", [P, 8], ctx=ctx)
        block = ctx.enter_context(nc.Block())
        NT_FILLS = 2 * 4 * NG

        @block.sync
        def _(sp):
            sp.dma_start(w[:, 0], w_v[:, :, OFF_QB:OFF_QB + 512]).then_inc(s_w[0], 16)
            sp.dma_start(w[:, 1], w_v[:, :, OFF_KB:OFF_KB + 512]).then_inc(s_w[1], 16)
            sp.dma_start(wsm[:, :, 0:24], w_v[:, :, OFF_GA:OFF_QB]).then_inc(s_ws, 16)
            sp.dma_start(wsm[:, :, 24:32], w_v[:, :, OFF_IFB:OFF_OB]).then_inc(s_ws, 16)
            sp.dma_start(gb[:, :], k.i["mlstm_gate_b"]).then_inc(s_gb, 16)
            sp.wait_ge(s_fill, 4 * NG)
            sp.dma_start(w[:, 0], w_v[:, :, OFF_VB:OFF_VB + 512]).then_inc(s_w[0], 16)
            sp.wait_ge(s_add, 2)
            sp.dma_start(k.smalltok_d, k.small_s[:, :]).then_inc(s_sm, 16)
            sp.wait_ge(s_sm, 16)

        def tokens(ti):
            return slice(P * ti, P * ti + P) if ti < NTI else slice(T, TT)

        @block.tensor
        def _(pe):
            fill = 0

            def bank():
                if fill >= 8:
                    old = fill - 8
                    if old < NT_FILLS:
                        pe.wait_ge(s_evT, old + 1)
                    else:
                        pe.wait_ge(s_evK, old - NT_FILLS + 1)
                return k.bank[fill % 8]

            for u in range(2):
                pe.wait_ge(s_w[u], 16)
                for c in range(4):
                    for g in range(NG):
                        b = bank()
                        for kk in range(DK):
                            mm = pe.matmul(b[:, 0:GT], w[:, u, kk, P * c:P * c + P], k.uT[:, kk, GT * g:GT * g + GT],
                                           start=(kk == 0), stop=(kk == DK - 1))
                        mm.then_inc(s_fill, 1)
                        fill += 1
            pe.wait_ge(s_w[0], 32)
            pe.wait_ge(s_ws, 32)
            for src, n in ((w[:, 0], 512), (wsm, 32)):
                for ti in range(NTI + 1):
                    b = bank()
                    m = P if ti < NTI else B
                    for kk in range(DK):
                        mm = pe.matmul(b[0:m, 0:n], k.uT[:, kk, tokens(ti)], src[:, kk, :],
                                       start=(kk == 0), stop=(kk == DK - 1))
                    mm.then_inc(s_fill, 1)
                    fill += 1
            pe.wait_ge(s_evT, NT_FILLS)
            for ti in range(NTI + 1):
                b = bank()
                m = P if ti < NTI else B
                for h in range(MH):
                    mm = pe.transpose(b[0:m, P * h:P * h + P], k.kbT[:, h, tokens(ti)], k.ident[:, :])
                mm.then_inc(s_fill, 1)
                fill += 1
            b = bank()
            pe.wait_ge(s_gb, 16)
            pe.matmul(b[:, 0:8], k.ones[0:1, :], gb[0:1, :], start=True, stop=True).then_inc(s_fill, 1)

        @block.scalar
        def _(act):
            f = 0
            for _, dst, scale in units:
                for c in range(4):
                    for g in range(NG):
                        act.wait_ge(s_fill, f + 1)
                        act.activation(dst[:, c, GT * g:GT * g + GT], k.bank[f % 8][:, 0:GT], ACT.Copy, scale=scale).then_inc(s_evT, 1)
                        f += 1

        @block.vector
        def _(dve):
            dve.memset(k.vb[:, :, :, MD:MD + 1], 1.0).then_inc(s_one, 1)
            dve.memset(k.vb_s[:, :, MD:MD + 1], 1.0).then_inc(s_one, 1)
            f = NT_FILLS
            for kind in range(3):
                for ti in range(NTI + 1):
                    dve.wait_ge(s_fill, f + 1)
                    m = P if ti < NTI else B
                    n = 32 if kind == 1 else 512
                    b = k.bank[f % 8][0:m, 0:n]
                    if kind == 0:
                        dst = k.vb[:, ti, :, 0:MD] if ti < NTI else k.vb_s[:, :, 0:MD]
                        b = b.rearrange("p (h d) -> p h d", h=MH)
                    elif kind == 1:
                        dst = k.small[:, ti, :] if ti < NTI else k.small_s[:, :]
                    else:
                        dst = k.kb[:, ti, :] if ti < NTI else k.kb_s[:, :]
                    dve.tensor_copy(dst, b).then_inc(s_evK, 1)
                    f += 1
            dve.wait_ge(s_fill, f + 1)
            dve.tensor_copy(gbb[:, :], k.bank[f % 8][:, 0:8]).then_inc(s_gbb, 1)
            dve.wait_ge(s_gbb, 1)
            dve.wait_ge(s_evK, 18)
            dve.tensor_tensor(k.small[:, :, 24:32], k.small[:, :, 24:32], gbb[:, :].unsqueeze(1).to_broadcast([P, NTI, 8]), ALU.add).then_inc(s_add, 1)
            dve.tensor_tensor(k.small_s[:, 24:32], k.small_s[:, 24:32], gbb[0:B, :], ALU.add).then_inc(s_add, 1)


def mlstm_scan(k):
    nc = k.nc
    s_tri, s_chain, s_lf, s_bc, s_e = k.sem("s_tri"), k.sem("s_mchain"), k.sem("s_lf"), k.sem("s_bc"), k.sem("s_me")
    s_diag, s_crow, s_cmrow, s_q, s_S, s_B, s_A, s_U, s_swT = (k.sem(f"s_m_{x}") for x in ("diag", "crow", "cm", "q", "S", "B", "A", "U", "swT"))
    s_E, s_w, s_sw, s_swTs, s_kw, s_num, s_C, s_QC = (k.sem(f"s_m_{x}") for x in ("E", "w", "sw", "swTs", "kw", "num", "C", "QC"))
    s_hn, s_hT, s_hTs, s_st, s_init, s_hsq, s_hrt = (k.sem(f"s_m_{x}") for x in ("hn", "hT", "hTs", "st", "init", "hsq", "hrt"))
    NC = T // P
    W = MD + 1
    with ExitStack() as ctx:
        tri = k.sb("tri", [P, P], ctx=ctx)
        low = k.sb("low", [P, P], ctx=ctx)
        g1 = k.sb("mg1", [P, NC, MH], ctx=ctx)
        g2 = k.sb("mg2", [P, NC, MH], ctx=ctx)
        lf = k.sb("lf", [P, NC, MH], ctx=ctx)
        bc = k.sb("bcum", [P, NC, MH], ctx=ctx)
        bl = k.sb("blast", [P, NC, MH], ctx=ctx)
        cs = k.sb("cs", [P, NC, MH], ctx=ctx)
        diag = k.sb("mdiag", [P, MH, P], ctx=ctx)
        cm = k.sb("cm", [P, MH, P], ctx=ctx)
        ee = k.sb("ee", [P, MH, P], ctx=ctx)
        sw = k.sb("sw", [P, MH, P], ctx=ctx)
        swT = k.sb("swT", [P, MH, P], ctx=ctx)
        kw = k.sb("kw", [P, MH, P], ctx=ctx)
        qc = k.sb("qc", [P, MH, P], ctx=ctx)
        rmax = k.sb("rmax", [P, MH], ctx=ctx)
        cmax = k.sb("cmax", [P, MH], ctx=ctx)
        mx = k.sb("mx", [P, MH], ctx=ctx)
        nmx = k.sb("nmx", [P, MH], ctx=ctx)
        ml = k.sb("ml", [P, MH], ctx=ctx)
        mst = k.sb("mst", [P, MH], ctx=ctx)
        ein = k.sb("ein", [P, 4, MH], ctx=ctx)
        wx = k.sb("wx", [P, 4, MH], ctx=ctx)
        C = k.sb("Cst", [P, MH, W], ctx=ctx)
        num = k.sb("num", [P, MH, W], ctx=ctx)
        den = k.sb("den", [P, MH], ctx=ctx)
        hb = k.sb("hbuf", [P, NC * MH, P], ctx=ctx)
        mu = k.sb("mu", [P, NC * MH], ctx=ctx)
        var = k.sb("var", [P, NC * MH], ctx=ctx)
        PER = 16
        block = ctx.enter_context(nc.Block())

        @block.gpsimd
        def _(pool):
            pool.memset(tri[:, :], 1.0).then_inc(s_tri, 1)
            pool.memset(low[:, :], 0.0).then_inc(s_tri, 1)
            pool.wait_ge(s_tri, 2)
            pool.affine_select(out=tri[:, :], in_=tri[:, :], compare_op=ALU.is_ge, fill=0.0, base=0,
                               pattern=[[1, P]], channel_multiplier=-1).then_inc(s_tri, 1)
            pool.affine_select(out=low[:, :], in_=low[:, :], compare_op=ALU.is_ge, fill=NEG, base=0,
                               pattern=[[-1, P]], channel_multiplier=1).then_inc(s_tri, 1)

        @block.vector
        def _(dve):
            ch = Chain(dve, s_chain)
            f, i_ = k.small[:, :, 28:32], k.small[:, :, 24:28]
            dve.memset(mst[:, :], 0.0).then_inc(s_init, 1)
            dve.memset(C[:, :, :], 0.0).then_inc(s_init, 1)
            ch.link(dve.scalar_tensor_tensor(out=g1[:, :, :], in0=f, scalar=-1.0, in1=f, op0=ALU.mult, op1=ALU.max))
            dve.tensor_scalar(g2[:, :, :], f, 0.0, None, ALU.min).then_inc(s_lf, 1)
            dve.wait_ge(s_e, 2)
            dve.wait_ge(s_lf, 1)
            dve.tensor_tensor(lf[:, :, :], g2[:, :, :], g1[:, :, :], ALU.subtract).then_inc(s_lf, 1)
            dve.wait_ge(s_bc, 1)
            dve.tensor_copy(bc[:, :, :], k.bank[0][:, 0:NC * MH].rearrange("p (c h) -> p c h", h=MH)).then_inc(s_lf, 1)
            dve.tensor_copy(bl[:, :, :], k.bank[1][:, 0:NC * MH].rearrange("p (c h) -> p c h", h=MH)).then_inc(s_lf, 1)
            dve.wait_ge(s_lf, 4)
            ch.link(dve.tensor_tensor(cs[:, :, :], i_, bc[:, :, :], ALU.subtract))
            dve.wait_ge(s_init, 2)
            dve.wait_ge(s_tri, 4)
            base = ch.n

            with dve.Fori(0, NC) as i:
                ch.base = base
                ch.start(i, PER)
                csi = cs[:, bass.ds(i, 1), :].rearrange("p o h -> p (o h)")
                bci = bc[:, bass.ds(i, 1), :].rearrange("p o h -> p (o h)")
                dve.tensor_tensor(diag[:, :, :], k.ident[:, :].unsqueeze(1).to_broadcast([P, MH, P]),
                                  csi.unsqueeze(2).to_broadcast([P, MH, P]), ALU.mult).then_inc(s_diag, 1)
                crow = k.bank[0][:, :].rearrange("p (h s) -> p h s", h=MH)
                dve.wait_ge(s_crow, i + 1)
                dve.tensor_reduce(cmax[:, :], crow, AX.X, ALU.max).then_inc(s_cmrow, 1)
                ch.link(dve.tensor_tensor(cm[:, :, :], crow, low[:, :].unsqueeze(1).to_broadcast([P, MH, P]), ALU.add))
                ch.link(dve.tensor_reduce(rmax[:, :], cm[:, :, :], AX.X, ALU.max))
                dve.wait_ge(s_cmrow, i * 2 + 1)
                ch.link(dve.tensor_tensor(mx[:, :], rmax[:, :], mst[:, :], ALU.max))
                ch.link(dve.tensor_tensor(ml[:, :], cmax[:, :], mst[:, :], ALU.max))
                ch.link(dve.tensor_scalar(nmx[:, :], mx[:, :], -1.0, None, ALU.mult))
                ch.link(dve.tensor_tensor(ein[:, 0], mst[:, :], mx[:, :], ALU.subtract))
                ch.link(dve.tensor_tensor(ein[:, 1], nmx[:, :], bci, ALU.subtract))
                ch.link(dve.tensor_tensor(ein[:, 2], csi, ml[:, :], ALU.subtract))
                ch.link(dve.tensor_tensor(ein[:, 3], mst[:, :], ml[:, :], ALU.subtract))
                dve.tensor_tensor(mst[:, :], bl[:, bass.ds(i, 1), :].rearrange("p o h -> p (o h)"), ml[:, :], ALU.add).then_inc(s_cmrow, 1)
                dve.wait_ge(s_w, i + 1)
                dve.tensor_tensor(kw[:, :, :], k.kb[:, bass.ds(i, 1), :].rearrange("p o (h d) -> p (o h) d", h=MH),
                                  wx[:, 2].unsqueeze(2).to_broadcast([P, MH, P]), ALU.mult).then_inc(s_kw, 1)
                dve.wait_ge(s_E, i * 4 + 4)
                dve.wait_ge(s_S, i + 1)
                dve.tensor_tensor(sw[:, :, :], k.bank[1][:, :].rearrange("p (h s) -> p h s", h=MH), ee[:, :, :], ALU.mult).then_inc(s_sw, 1)
                dve.wait_ge(s_B, i + 1)
                for a in range(2):
                    last = dve.tensor_tensor(num[:, 2 * a:2 * a + 2, :], k.bank[5 + a][:, 0:2 * W].rearrange("p (h e) -> p h e", h=2),
                                             wx[:, 0, 2 * a:2 * a + 2].unsqueeze(2).to_broadcast([P, 2, W]), ALU.mult)
                    last.then_inc(s_QC, 1)
                ch.link(dve.tensor_tensor(C[:, :, :], C[:, :, :], wx[:, 3].unsqueeze(2).to_broadcast([P, MH, W]), ALU.mult))
                dve.wait_ge(s_QC, i * 2 + 2)
                dve.wait_ge(s_A, i + 1)
                for a in range(2):
                    ch.link(dve.tensor_tensor(num[:, 2 * a:2 * a + 2, :], num[:, 2 * a:2 * a + 2, :],
                                              k.bank[3 + a][:, 0:2 * W].rearrange("p (h e) -> p h e", h=2), ALU.add))
                dve.wait_ge(s_U, i + 1)
                for a in range(2):
                    dve.tensor_tensor(C[:, 2 * a:2 * a + 2, :], C[:, 2 * a:2 * a + 2, :],
                                      k.bank[5 + a][:, 0:2 * W].rearrange("p (h e) -> p h e", h=2), ALU.add).then_inc(s_C, 1)
                ch.link(dve.scalar_tensor_tensor(out=den[:, :].unsqueeze(2), in0=num[:, :, MD:W], scalar=-1.0, in1=num[:, :, MD:W],
                                                 op0=ALU.mult, op1=ALU.max))
                ch.link(dve.tensor_tensor(den[:, :], den[:, :], wx[:, 1], ALU.max))
                ch.link(dve.reciprocal(den[:, :], den[:, :]))
                ch.link(dve.tensor_tensor(hb[:, bass.ds(i * MH, MH), :], num[:, :, 0:MD],
                                          den[:, :].unsqueeze(2).to_broadcast([P, MH, MD]), ALU.mult))
                ch.done()
            ch.per, ch.base = None, base + NC * PER
            ch.n = 0
            n = NC * MH
            ch.link(dve.tensor_reduce(mu[:, :], hb[:, :, :], AX.X, ALU.add))
            ch.link(dve.tensor_scalar(mu[:, :], mu[:, :], 1.0 / MD, None, ALU.mult))
            for c in range(NC):
                s = slice(MH * c, MH * c + MH)
                dve.tensor_tensor(hb[:, s, :], hb[:, s, :], mu[:, s].unsqueeze(2).to_broadcast([P, MH, MD]), ALU.subtract).then_inc(s_hn, 1)
            for c in range(NC):
                dve.wait_ge(s_hsq, c + 1)
                dve.tensor_reduce(var[:, MH * c:MH * c + MH], (ee if c % 2 else cm)[:, :, :], AX.X, ALU.add).then_inc(s_hn, 1)
            dve.wait_ge(s_hn, 2 * NC)
            ch.link(dve.tensor_scalar(var[:, :], var[:, :], 1.0 / MD, EPS, ALU.mult, ALU.add))
            dve.wait_ge(s_hrt, 1)
            ch.link(dve.reciprocal(var[:, :], var[:, :]))
            for c in range(NC):
                s = slice(MH * c, MH * c + MH)
                dve.tensor_tensor(hb[:, s, :], hb[:, s, :], var[:, s].unsqueeze(2).to_broadcast([P, MH, MD]), ALU.mult).then_inc(s_hn, 1)
            for c in range(NC):
                dve.wait_ge(s_hT, c + 1)
                dve.tensor_tensor(k.hbT[:, :, P * c:P * c + P], k.bank[c % 4][:, :].rearrange("p (h t) -> p h t", h=MH),
                                  k.vecT[:, 88:92].unsqueeze(2).to_broadcast([P, MH, P]), ALU.mult).then_inc(s_hTs, 1)

        @block.scalar
        def _(act):
            act.wait_ge(s_chain, 1)
            act.activation(g1[:, :, :], g1[:, :, :], ACT.Exp, scale=-1.0).then_inc(s_e, 1)
            act.wait_ge(s_e, 1)
            act.activation(g1[:, :, :], g1[:, :, :], ACT.Ln, bias=1.0).then_inc(s_e, 1)
            with act.Fori(0, NC) as i:
                act.wait_ge(s_U, i)
                act.activation(qc[:, :, :], k.qbT[:, :, bass.ds(i * P, P)], ACT.Copy).then_inc(s_q, 1)
                act.wait_ge(s_cmrow, i * 2 + 2)
                act.activation(wx[:, :, :], ein[:, :, :], ACT.Exp).then_inc(s_w, 1)
                for h in range(MH):
                    act.activation(ee[:, h, :], cm[:, h, :], ACT.Exp, bias=nmx[:, h:h + 1]).then_inc(s_E, 1)
                act.wait_ge(s_swT, i + 1)
                act.activation(swT[:, :, :], k.bank[2][:, :].rearrange("p (h s) -> p h s", h=MH), ACT.Copy).then_inc(s_swTs, 1)
            for c in range(NC):
                act.wait_ge(s_hn, c + 1)
                if c >= 2:
                    act.wait_ge(s_hn, NC + c - 1)
                act.activation((ee if c % 2 else cm)[:, :, :], hb[:, MH * c:MH * c + MH, :], ACT.Square).then_inc(s_hsq, 1)
            act.wait_ge(s_chain, 2 + NC * PER + 3)
            act.activation(var[:, :], var[:, :], ACT.Sqrt).then_inc(s_hrt, 1)

        @block.tensor
        def _(pe):
            pe.wait_ge(s_lf, 2)
            pe.wait_ge(s_tri, 4)
            pe.matmul(k.bank[0][:, 0:NC * MH], tri[:, :], lf[:, :, :].rearrange("p c h -> p (c h)"), start=True, stop=True)
            pe.matmul(k.bank[1][:, 0:NC * MH], k.ones[:, :], lf[:, :, :].rearrange("p c h -> p (c h)"), start=True, stop=True).then_inc(s_bc, 1)
            pe.wait_ge(s_lf, 4)
            with pe.Fori(0, NC) as i:
                pe.wait_ge(s_diag, i + 1)
                pe.matmul(k.bank[0][:, :], k.ones[:, :], diag[:, :, :].rearrange("p h s -> p (h s)"), start=True, stop=True).then_inc(s_crow, 1)
                pe.wait_ge(s_q, i + 1)
                pe.wait_ge(s_sw, i)
                for h in range(MH):
                    mm = pe.matmul(k.bank[1][:, P * h:P * h + P], qc[:, h, :], k.kbT[:, h:h + 1, bass.ds(i * P, P)].rearrange("p o t -> p (o t)"),
                                   start=True, stop=True)
                mm.then_inc(s_S, 1)
                pe.wait_ge(s_C, i * 2)
                for h in range(MH):
                    mm = pe.matmul(k.bank[5 + h // 2][:, W * (h % 2):W * (h % 2) + W], qc[:, h, :], C[:, h, :], start=True, stop=True)
                mm.then_inc(s_B, 1)
                pe.wait_ge(s_sw, i + 1)
                for h in range(MH):
                    mm = pe.transpose(k.bank[2][:, P * h:P * h + P], sw[:, h, :], k.ident[:, :])
                mm.then_inc(s_swT, 1)
                pe.wait_ge(s_swTs, i + 1)
                v = k.vb[:, bass.ds(i, 1), :, :]
                for h in range(MH):
                    mm = pe.matmul(k.bank[3 + h // 2][:, W * (h % 2):W * (h % 2) + W], swT[:, h, :], v[:, :, h, :].rearrange("p o e -> p (o e)"),
                                   start=True, stop=True)
                mm.then_inc(s_A, 1)
                pe.wait_ge(s_QC, i * 2 + 2)
                for h in range(MH):
                    mm = pe.matmul(k.bank[5 + h // 2][:, W * (h % 2):W * (h % 2) + W], kw[:, h, :], v[:, :, h, :].rearrange("p o e -> p (o e)"),
                                   start=True, stop=True)
                mm.then_inc(s_U, 1)
            for c in range(NC):
                pe.wait_ge(s_hn, 2 * NC + c + 1)
                if c >= 4:
                    pe.wait_ge(s_hTs, c - 3)
                for h in range(MH):
                    mm = pe.transpose(k.bank[c % 4][:, P * h:P * h + P], hb[:, MH * c + h, :], k.ident[:, :])
                mm.then_inc(s_hT, 1)

        @block.sync
        def _(sp):
            sp.wait_ge(s_C, 2 * NC)
            sp.dma_start(k.o["C_prompt"][0, 0].rearrange("h d e -> d h e"), C[:, :, 0:MD]).then_inc(s_st, 16)
            with nc.allow_non_contiguous_dma(reason="512 normalizer entries"):
                sp.dma_start(k.o["n_prompt"][0, 0].rearrange("h d -> d h"), C[:, :, MD:W].rearrange("p h o -> p (h o)")).then_inc(s_st, 16)
            sp.wait_ge(s_cmrow, 2 * NC)
            sp.dma_start(k.o["m_prompt"][0], mst[0:1, :]).then_inc(s_st, 16)
            sp.wait_ge(s_st, 48)


def mlstm_decode(k):
    nc = k.nc
    W = MD + 1
    BH = B * MH
    s_in, s_chain, s_e, s_bcp, s_bcs, s_km, s_U, s_C = (k.sem(f"s_d_{x}") for x in ("in", "chain", "e", "bcp", "bcs", "km", "U", "C"))
    s_nT, s_h, s_sum, s_sq, s_rt, s_st, s_nrow = (k.sem(f"s_d_{x}") for x in ("nT", "h", "sum", "sq", "rt", "st", "nrow"))
    with ExitStack() as ctx:
        C = k.sb("Cs", [P, BH, W], ctx=ctx)
        n0 = k.sb("n0", [BH, P], ctx=ctx)
        nrow = k.sb("nrow", [BH, P], ctx=ctx)
        ncol = k.sb("ncol", [P, BH], ctx=ctx)
        m0 = k.sb("m0", [B, MH], ctx=ctx)
        g1 = k.sb("dg1", [B, MH], ctx=ctx)
        g2 = k.sb("dg2", [B, MH], ctx=ctx)
        mm_ = k.sb("dm", [B, MH], ctx=ctx)
        ein = k.sb("dein", [B, 3, MH], ctx=ctx)
        dg = k.sb("ddiag", [B, 2, B, MH], ctx=ctx)
        wb = k.sb("dwb", [P, 2, BH], ctx=ctx)
        kws = k.sb("kws", [B, 512], ctx=ctx)
        km = k.sb("km", [B, B, 512], ctx=ctx)
        prod = k.sb("dprod", [P, MH, B], ctx=ctx)
        hT = k.sb("dhT", [P, MH, B], ctx=ctx)
        t1 = k.sb("dt1", [P, MH, B], ctx=ctx)
        t2 = k.sb("dt2", [P, MH, B], ctx=ctx)
        block = ctx.enter_context(nc.Block())
        groups = [(a, min(3, BH - a)) for a in range(0, BH, 3)]
        i_, f = k.small_s[:, 24:28], k.small_s[:, 28:32]

        @block.sync
        def _(sp):
            sp.dma_start(m0[:, :], k.i["state_mlstm_m"][0]).then_inc(s_in, 16)
            sp.dma_start(n0[:, :], k.i["state_mlstm_n"][0].rearrange("b h d -> (b h) d")).then_inc(s_in, 16)
            sp.dma_start(C[:, :, 0:MD], k.i["state_mlstm_C"][0].rearrange("b h d e -> d (b h) e")).then_inc(s_in, 16)
            sp.wait_ge(s_C, 2 + len(groups))
            sp.dma_start(k.o["C_sample"][0].rearrange("b h d e -> d (b h) e"), C[:, :, 0:MD]).then_inc(s_st, 16)
            sp.wait_ge(s_chain, 4)
            sp.dma_start(k.o["m_sample"][0], mm_[:, :]).then_inc(s_st, 16)
            sp.wait_ge(s_nrow, 1)
            sp.dma_start(k.o["n_sample"][0].rearrange("b h d -> (b h) d"), nrow[:, :]).then_inc(s_st, 16)
            sp.wait_ge(s_st, 48)

        @block.vector
        def _(dve):
            ch = Chain(dve, s_chain)
            ch.link(dve.scalar_tensor_tensor(out=g1[:, :], in0=f, scalar=-1.0, in1=f, op0=ALU.mult, op1=ALU.max))
            dve.wait_ge(s_e, 2)
            dve.wait_ge(s_in, 48)
            ch.link(dve.scalar_tensor_tensor(out=g2[:, :], in0=f, scalar=0.0, in1=g1[:, :], op0=ALU.min, op1=ALU.subtract))
            ch.link(dve.tensor_tensor(g2[:, :], g2[:, :], m0[:, :], ALU.add))
            ch.link(dve.tensor_tensor(mm_[:, :], g2[:, :], i_, ALU.max))
            ch.link(dve.tensor_tensor(ein[:, 0], g2[:, :], mm_[:, :], ALU.subtract))
            ch.link(dve.tensor_scalar(ein[:, 1], mm_[:, :], -1.0, None, ALU.mult))
            ch.link(dve.tensor_tensor(ein[:, 2], i_, mm_[:, :], ALU.subtract))
            dve.wait_ge(s_e, 3)
            ch.link(dve.tensor_tensor(dg[:, :, :, :], k.ident[0:B, 0:B].unsqueeze(1).unsqueeze(3).to_broadcast([B, 2, B, MH]),
                                      ein[:, 0:2].unsqueeze(2).to_broadcast([B, 2, B, MH]), ALU.mult))
            ch.link(dve.tensor_tensor(kws[:, :].rearrange("b (h d) -> b h d", h=MH), k.kb_s[:, :].rearrange("b (h d) -> b h d", h=MH),
                                      ein[:, 2].unsqueeze(2).to_broadcast([B, MH, MD]), ALU.mult))
            for b in range(B):
                dve.tensor_scalar(km[:, b, :], kws[:, :], k.ident[0:B, b:b + 1], None, ALU.mult).then_inc(s_km, 1)
            dve.wait_ge(s_bcp, 1)
            dve.tensor_copy(wb[:, :, :], k.bank[7][:, 0:2 * BH].rearrange("p (a n) -> p a n", a=2)).then_inc(s_bcs, 1)
            dve.wait_ge(s_nT, 1)
            dve.tensor_copy(C[:, :, MD:W], k.bank[6][:, 0:BH].unsqueeze(2)).then_inc(s_C, 1)
            dve.wait_ge(s_bcs, 1)
            dve.wait_ge(s_C, 1)
            dve.tensor_tensor(C[:, :, :], C[:, :, :], wb[:, 0].unsqueeze(2).to_broadcast([P, BH, W]), ALU.mult).then_inc(s_C, 1)
            dve.wait_ge(s_C, 2)
            for n, (a, w) in enumerate(groups):
                dve.wait_ge(s_U, n + 1)
                dve.tensor_tensor(C[:, a:a + w, :], C[:, a:a + w, :],
                                  k.bank[n % 6][:, 0:w * W].rearrange("p (n e) -> p n e", n=w), ALU.add).then_inc(s_C, 1)
            dve.wait_ge(s_C, 2 + len(groups))
            ch.link(dve.tensor_copy(ncol[:, :], C[:, :, MD:W].rearrange("p n o -> p (n o)")))
            ch.link(dve.tensor_tensor(prod[:, :, :], ncol[:, :].rearrange("p (b h) -> p h b", h=MH), k.qbT[:, :, T:TT], ALU.mult))
            dve.wait_ge(s_h, 2)
            den = k.bank[1][:, 0:BH].rearrange("p (h b) -> p h b", h=MH)
            ch.link(dve.tensor_copy(t2[:, :, :], den))
            ch.link(dve.scalar_tensor_tensor(out=t1[:, :, :], in0=t2[:, :, :], scalar=-1.0, in1=t2[:, :, :], op0=ALU.mult, op1=ALU.max))
            ch.link(dve.tensor_tensor(t1[:, :, :], t1[:, :, :], wb[:, 1].rearrange("p (b h) -> p h b", h=MH), ALU.max))
            ch.link(dve.reciprocal(t1[:, :, :], t1[:, :, :]))
            ch.link(dve.tensor_tensor(hT[:, :, :], k.bank[0][:, 0:BH].rearrange("p (h b) -> p h b", h=MH), t1[:, :, :], ALU.mult))
            dve.wait_ge(s_sum, 1)
            ch.link(dve.scalar_tensor_tensor(out=hT[:, :, :], in0=k.bank[2][:, 0:BH].rearrange("p (h b) -> p h b", h=MH), scalar=-1.0 / MD,
                                             in1=hT[:, :, :], op0=ALU.mult, op1=ALU.add))
            ch.link(dve.tensor_tensor(t2[:, :, :], hT[:, :, :], hT[:, :, :], ALU.mult))
            dve.wait_ge(s_sum, 2)
            ch.link(dve.tensor_scalar(t1[:, :, :], k.bank[3][:, 0:BH].rearrange("p (h b) -> p h b", h=MH), 1.0 / MD, EPS, ALU.mult, ALU.add))
            dve.wait_ge(s_rt, 1)
            ch.link(dve.reciprocal(t1[:, :, :], t1[:, :, :]))
            ch.link(dve.tensor_tensor(hT[:, :, :], hT[:, :, :], t1[:, :, :], ALU.mult))
            ch.link(dve.tensor_tensor(k.hbT[:, :, T:TT], hT[:, :, :], k.vecT[:, 88:92].unsqueeze(2).to_broadcast([P, MH, B]), ALU.mult))
            dve.wait_ge(s_nT, 2)
            dve.tensor_copy(nrow[:, :], k.bank[5][0:BH, 0:P]).then_inc(s_nrow, 1)

        @block.scalar
        def _(act):
            act.wait_ge(s_chain, 1)
            act.activation(g1[:, :], g1[:, :], ACT.Exp, scale=-1.0).then_inc(s_e, 1)
            act.wait_ge(s_e, 1)
            act.activation(g1[:, :], g1[:, :], ACT.Ln, bias=1.0).then_inc(s_e, 1)
            act.wait_ge(s_chain, 7)
            act.activation(ein[:, :, :], ein[:, :, :], ACT.Exp).then_inc(s_e, 1)
            act.wait_ge(s_chain, 19)
            act.activation(t1[:, :, :], t1[:, :, :], ACT.Sqrt).then_inc(s_rt, 1)

        @block.tensor
        def _(pe):
            pe.wait_ge(s_in, 48)
            pe.transpose(k.bank[6][:, 0:BH], n0[:, :], k.ident[0:BH, 0:BH]).then_inc(s_nT, 1)
            pe.wait_ge(s_chain, 8)
            pe.matmul(k.bank[7][:, 0:2 * BH], k.ones[0:B, :], dg[:, :, :, :].rearrange("b a c h -> b (a c h)"), start=True, stop=True).then_inc(s_bcp, 1)
            pe.wait_ge(s_km, B)
            for n, (a, w) in enumerate(groups):
                if n >= 6:
                    pe.wait_ge(s_C, n - 3)
                for q in range(w):
                    b, h = (a + q) // MH, (a + q) % MH
                    mm = pe.matmul(k.bank[n % 6][:, q * W:q * W + W], km[:, b, P * h:P * h + P], k.vb_s[:, h, :], start=True, stop=True)
                mm.then_inc(s_U, 1)
            pe.wait_ge(s_C, 2 + len(groups))
            for b in range(B):
                for h in range(MH):
                    mm = pe.matmul(k.bank[0][:, h * B + b:h * B + b + 1], C[:, MH * b + h, 0:MD], k.qbT[:, h, T + b:T + b + 1], start=True, stop=True)
            mm.then_inc(s_h, 1)
            pe.wait_ge(s_chain, 10)
            pe.transpose(k.bank[5][0:BH, 0:P], ncol[:, :], k.ident[:, :]).then_inc(s_nT, 1)
            pe.wait_ge(s_chain, 11)
            pe.matmul(k.bank[1][:, 0:BH], k.ones[:, :], prod[:, :, :].rearrange("p h b -> p (h b)"), start=True, stop=True).then_inc(s_h, 1)
            pe.wait_ge(s_chain, 16)
            pe.matmul(k.bank[2][:, 0:BH], k.ones[:, :], hT[:, :, :].rearrange("p h b -> p (h b)"), start=True, stop=True).then_inc(s_sum, 1)
            pe.wait_ge(s_chain, 18)
            pe.matmul(k.bank[3][:, 0:BH], k.ones[:, :], t2[:, :, :].rearrange("p h b -> p (h b)"), start=True, stop=True).then_inc(s_sum, 1)


def nsa_project(k):
    nc = k.nc
    w_v = k.i["w_in"][0].rearrange("(k p) n -> p k n", p=P)
    s_wq, s_wk, s_fill, s_evq, s_evk, s_kT, s_out = (k.sem(f"s_n_{x}") for x in ("wq", "wk", "fill", "evq", "evk", "kT", "out"))
    s_kTs = k.sem("s_n_kTs")
    s_gate, s_u = k.sem("s_n_gate"), k.sem("s_n_u")
    with ExitStack() as ctx:
        uT = k.sb("nuT", [P, DK, TT], ctx=ctx)
        kv_s = k.sb("kv_s", [B, 768], ctx=ctx)
        wq = k.sb("nwq", [P, DK, 4, G, HD], ctx=ctx)
        wk = k.sb("nwk", [P, DK, 768], ctx=ctx)
        block = ctx.enter_context(nc.Block())
        NQ = 4 * NG

        @block.sync
        def _(sp):
            sp.dma_start(uT[:, :, :], k.uT_d).then_inc(s_u, 16)
            for c in range(DK):
                for g in range(G):
                    sp.dma_start(wq[:, c, :, g, :], w_v[:, c, 256 * g:256 * g + 256].rearrange("p (j d) -> p j d", j=4)).then_inc(s_wq, 16)
            sp.dma_start(wk[:, :, :], w_v[:, :, OFF_KVA:OFF_GA]).then_inc(s_wk, 16)
            win = k.o["win_sample"][0].rearrange("b w v g d -> b w (v g d)")
            old = k.i["cache_nsa_win"][0].rearrange("b w v g d -> b w (v g d)")
            sp.dma_start(win[:, 0:WIN - 1, :], old[:, 1:WIN, :]).then_inc(s_out, 16)
            sp.wait_ge(s_evk, 2 * (NTI + 1))
            kv = k.o["kv_prompt"][0, 0].rearrange("(c p) v g d -> p c (v g d)", p=P)
            sp.dma_start(kv, k.kv[:, :, 0:512]).then_inc(s_out, 16)
            wp = k.o["win_prompt"][0, 0].rearrange("(c p) v g d -> p c (v g d)", p=P)
            sp.dma_start(wp, k.kv[:, NTI - WIN // P:NTI, 512:768]).then_inc(s_out, 16)
            sp.dma_start(k.o["kv_sample"][0].rearrange("b o v g d -> b (o v g d)"), kv_s[:, 0:512]).then_inc(s_out, 16)
            sp.dma_start(win[:, WIN - 1, :], kv_s[:, 512:768]).then_inc(s_out, 16)
            sp.wait_ge(s_out, 80)

        @block.tensor
        def _(pe):
            fill = 0
            pe.wait_ge(s_u, 16)
            pe.wait_ge(s_wq, 16 * DK * G)
            for j in range(4):
                for g in range(NG):
                    if fill >= 8:
                        pe.wait_ge(s_evq, fill - 7)
                    for kk in range(DK):
                        mm = pe.matmul(k.bank[fill % 8][:, 0:GT], wq[:, kk, j].rearrange("p g d -> p (g d)"),
                                       uT[:, kk, GT * g:GT * g + GT], start=(kk == 0), stop=(kk == DK - 1))
                    mm.then_inc(s_fill, 1)
                    fill += 1
            pe.wait_ge(s_wk, 16)
            for ti in range(NTI + 1):
                m = P if ti < NTI else B
                for half in range(2):
                    old = fill - 8
                    if old < NQ:
                        pe.wait_ge(s_evq, old + 1)
                    else:
                        pe.wait_ge(s_evk, old - NQ + 1)
                    for kk in range(DK):
                        mm = pe.matmul(k.bank[fill % 8][0:m, 0:384], uT[:, kk, P * ti:P * ti + m],
                                       wk[:, kk, 384 * half:384 * half + 384], start=(kk == 0), stop=(kk == DK - 1))
                    mm.then_inc(s_fill, 1)
                    fill += 1
            pe.wait_ge(s_evk, 2 * (NTI + 1))
            for n in range(4):
                for q in range(4):
                    ti = 4 * (n % 2) + q
                    off = 256 if n < 2 else 512
                    mm = pe.transpose(k.bank[n][:, P * q:P * q + P], k.kv[:, ti, off:off + P], k.ident[:, :])
                mm.then_inc(s_kT, 1)

        @block.scalar
        def _(act):
            act.activation(k.small[:, :, 0:24], k.small[:, :, 0:24], ACT.Sigmoid).then_inc(s_gate, 1)
            for f in range(NQ):
                act.wait_ge(s_fill, f + 1)
                j, g = f // NG, f % NG
                act.activation(k.qT[:, j, GT * g:GT * g + GT], k.bank[f % 8][:, 0:GT], ACT.Copy, scale=float(HD) ** -0.5).then_inc(s_evq, 1)

        @block.vector
        def _(dve):
            for n in range(2 * (NTI + 1)):
                f = NQ + n
                ti, half = n // 2, n % 2
                dve.wait_ge(s_fill, f + 1)
                m = P if ti < NTI else B
                dst = k.kv[:, ti, 384 * half:384 * half + 384] if ti < NTI else kv_s[:, 384 * half:384 * half + 384]
                dve.tensor_copy(dst, k.bank[f % 8][0:m, 0:384]).then_inc(s_evk, 1)
            dve.wait_ge(s_evq, NQ)
            dve.tensor_copy(k.qTs[:, :, :], k.qT[:, :, T:TT]).then_inc(s_kTs, 1)
            for n in range(4):
                dve.wait_ge(s_kT, n + 1)
                dst = k.ksT if n < 2 else k.kwT
                dve.tensor_copy(dst[:, 512 * (n % 2):512 * (n % 2) + 512], k.bank[n][:, :]).then_inc(s_kTs, 1)


def prompt_compress(k):
    nc = k.nc
    NPP = T // STRIDE
    s_raw, s_w1, s_w2, s_pe = k.sem("s_pr_raw"), k.sem("s_pr_w1"), k.sem("s_pr_w2"), k.sem("s_pr_pe")
    s_tr, s_xt, s_hid, s_gelu, s_out, s_outs, s_zero = (k.sem(f"s_pr_{x}") for x in ("tr", "xt", "hid", "gelu", "o", "os", "z"))
    with ExitStack() as ctx:
        w1 = k.sb("pw1", [P, 2, 2, 8, CH], ctx=ctx)
        w2 = k.sb("pw2", [P, 2, 2, HD], ctx=ctx)
        perow = k.sb("pperow", [32, P], ctx=ctx)
        turned = k.sb("pturned", [NPP, G, STRIDE, HD], ctx=ctx)
        xt = k.sb("pxt", [P, 2, 8, G, NPP], ctx=ctx)
        hid = k.sb("phid", [P, 2, 2, G, NPP], ctx=ctx)
        block = ctx.enter_context(nc.Block())

        @block.sync
        def _(sp):
            load_cmp_weights(k, sp, w1, w2, perow, (s_w1, s_w2, s_pe))
            src = k.o["kv_prompt"][0, 0].rearrange("(n s) v g d -> n s v g d", s=STRIDE)
            for kv in range(2):
                if kv:
                    sp.wait_ge(s_tr, 2)
                for g in range(G):
                    sp.dma_start(turned[:, g], src[:, :, kv, g, :]).then_inc(s_raw, 16)
            sp.wait_ge(s_pe, 16)

        @block.gpsimd
        def _(pool):
            pool.memset(hid[:, :, :, :, NCP:NPP], 0.0).then_inc(s_zero, 1)

        @block.tensor
        def _(pe):
            for f in range(4):
                kv, half = f // 2, f % 2
                pe.wait_ge(s_raw, 32 * (kv + 1))
                for q in range(4):
                    for g in range(G):
                        s2 = 2 * (4 * half + q)
                        mm = pe.transpose(k.bank[f][:, NPP * (2 * q + g):NPP * (2 * q + g) + NPP],
                                          turned[:, g, s2:s2 + 2, :].rearrange("p s d -> p (s d)"), k.ident[0:NPP, 0:NPP])
                mm.then_inc(s_tr, 1)
            pe.wait_ge(s_w1, 32)
            pe.wait_ge(s_w2, 32)
            pe.wait_ge(s_xt, 4)
            for kv in range(2):
                for c in range(2):
                    for j in range(16):
                        mm = pe.matmul(k.bank[4 + 2 * kv + c][:, 0:2 * NCP], w1[:, kv, j // 8, j % 8, P * c:P * c + P],
                                       xt[:, kv, j % 8, :, j // 8:j // 8 + NCP], start=(j == 0), stop=(j == 15))
                    mm.then_inc(s_hid, 1)
            for kv in range(2):
                pe.wait_ge(s_gelu, 2 * kv + 2)
                for g in range(G):
                    for c in range(2):
                        if kv == 0:
                            mm = pe.matmul(k.bank[0][HD * g:HD * g + HD, 0:NPP], w2[:, 0, c, :], hid[:, 0, c, g, :],
                                           start=(c == 0), stop=(c == 1))
                        else:
                            mm = pe.matmul(k.bank[1][0:NPP, HD * g:HD * g + HD], hid[:, 1, c, g, :], w2[:, 1, c, :],
                                           start=(c == 0), stop=(c == 1))
                mm.then_inc(s_out, 1)

        @block.vector
        def _(dve):
            for f in range(4):
                kv, half = f // 2, f % 2
                dve.wait_ge(s_tr, f + 1)
                dve.tensor_copy(xt[:, kv, 4 * half:4 * half + 4].rearrange("p q g n -> p (q g n)"), k.bank[f][:, :]).then_inc(s_xt, 1)
            dve.wait_ge(s_out, 1)
            dve.tensor_copy(k.kcpT[:, :], k.bank[0][:, 0:NPP]).then_inc(s_outs, 1)
            dve.wait_ge(s_out, 2)
            dve.tensor_copy(k.vcp[:, :], k.bank[1][0:NPP, 0:P]).then_inc(s_outs, 1)

        @block.scalar
        def _(act):
            act.wait_ge(s_zero, 1)
            for kv in range(2):
                for c in range(2):
                    act.wait_ge(s_hid, 2 * kv + c + 1)
                    act.activation(hid[:, kv, c, :, 0:NCP], k.bank[4 + 2 * kv + c][:, 0:2 * NCP].rearrange("p (g n) -> p g n", g=G),
                                   ACT.Gelu_apprx_tanh, bias=k.peb[:, kv, c:c + 1]).then_inc(s_gelu, 1)


def prompt_attention(k):
    nc = k.nc
    assert T // SEL <= TOPN
    s_strip = [k.sem(f"s_pa_strip{g}") for g in range(G)]
    s_q, s_wf, s_sc, s_add, s_nm, s_exp, s_T, s_pta, s_ptd, s_pv, s_o, s_ch = (
        k.sem(f"s_pa_{x}") for x in ("q", "wf", "sc", "add", "nm", "exp", "T", "pta", "ptd", "pv", "o", "ch"))
    s_l, s_oT, s_oTs, s_mz = (k.sem(f"s_pa_{x}") for x in ("l", "oT", "oTs", "mz"))
    NU = G * NTI
    units = [(g, ti) for g in range(G) for ti in range(NTI)]
    GATE = (1, 2, 0)
    WOFF, COFF, SW = T, T + 5 * P, T + 5 * P + 64

    def ptiles(ti):
        sel = [(P * s, P) for s in range(ti + 1)]
        nw = min(ti + 1, 5)
        win = [(WOFF + P * s, P) for s in range(5 - nw, 5)]
        return sel, win, [(COFF, min(8 * ti + 7, NCP))]

    fills = []
    for u, (g, ti) in enumerate(units):
        n = sum(len(x) for x in ptiles(ti))
        a = m = 0
        while a < n:
            w = min(4, n - a) - (n - a == 5)
            fills.append((u, a, w, m))
            a, m = a + w, m + 1
    NFA = sum(1 for f in fills if f[3] % 2 == 0)
    NFD = len(fills) - NFA

    def copied(upto, odd):
        return sum(1 for f in fills[:upto] if f[3] % 2 == odd)

    with ExitStack() as ctx:
        strip = k.sb("strip", [P, G, T], ctx=ctx)
        wf = k.sb("wfirst", [P, G, P], ctx=ctx)
        qh = k.sb("qh", [P, T], ctx=ctx)
        S = k.sb("Sp", [P, 2, SW], ctx=ctx)
        E = k.sb("Ep", [P, 2, SW], ctx=ctx)
        PT = k.sb("PTp", [P, 2, 14, P], ctx=ctx)
        mxp = k.sb("mxp", [P, 3, 2], ctx=ctx)
        mx3 = k.sb("mx3", [P, 3], ctx=ctx)
        nm = k.sb("nm", [P, 2, 3], ctx=ctx)
        ls = k.sb("ls", [P, 4, 3], ctx=ctx)
        rr = k.sb("rr", [P, 3], ctx=ctx)
        ob = k.sb("ob", [P, 3, HD], ctx=ctx)
        oA = k.sb("oA", [P, NTI, 4, G, HD], ctx=ctx)
        block = ctx.enter_context(nc.Block())

        @block.sync
        def _(sp):
            def load(i, g):
                h_off = (i + 4 * g) * NFWD
                src = bass.AP(k.biasfwd_d.tensor, h_off, [[1, P], [1, T]])
                sp.dma_start(strip[:, g, :], src).then_inc(s_strip[g], 16)

            load(0, 0)
            load(0, 1)
            with sp.Fori(1, 4) as i:
                for g in range(G):
                    sp.wait_ge(s_add, i * NU + (NTI * (g + 1) - NU))
                    load(i, g)

        @block.gpsimd
        def _(pool):
            def prepare(i, g):
                half = slice(HD * g, HD * g + HD)
                if i:
                    pool.wait_ge(s_sc, i * NU + (NTI * (g + 1) - NU))
                if i or g:
                    pool.wait_ge(s_wf, i * G + g)
                pool.tensor_copy(qh[half, :], k.qT[half, bass.ds(i, 1), 0:T].rearrange("p o t -> p (o t)")).then_inc(s_q, 1)
                pool.wait_ge(s_q, i * G + (g + 1))
                pool.wait_ge(s_strip[g], i * 16 + 16)
                pool.affine_select(out=wf[:, g, :], in_=strip[:, g, 5 * P - 1:4 * P - 1:-1], compare_op=ALU.is_ge, fill=NEG,
                                   base=-1, pattern=[[1, P]], channel_multiplier=-1).then_inc(s_wf, 1)

            for i in range(4):
                prepare(i, 0)
                prepare(i, 1)

        @block.tensor
        def _(pe):
            def scores(i, u):
                g, ti = units[u]
                half = slice(HD * g, HD * g + HD)
                q = qh[half, P * ti:P * ti + P]
                if ti == 0:
                    pe.wait_ge(s_q, i * G + (g + 1))
                pe.wait_ge(s_add, i * NU + u)
                n = P * (ti + 1)
                for a in range(0, n, 512):
                    pe.matmul(k.bank[a // 512][:, 0:min(512, n - a)], q, k.ksT[half, a:min(a + 512, n)], start=True, stop=True)
                if ti >= 4:
                    pe.matmul(k.bank[2][:, 0:P], q, k.kwT[half, P * (ti - 4):P * (ti - 3)], start=True, stop=True)
                lo = P * max(ti - 3, 0)
                pe.matmul(k.bank[3][:, 0:n - lo], q, k.kwT[half, lo:n], start=True, stop=True)
                nn = min(8 * ti + 7, NCP)
                pe.matmul(k.bank[2][:, P:P + nn], q, k.kcpT[half, 0:nn], start=True, stop=True).then_inc(s_sc, 1)

            def turn(i, u):
                g, ti = units[u]
                tiles = [t for x in ptiles(ti) for t in x]
                pe.wait_ge(s_exp, i * NU + (u + 1))
                for n, (uu, a, w, m) in enumerate(fills):
                    if uu != u:
                        continue
                    if m == 3:
                        pe.wait_ge(s_pta, i * NFA + copied(n - 2, 0))
                    elif m == 0:
                        pe.wait_ge(s_pta, i * NFA + copied(n, 0))
                        pe.wait_ge(s_ptd, i * NFD + copied(n, 1))
                    for q in range(w):
                        col, kk = tiles[a + q]
                        mm = pe.transpose(k.bank[4 + m % 3][0:kk, P * q:P * q + P], E[:, u % 2, col:col + kk], k.ident[:, :])
                    mm.then_inc(s_T, 1)

            def products(i, u):
                g, ti = units[u]
                n = max(m for m, f in enumerate(fills) if f[0] == u) + 1
                pe.wait_ge(s_pta, i * NFA + copied(n, 0))
                pe.wait_ge(s_ptd, i * NFD + copied(n, 1))
                pe.wait_ge(s_o, i * NU + u)
                t = 0
                for br, tl in enumerate(ptiles(ti)):
                    for m in range(len(tl)):
                        if br == 0:
                            v = k.kv[:, m, 384 + HD * g:384 + HD * g + HD]
                        elif br == 1:
                            v = k.kv[:, ti + 1 - len(tl) + m, 640 + HD * g:640 + HD * g + HD]
                        else:
                            v = k.vcp[0:tl[0][1], HD * g:HD * g + HD]
                        mm = pe.matmul(k.bank[7][:, HD * GATE[br]:HD * GATE[br] + HD], PT[0:tl[m][1], u % 2, t, :], v,
                                       start=(m == 0), stop=(m == len(tl) - 1))
                        t += 1
                mm.then_inc(s_pv, 1)

            with pe.Fori(0, 4) as i:
                scores(i, 0)
                for u in range(NU):
                    if u + 1 < NU:
                        scores(i, u + 1)
                    turn(i, u)
                    if u:
                        products(i, u - 1)
                products(i, NU - 1)
            pe.wait_ge(s_o, 4 * NU)
            for ti in range(NTI):
                if ti >= 4:
                    pe.wait_ge(s_oTs, ti - 3)
                for j in range(4):
                    mm = pe.transpose(k.bank[ti % 4][:, P * j:P * j + P], oA[:, ti, j].rearrange("p g d -> p (g d)"), k.ident[:, :])
                mm.then_inc(s_oT, 1)

        def copies(eng, i, u, odd, sem):
            for n, (uu, a, w, m) in enumerate(fills):
                if uu != u or m % 2 != odd:
                    continue
                g, ti = units[u]
                eng.wait_ge(s_T, i * len(fills) + (n + 1))
                if m < 2:
                    eng.wait_ge(s_pv, i * NU + max(u - 1, 0))
                tiles = [t for x in ptiles(ti) for t in x]
                full = [x for x in tiles[a:a + w] if x[1] == P]
                parts = []
                if full:
                    parts.append((PT[:, u % 2, a:a + len(full), :], k.bank[4 + m % 3][:, 0:P * len(full)].rearrange("p (q t) -> p q t", t=P)))
                if len(full) < w:
                    kk = tiles[a + w - 1][1]
                    parts.append((PT[0:kk, u % 2, a + w - 1, :], k.bank[4 + m % 3][0:kk, P * (w - 1):P * w]))
                for dst, src in parts:
                    ins = eng.tensor_copy(dst, src) if odd else eng.activation(dst, src, ACT.Copy)
                ins.then_inc(sem, 1)

        @block.vector
        def _(dve):
            ch = Chain(dve, s_ch)
            PER = 6 * NU

            def addmax(i, u):
                g, ti = units[u]
                if ti == 0:
                    dve.wait_ge(s_strip[g], i * 16 + 16)
                    dve.wait_ge(s_wf, i * G + (g + 1))
                if u >= 2:
                    dve.wait_ge(s_exp, i * NU + (u - 1))
                else:
                    dve.wait_ge(s_exp, i * NU)
                dve.wait_ge(s_sc, i * NU + (u + 1))
                nn = min(8 * ti + 7, NCP)
                dve.tensor_tensor(S[:, u % 2, COFF:COFF + nn], k.bank[2][:, P:P + nn], strip[:, g, P * ti + 96:(P * ti + 96 - STRIDE * nn if P * ti + 96 >= STRIDE * nn else None):-STRIDE],
                                  ALU.add).then_inc(s_mz, 1)
                n = P * (ti + 1)
                parts = []
                x0 = P * ti + P - 1
                for a in range(0, n, 512):
                    w = min(512, n - a)
                    lo = x0 - a - w
                    parts.append((0, a // 512, a, w, a // 512, 0, strip[:, g, x0 - a:lo if lo >= 0 else None:-1]))
                lo = P * max(ti - 3, 0)
                w = n - lo
                parts.append((1, 0, WOFF + 5 * P - w, w, 3, 0, strip[:, g, w - 1::-1]))
                if ti >= 4:
                    parts.append((1, 1, WOFF, P, 2, 0, wf[:, g, :]))
                for m, (br, sl, col, w, bank, bc, bias) in enumerate(parts):
                    dve.tensor_tensor_reduce(S[:, u % 2, col:col + w], k.bank[bank][:, bc:bc + w], bias, 1.0, NEG,
                                             ALU.add, ALU.max, mxp[:, br, sl:sl + 1]).then_inc(s_add if m == len(parts) - 1 else s_mz, 1)

            mz = [sum(4 if t >= 4 else 2 for _, t in units[:u + 1]) for u in range(NU)]

            def bounds(i, u):
                g, ti = units[u]
                dve.wait_ge(s_mz, i * mz[-1] + (mz[u] + 1))
                dve.wait_ge(s_add, i * NU + (u + 1))
                ch.step(dve.tensor_reduce(mx3[:, 0:2], mxp[:, 0:2, 0:2 if ti >= 4 else 1], AX.X, ALU.max))
                ch.link(dve.tensor_reduce(mx3[:, 2:3], S[:, u % 2, COFF:COFF + min(8 * ti + 7, NCP)], AX.X, ALU.max))
                dve.tensor_scalar(nm[:, u % 2, :], mx3[:, :], FLOOR, -1.0, ALU.max, ALU.mult).then_inc(s_nm, 1)

            def output(i, u):
                g, ti = units[u]
                ch.link(dve.tensor_scalar(rr[:, :], ls[:, u % 4, :], 1e-30, None, ALU.max))
                ch.link(dve.reciprocal(rr[:, :], rr[:, :]))
                ch.link(dve.tensor_tensor(rr[:, :], rr[:, :], k.small[:, ti, bass.ds(i * 3 + 12 * g, 3)], ALU.mult))
                dve.wait_ge(s_pv, i * NU + (u + 1))
                ch.link(dve.tensor_tensor(ob[:, :, :], k.bank[7][:, 0:3 * HD].rearrange("p (b d) -> p b d", b=3),
                                          rr[:, :].unsqueeze(2).to_broadcast([P, 3, HD]), ALU.mult))
                dve.tensor_reduce(oA[:, ti, bass.ds(i, 1), g, :].rearrange("p o d -> p (o d)"), ob[:, :, :].rearrange("p b d -> p d b"),
                                  AX.X, ALU.add).then_inc(s_o, 1)
                dve.wait_ge(s_o, i * NU + (u + 1))

            dve.memset(mxp[:, :, :], NEG).then_inc(s_mz, 1)
            dve.wait_ge(s_mz, 1)
            with dve.Fori(0, 4) as i:
                ch.start(i, 6 * NU)
                addmax(i, 0)
                bounds(i, 0)
                for u in range(NU):
                    if u + 1 < NU:
                        addmax(i, u + 1)
                        bounds(i, u + 1)
                    copies(dve, i, u, 1, s_ptd)
                    if u:
                        output(i, u - 1)
                output(i, NU - 1)
                ch.done()
            for ti in range(NTI):
                dve.wait_ge(s_oT, ti + 1)
                dve.tensor_copy(k.oaT[:, :, P * ti:P * ti + P], k.bank[ti % 4][:, :].rearrange("p (j t) -> p j t", j=4)).then_inc(s_oTs, 1)

        @block.scalar
        def _(act):
            def exps(i, u):
                g, ti = units[u]
                act.wait_ge(s_nm, i * NU + (u + 1))
                act.wait_ge(s_T, i * len(fills) + (sum(1 for f in fills if f[0] < u - 1)))
                act.wait_ge(s_o, i * NU + max(u - 3, 0))
                nn = min(8 * ti + 7, NCP)
                nw = P * min(ti + 1, 5)
                for br, (col, w) in enumerate(((0, P * (ti + 1)), (WOFF + 5 * P - nw, nw), (COFF, nn))):
                    ins = act.activation(E[:, u % 2, col:col + w], S[:, u % 2, col:col + w], ACT.Exp,
                                         bias=nm[:, u % 2, br:br + 1], accum_out=ls[:, u % 4, GATE[br]:GATE[br] + 1])
                ins.then_inc(s_exp, 1)

            with act.Fori(0, 4) as i:
                exps(i, 0)
                for u in range(NU):
                    copies(act, i, u, 0, s_pta)
                    if u + 1 < NU:
                        exps(i, u + 1)


def decode_attention(k):
    nc = k.nc
    BG = B * G
    NSELK = TOPN * SEL
    s_q0, s_qp, s_win, s_pt, s_gt = (k.sem(f"s_da_{x}") for x in ("q0", "qp", "win", "pt", "gt"))
    s_new = [k.sem(f"s_da_new{j}") for j in range(2)]
    s_const, s_cst2, s_kT, s_kTs, s_sc, s_ch = (k.sem(f"s_da_{x}") for x in ("const", "cst2", "kT", "kTs", "sc", "ch"))
    s_exp, s_imp, s_tb, s_idx, s_bidx, s_bg, s_rows = (k.sem(f"s_da_{x}") for x in ("exp", "imp", "tb", "idx", "bidx", "bg", "rows"))
    s_ga = [k.sem(f"s_da_ga{j}") for j in range(2)]
    s_sT, s_sTd, s_sTs, s_vs, s_ssc, s_pT, s_pTs, s_o, s_od = (k.sem(f"s_da_{x}") for x in ("sT", "sTd", "sTs", "vs", "ssc", "pT", "pTs", "o", "od"))
    s_sig, s_kcv = k.sem("s_da_sig"), k.sem("s_da_kcv")
    rows = k.i["cache_nsa_kv"][0].rearrange("q t (s v) g d -> (q t s) (v g d)", s=2)
    brow = k.biasrev_d.rearrange("h (n r) -> (h n) r", r=SEL)
    NBR = NREV // SEL
    with ExitStack() as ctx:
        kcT = k.sb("dkcT", [P, B, NPIECE], ctx=ctx)
        vc = k.sb("dvc", [P, B, 4, P], ctx=ctx)
        qp = k.sb("qpad", [P, 8 * 72], ctx=ctx)
        win = k.sb("dwin", [P, B, 4, 256], ctx=ctx)
        wT = k.sb("dwT", [P, 2, WIN], ctx=ctx)
        S = k.sb("dS", [64, 2 * 512 + NSELK], ctx=ctx)
        mx = k.sb("dmx", [64, 4], ctx=ctx)
        nm = k.sb("dnm", [64, 4], ctx=ctx)
        ls = k.sb("dls", [64, 4], ctx=ctx)
        gt = k.sb("dgt", [64, 3], ctx=ctx)
        gsel = k.sb("gsel", [64, BG], ctx=ctx)
        gselT = k.sb("gselT", [BG, 64], ctx=ctx)
        iota = k.sb("diota", [BG, P], ctx=ctx)
        coli = k.sb("dcoli", [P, 1], I32, ctx=ctx)
        colf = k.sb("dcolf", [P, 1], ctx=ctx)
        hrow = k.sb("dhrow", [64, 1], ctx=ctx)
        prow = k.sb("dprow", [P, 1], ctx=ctx)
        iti = k.sb("diti", [P, P], I32, ctx=ctx)
        pti = k.sb("dpti", [BG, NPAGES], I32, ctx=ctx)
        tokb = k.sb("dtokb", [BG, NPAGES, 2], ctx=ctx)
        imp = k.sb("dimp", [BG, P], ctx=ctx)
        imp2 = k.sb("dimp2", [BG, P], ctx=ctx)
        v8 = k.sb("dv8", [BG, TOPN], ctx=ctx)
        ix = k.sb("dix", [BG, TOPN], U32, ctx=ctx)
        ixf = k.sb("dixf", [BG, TOPN], ctx=ctx)
        tb = k.sb("dtb", [BG, TOPN], ctx=ctx)
        hit = k.sb("dhit", [BG, 2, P], ctx=ctx)
        tbd = k.sb("dtbd", [BG, BG, TOPN], ctx=ctx)
        gidx = k.sb("dgidx", [P, BG, 8], U32, ctx=ctx)
        bidx = k.sb("dbidx", [64, TOPN], U32, ctx=ctx)
        bsel = k.sb("dbsel", [64, NSELK], ctx=ctx)
        kvs = k.sb("dkvs", [P, 2, 8, 256], ctx=ctx)
        sT = k.sb("dsT", [P, 2, NSELK], ctx=ctx)
        vsel = k.sb("dvsel", [P, BG, 8, HD], ctx=ctx)
        pT = k.sb("dpT", [P, 16, 64], ctx=ctx)
        block = ctx.enter_context(nc.Block())

        @block.sync
        def _(sp):
            sp.dma_start(kcT[:, :, :], k.kcT_d).then_inc(s_kcv, 16)
            for b in range(B):
                sp.dma_start(win[:, b], k.o["win_sample"][0, b].rearrange("(c p) v g d -> p c (v g d)", p=P)).then_inc(s_win, 16)
            for bg in range(BG):
                sp.dma_start(pti[bg:bg + 1, :], k.i["page_table"][bg // G:bg // G + 1, :]).then_inc(s_pt, 16)
            for b in range(B):
                sp.dma_start(gt[8 * b:8 * b + 8, :], k.smalltok_d[b, 0:24].rearrange("(h r) -> h r", r=3)).then_inc(s_gt, 16)
            sp.dma_start(vc[:, :, :, :], k.vc_d).then_inc(s_kcv, 16)
            new = k.o["kv_sample"][0].rearrange("b o v g d -> b (o v g d)")
            for bg in range(BG):
                sp.wait_ge(s_ga[bg % 2], 128 * (bg // 2 + 1))
                sp.dma_start(kvs[64:65, bg % 2, 7, :], new[bg // 2:bg // 2 + 1, 256:512]).then_inc(s_new[bg % 2], 16)
            for j in range(2):
                sp.wait_ge(s_new[j], 8 * BG)

        @block.gpsimd
        def _(pool):
            pool.memset(qp[:, :], 0.0).then_inc(s_q0, 1)
            pool.memset(gsel[:, :], 1.0).then_inc(s_const, 1)
            pool.memset(gselT[:, :], 1.0).then_inc(s_const, 1)
            pool.iota(iti[:, :], pattern=[[1, P]], base=0, channel_multiplier=0).then_inc(s_const, 1)
            pool.iota(coli[:, :], pattern=[[0, 1]], base=0, channel_multiplier=1).then_inc(s_const, 1)
            pool.wait_ge(s_const, 4)
            pool.affine_select(out=gsel[:, :], in_=gsel[:, :], compare_op=ALU.is_ge, fill=0.0, base=0,
                               pattern=[[-4, BG]], channel_multiplier=1).then_inc(s_const, 1)
            pool.affine_select(out=gselT[:, :], in_=gselT[:, :], compare_op=ALU.is_ge, fill=0.0, base=0,
                               pattern=[[1, 64]], channel_multiplier=-4).then_inc(s_const, 1)
            pool.wait_ge(s_const, 6)
            pool.affine_select(out=gsel[:, :], in_=gsel[:, :], compare_op=ALU.is_ge, fill=0.0, base=3,
                               pattern=[[4, BG]], channel_multiplier=-1).then_inc(s_const, 1)
            pool.affine_select(out=gselT[:, :], in_=gselT[:, :], compare_op=ALU.is_ge, fill=0.0, base=3,
                               pattern=[[-1, 64]], channel_multiplier=4).then_inc(s_const, 1)
            pool.wait_ge(s_bidx, 1)
            for n in range(TOPN):
                pool.indirect_dma_start(out=bsel[:, SEL * n:SEL * n + SEL], out_offset=None, in_=brow,
                                        in_offset=bass.IndirectOffsetOnAxis(ap=bidx[:, n:n + 1], axis=0)).then_inc(s_bg, 16)
            pool.wait_ge(s_idx, 2)
            for bg in range(BG):
                if bg >= 2:
                    pool.wait_ge(s_sT, 2 * (bg - 1))
                    pool.wait_ge(s_vs, bg - 1)
                for m in range(8):
                    pool.indirect_dma_start(out=kvs[:, bg % 2, m, :], out_offset=None, in_=rows,
                                            in_offset=bass.IndirectOffsetOnAxis(ap=gidx[:, bg, m:m + 1], axis=0)).then_inc(s_ga[bg % 2], 16)

        @block.vector
        def _(dve):
            ch = Chain(dve, s_ch)
            dve.wait_ge(s_q0, 1)
            for g in range(G):
                half = slice(HD * g, HD * g + HD)
                dve.tensor_copy(qp[half, :].rearrange("p (b x) -> p b x", x=72)[:, :, 4 * g:4 * g + 4],
                                k.qTs[half, :, :].rearrange("p j b -> p b j")).then_inc(s_qp, 1)
            for b in range(B):
                dve.wait_ge(s_kT, b + 1)
                if b >= 2:
                    dve.wait_ge(s_sc, b - 1 + 1)
                dve.tensor_copy(wT[:, b % 2, :], k.bank[2 + b % 2][:, :]).then_inc(s_kTs, 1)
            dve.wait_ge(s_sc, 1)
            ch.link(dve.tensor_tensor_reduce(S[:, 0:512], k.bank[0][0:64, :], k.bias_cmp[:, :], 1.0, NEG, ALU.add, ALU.max, mx[:, 0:1]))
            ch.link(dve.tensor_scalar(nm[:, 0:1], mx[:, 0:1], FLOOR, -1.0, ALU.max, ALU.mult))
            dve.wait_ge(s_exp, 1)
            ch.link(dve.tensor_scalar(mx[:, 0:1], ls[:, 0:1], 1e-30, None, ALU.max))
            ch.link(dve.reciprocal(mx[:, 0:1], mx[:, 0:1]))
            ch.link(dve.tensor_scalar(S[:, 0:512], S[:, 0:512], mx[:, 0:1], None, ALU.mult))
            dve.wait_ge(s_imp, 1)
            ch.link(dve.tensor_reduce(imp[:, :], k.bank[4][0:BG, :].rearrange("p (j r) -> p j r", r=4), AX.X, ALU.add))
            ch.link(dve.tensor_tensor(imp[:, 1:P], imp[:, 1:P], k.bank[4][0:BG, 3:3 + 4 * (P - 1):4], ALU.add))
            ch.link(dve.memset(imp[:, 0:1], 1e9))
            ch.link(dve.memset(imp[:, P - 1:P], 1e9))
            ch.link(dve.max(v8[:, 0:8], imp[:, :]))
            ch.link(dve.max_index(ix[:, 0:8], v8[:, 0:8], imp[:, :]))
            ch.link(dve.match_replace(imp2[:, :], v8[:, 0:8], imp[:, :], NEG))
            ch.link(dve.max(v8[:, 8:16], imp2[:, :]))
            ch.link(dve.max_index(ix[:, 8:16], v8[:, 8:16], imp2[:, :]))
            ch.link(dve.tensor_copy(ixf[:, :], ix[:, :]))
            dve.wait_ge(s_const, 8)
            ch.link(dve.tensor_copy(iota[:, :], iti[0:BG, :]))
            dve.wait_ge(s_pt, 16 * BG)
            for r in range(2):
                ch.link(dve.tensor_scalar(tokb[:, :, r], pti[:, :], 2.0 * PAGE, 2.0 * SEL * r, ALU.mult, ALU.add))
            for n in range(TOPN):
                if n >= 2:
                    dve.wait_ge(s_tb, n - 1)
                dve.scalar_tensor_tensor(out=hit[:, n % 2, :], in0=iota[:, :], scalar=ixf[:, n:n + 1],
                                         in1=tokb[:, :, :].rearrange("p a r -> p (a r)"), op0=ALU.is_equal, op1=ALU.mult).then_inc(s_rows, 1)
                dve.wait_ge(s_rows, n + 1)
                dve.tensor_reduce(tb[:, n:n + 1], hit[:, n % 2, :], AX.X, ALU.add).then_inc(s_tb, 1)
            dve.wait_ge(s_tb, TOPN)
            ch.link(dve.tensor_tensor(tbd[:, :, :], k.ident[0:BG, 0:BG].unsqueeze(2).to_broadcast([BG, BG, TOPN]),
                                      tb[:, :].unsqueeze(1).to_broadcast([BG, BG, TOPN]), ALU.mult))
            ch.link(dve.memset(ixf[:, TOPN - 1:TOPN], float(PAST // SEL)))
            ch.link(dve.tensor_copy(colf[:, :], coli[:, :]))
            ch.link(dve.tensor_scalar(hrow[:, :], colf[0:64, :], float(NBR), None, ALU.mult))
            ch.link(dve.tensor_scalar(prow[:, :], colf[:, :], 2.0, 1.0, ALU.mult, ALU.add))
            ch.link(dve.tensor_scalar(prow[64:P, :], prow[64:P, :], -2.0 * SEL, None, ALU.add))
            dve.wait_ge(s_imp, 2)
            dve.tensor_scalar(bidx[:, :], k.bank[5][0:64, 0:TOPN], hrow[:, :], None, ALU.add).then_inc(s_bidx, 1)
            dve.wait_ge(s_imp, 3)
            for r in range(2):
                half = slice(64 * r, 64 * r + 64)
                dve.tensor_scalar(gidx[half, :, :], k.bank[6][half, 0:BG * TOPN].rearrange("p (n m r) -> p n m r", m=8, r=2)[:, :, :, r],
                                  prow[half, :], None, ALU.add).then_inc(s_idx, 1)
            dve.wait_ge(s_sc, 1 + B)
            ch.link(dve.tensor_tensor_reduce(S[:, 512:1024], k.bank[1][0:64, :], k.bias_win[:, :], 1.0, NEG, ALU.add, ALU.max, mx[:, 1:2]))
            ch.link(dve.tensor_scalar(nm[:, 1:2], mx[:, 1:2], FLOOR, -1.0, ALU.max, ALU.mult))
            for bg in range(BG):
                g = bg % 2
                half = slice(HD * g, HD * g + HD)
                for a in range(2):
                    dve.wait_ge(s_sT, 2 * bg + a + 1)
                    if a == 0 and bg >= 2:
                        dve.wait_ge(s_ssc, bg - 1)
                    dve.tensor_copy(sT[half, bg % 2, 512 * a:512 * a + 512], k.bank[2 + a][half, :]).then_inc(s_sTs, 1)
            dve.wait_ge(s_ssc, BG)
            dve.wait_ge(s_bg, 16 * TOPN)
            for a in range(2):
                ch.link(dve.tensor_tensor_reduce(S[:, 1024 + 512 * a:1536 + 512 * a], k.bank[5 + a][0:64, :],
                                                 bsel[:, 512 * a:512 * a + 512], 1.0, NEG, ALU.add, ALU.max, mx[:, 2 + a:3 + a]))
            ch.link(dve.tensor_tensor(mx[:, 2:3], mx[:, 2:3], mx[:, 3:4], ALU.max))
            ch.link(dve.tensor_scalar(nm[:, 2:3], mx[:, 2:3], FLOOR, -1.0, ALU.max, ALU.mult))
            dve.wait_ge(s_exp, 3)
            dve.wait_ge(s_sig, 1)
            ch.link(dve.tensor_scalar(ls[:, 1:3], ls[:, 1:3], 1e-30, None, ALU.max))
            ch.link(dve.reciprocal(ls[:, 1:3], ls[:, 1:3]))
            ch.link(dve.memset(ls[:, 0:1], 1.0))
            ch.link(dve.tensor_tensor(mx[:, 0:1], gt[:, 0:1], ls[:, 0:1], ALU.mult))
            ch.link(dve.tensor_tensor(mx[:, 1:2], gt[:, 2:3], ls[:, 1:2], ALU.mult))
            ch.link(dve.tensor_tensor(mx[:, 2:3], gt[:, 1:2], ls[:, 2:3], ALU.mult))
            dve.wait_ge(s_imp, 3)
            ch.link(dve.tensor_scalar(S[:, 0:512], S[:, 0:512], mx[:, 0:1], None, ALU.mult))
            ch.link(dve.tensor_scalar(S[:, 512:1024], S[:, 512:1024], mx[:, 1:2], None, ALU.mult))
            ch.link(dve.tensor_scalar(S[:, 1024:2048], S[:, 1024:2048], mx[:, 2:3], None, ALU.mult))
            for a in range(2):
                dve.wait_ge(s_pT, a + 1)
                dve.tensor_copy(pT[:, 8 * a:8 * a + 8, :], k.bank[2 + a][:, :].rearrange("p (t r) -> p t r", t=8)).then_inc(s_pTs, 1)
            dve.wait_ge(s_o, 1)
            dve.tensor_copy(k.oaT[:, :, T:TT], k.bank[0][:, 0:32].rearrange("p (b j) -> p j b", j=4)).then_inc(s_od, 1)

        @block.scalar
        def _(act):
            act.wait_ge(s_gt, 16 * B)
            act.activation(gt[:, :], gt[:, :], ACT.Sigmoid).then_inc(s_sig, 1)
            act.wait_ge(s_ch, 2)
            act.activation(S[:, 0:512], S[:, 0:512], ACT.Exp, bias=nm[:, 0:1], accum_out=ls[:, 0:1]).then_inc(s_exp, 1)
            act.wait_ge(s_ch, 26)
            act.activation(S[:, 512:1024], S[:, 512:1024], ACT.Exp, bias=nm[:, 1:2], accum_out=ls[:, 1:2]).then_inc(s_exp, 1)
            for bg in range(BG):
                g = bg % 2
                act.wait_ge(s_new[bg % 2], 16 * (bg // 2 + 1))
                act.activation(vsel[:, bg], kvs[:, bg % 2, :, P + HD * g:P + HD * g + HD], ACT.Copy).then_inc(s_vs, 1)
            act.wait_ge(s_ch, 30)
            act.activation(S[:, 1024:2048], S[:, 1024:2048], ACT.Exp, bias=nm[:, 2:3], accum_out=ls[:, 2:3]).then_inc(s_exp, 1)

        @block.tensor
        def _(pe):
            pe.wait_ge(s_qp, 2)
            pe.wait_ge(s_kcv, 32)
            for b in range(B):
                mm = pe.matmul(k.bank[0][0:64, :], qp[:, 64 * b:64 * b + 64], kcT[:, b, :], start=(b == 0), stop=(b == B - 1))
            mm.then_inc(s_sc, 1)
            pe.wait_ge(s_win, 16 * B)

            def win_turn(b):
                if b >= 2:
                    pe.wait_ge(s_kTs, b - 1)
                for c in range(4):
                    mm = pe.transpose(k.bank[2 + b % 2][:, P * c:P * c + P], win[:, b, c, 0:P], k.ident[:, :])
                mm.then_inc(s_kT, 1)

            win_turn(0)
            for b in range(B):
                if b + 1 < B:
                    win_turn(b + 1)
                pe.wait_ge(s_kTs, b + 1)
                pe.matmul(k.bank[1][0:64, :], qp[:, 64 * b:64 * b + 64], wT[:, b % 2, :], start=(b == 0), stop=(b == B - 1)).then_inc(s_sc, 1)
            pe.wait_ge(s_const, 8)
            pe.wait_ge(s_ch, 5)
            pe.matmul(k.bank[4][0:BG, :], gsel[:, :], S[:, 0:512], start=True, stop=True).then_inc(s_imp, 1)
            pe.wait_ge(s_ch, 20)
            pe.matmul(k.bank[5][0:64, 0:TOPN], gselT[:, :], ixf[:, :], start=True, stop=True).then_inc(s_imp, 1)
            pe.matmul(k.bank[6][:, 0:BG * TOPN], k.ones[0:BG, :], tbd[:, :, :].rearrange("p n m -> p (n m)"), start=True, stop=True).then_inc(s_imp, 1)
            pe.wait_ge(s_idx, 2)
            pe.wait_ge(s_bidx, 1)

            def sel_turn(bg):
                pe.wait_ge(s_new[bg % 2], 16 * (bg // 2 + 1))
                pe.wait_ge(s_sTs, 2 * bg)
                for a in range(2):
                    for q in range(4):
                        mm = pe.transpose(k.bank[2 + a][:, P * q:P * q + P], kvs[:, bg % 2, 4 * a + q, 0:P], k.ident[:, :])
                    mm.then_inc(s_sT, 1)

            def sel_scores(bg):
                b, g = bg // 2, bg % 2
                half = slice(HD * g, HD * g + HD)
                pe.wait_ge(s_sTs, 2 * bg + 2)
                if bg:
                    pe.wait_ge(s_ssc, bg)
                for a in range(2):
                    mm = pe.matmul(k.bank[5 + a][0:64, :], qp[half, 64 * b:64 * b + 64], sT[half, bg % 2, 512 * a:512 * a + 512],
                                   start=(bg == 0), stop=(bg == BG - 1), skip_group_check=True)
                mm.then_inc(s_ssc, 1)

            for bg in range(BG):
                sel_turn(bg)
                if bg:
                    sel_scores(bg - 1)
            sel_scores(BG - 1)
            pe.wait_ge(s_ch, 39)
            for a in range(2):
                for q in range(8):
                    t = 8 * a + q
                    mm = pe.transpose(k.bank[2 + a][:, 64 * q:64 * q + 64], S[:, P * t:P * t + P], k.ident[0:64, 0:64])
                mm.then_inc(s_pT, 1)
            pe.wait_ge(s_pTs, 2)
            pe.wait_ge(s_vs, BG)
            for g in range(G):
                for b in range(B):
                    bg = G * b + g
                    col = slice(8 * b + 4 * g, 8 * b + 4 * g + 4)
                    vals = ([(vc[:, b, t, HD * g:HD * g + HD], t) for t in range(4)]
                            + [(win[:, b, c, P + HD * g:P + HD * g + HD], 4 + c) for c in range(4)]
                            + [(vsel[:, bg, m, :], 8 + m) for m in range(8)])
                    for n, (v, t) in enumerate(vals):
                        mm = pe.matmul(k.bank[0][HD * g:HD * g + HD, 4 * b:4 * b + 4], v, pT[:, t, col], start=(n == 0), stop=(n == 15))
            mm.then_inc(s_o, 1)


def add_gated(k, dve, xT, c, g, bank, gate, tmp, sem_x, sem_t, n_t):
    w = GT if g < NG - 1 else T - GT * (NG - 1)
    cs = c if isinstance(c, slice) else bass.ds(c, 1)
    if w < GT:
        dve.wait_ge(sem_t, n_t)
        dve.tensor_tensor(tmp[:, :], bank[:, w:GT], k.modT[:, bass.ds(gate + c, 1), 1:9].rearrange("p o b -> p (o b)"), ALU.mult).then_inc(sem_t, 1)
        dve.wait_ge(sem_t, n_t + 1)
        dve.tensor_tensor(xT[:, cs, T:TT].rearrange("p o b -> p (o b)"), xT[:, cs, T:TT].rearrange("p o b -> p (o b)"), tmp[:, :], ALU.add).then_inc(sem_t, 1)
    x = xT[:, cs, GT * g:GT * g + w].rearrange("p o t -> p (o t)")
    dve.scalar_tensor_tensor(out=x, in0=bank[:, 0:w], scalar=k.modT[:, bass.ds(gate + c, 1), 0:1].rearrange("p o b -> p (o b)"),
                             in1=x, op0=ALU.mult, op1=ALU.add).then_inc(sem_x, 1)


def merge(k):
    nc = k.nc
    w_v = k.i["w_in"][0].rearrange("(k p) n -> p k n", p=P)
    wa_v = k.i["w_branch_a"][0].rearrange("(g j d) n -> g d j n", g=G, j=4)
    wb_v = k.i["w_branch_b"][0].rearrange("(k p) n -> p k n", p=P)
    wo_v = k.i["w_out"][0].rearrange("(k p) n -> p k n", p=P)
    s_ux, s_wo, s_of, s_osig, s_ob = (k.sem(f"s_g_{x}") for x in ("ux", "wo", "of", "osig", "ob"))
    s_wm, s_wr = [k.sem(f"s_g_wm{j}") for j in range(2)], [k.sem(f"s_g_wr{j}") for j in range(2)]
    s_mf, s_sig, s_t, s_mix, s_rf, s_x, s_xs = (k.sem(f"s_g_{x}") for x in ("mf", "sig", "t", "mix", "rf", "x", "xs"))
    s_xin, s_xst = k.sem("s_g_xin"), k.sem("s_g_xst")
    with ExitStack() as ctx:
        uT = k.sb("guT", [P, DK, TT], ctx=ctx)
        xT = k.sb("gxT", [P, DK, TT], ctx=ctx)
        mixT = k.sb("mixT", [P, DK, TT], ctx=ctx)
        wo = k.sb("gwo", [P, DK, 512], ctx=ctx)
        wg = k.sb("gwg", [P, 2, DK, 2, P], ctx=ctx)
        wb = k.sb("gwb", [P, 2, 2, 4, P], ctx=ctx)
        wr = k.sb("gwr", [P, 2, DK, P], ctx=ctx)
        ob = k.sb("gob", [P, 2, GT], ctx=ctx)
        sig = k.sb("gsig", [P, 2, 2, GT], ctx=ctx)
        tt = k.sb("gtt", [P, 2, 2, GT], ctx=ctx)
        tmp = k.sb("gtmp", [P, B], ctx=ctx)
        block = ctx.enter_context(nc.Block())

        @block.sync
        def _(sp):
            sp.dma_start(uT[:, :, :], k.uT_d).then_inc(s_ux, 16)
            sp.dma_start(wo[:, :, :], w_v[:, :, OFF_OB:OFF_MG]).then_inc(s_wo, 16)

            def load(c, j):
                for br in range(2):
                    sp.dma_start(wg[:, j, :, br, :], w_v[:, :, bass.ds(c * P + (OFF_MG + D * br), P)]).then_inc(s_wm[j], 16)
                for g in range(G):
                    sp.dma_start(wb[HD * g:HD * g + HD, j, 0], wa_v[g, :, :, bass.ds(c * P, P)]).then_inc(s_wm[j], 16)
                sp.dma_start(wb[:, j, 1], wb_v[:, :, bass.ds(c * P, P)]).then_inc(s_wm[j], 16)

            for j in range(2):
                load(j, j)
            sp.dma_start(xT[:, :, :], k.xT_d).then_inc(s_xin, 16)
            for j in range(2):
                sp.dma_start(wr[:, j], wo_v[:, :, P * j:P * j + P]).then_inc(s_wr[j], 16)
            with sp.Fori(1, 4) as i:
                for j in range(2):
                    sp.wait_ge(s_mf, i * 6 + (3 * j + 3 - 6))
                    load(i * 2 + j, j)
            with sp.Fori(1, 4) as i:
                for j in range(2):
                    sp.wait_ge(s_rf, i * 6 + (3 * j + 3 - 6))
                    sp.dma_start(wr[:, j], wo_v[:, :, bass.ds(i * 2 * P + P * j, P)]).then_inc(s_wr[j], 16)
            sp.wait_ge(s_x, 24)
            sp.wait_ge(s_xs, 16)
            sp.dma_start(k.xT_d, xT[:, :, :]).then_inc(s_xst, 16)
            sp.wait_ge(s_xst, 16)

        @block.tensor
        def _(pe):
            pe.wait_ge(s_ux, 16)
            pe.wait_ge(s_wo, 16)
            for f in range(4 * NG):
                c, g = f // NG, f % NG
                if f >= 8:
                    pe.wait_ge(s_osig, f - 7)
                for kk in range(DK):
                    mm = pe.matmul(k.bank[f % 8][:, 0:GT], wo[:, kk, P * c:P * c + P], uT[:, kk, GT * g:GT * g + GT],
                                   start=(kk == 0), stop=(kk == DK - 1))
                mm.then_inc(s_of, 1)
            pe.wait_ge(s_osig, 4 * NG)
            pe.wait_ge(s_ob, 4 * NG)
            with pe.Fori(0, 4) as i:
                for j in range(2):
                    pe.wait_ge(s_wm[j], i * 80 + 80)
                    for g in range(NG):
                        u = NG * j + g
                        b = 4 * (u % 2)
                        pe.wait_ge(s_mix, i * 6 + (u + 1))
                        t = slice(GT * g, GT * g + GT)
                        for br in range(2):
                            for kk in range(DK):
                                pe.matmul(k.bank[b + br][:, 0:GT], wg[:, j, kk, br, :], uT[:, kk, t], start=(kk == 0), stop=(kk == DK - 1))
                        for br, src in ((0, k.oaT), (1, k.hbT)):
                            for kk in range(4):
                                mm = pe.matmul(k.bank[b + 2 + br][:, 0:GT], wb[:, j, br, kk, :], src[:, kk, t], start=(kk == 0), stop=(kk == 3))
                        mm.then_inc(s_mf, 1)
            pe.wait_ge(s_mix, 26)
            with pe.Fori(0, 4) as i:
                for j in range(2):
                    pe.wait_ge(s_wr[j], i * 16 + 16)
                    for g in range(NG):
                        u = NG * j + g
                        pe.wait_ge(s_x, i * 6)
                        for kk in range(DK):
                            mm = pe.matmul(k.bank[u][:, 0:GT], wr[:, j, kk, :], mixT[:, kk, GT * g:GT * g + GT], start=(kk == 0), stop=(kk == DK - 1))
                        mm.then_inc(s_rf, 1)

        @block.scalar
        def _(act):
            for f in range(4 * NG):
                act.wait_ge(s_of, f + 1)
                if f >= 2:
                    act.wait_ge(s_ob, f - 1)
                act.activation(ob[:, f % 2, :], k.bank[f % 8][:, 0:GT], ACT.Sigmoid).then_inc(s_osig, 1)
            with act.Fori(0, 4) as i:
                for u in range(6):
                    act.wait_ge(s_mf, i * 6 + (u + 1))
                    act.wait_ge(s_mix, i * 6 + (u + 1))
                    for br in range(2):
                        act.activation(sig[:, u % 2, br, :], k.bank[4 * (u % 2) + br][:, 0:GT], ACT.Sigmoid).then_inc(s_sig, 1)

        @block.vector
        def _(dve):
            for f in range(4 * NG):
                c, g = f // NG, f % NG
                dve.wait_ge(s_osig, f + 1)
                h = k.hbT[:, c, GT * g:GT * g + GT]
                dve.tensor_tensor(h, h, ob[:, f % 2, :], ALU.mult).then_inc(s_ob, 1)
            dve.memset(tmp[:, :], 0.0).then_inc(s_mix, 2)
            with dve.Fori(0, 4) as i:
                for u in range(6):
                    j, g = u // NG, u % NG
                    b = 4 * (u % 2)
                    dve.wait_ge(s_sig, i * 12 + (2 * u + 2))
                    dve.wait_ge(s_mix, i * 6 + (u + 1))
                    for br in range(2):
                        dve.tensor_tensor(tt[:, u % 2, br, :], k.bank[b + 2 + br][:, 0:GT], sig[:, u % 2, br, :], ALU.mult).then_inc(s_t, 1)
                    dve.wait_ge(s_t, i * 12 + (2 * u + 2))
                    dve.tensor_tensor(mixT[:, bass.ds(i * 2 + j, 1), GT * g:GT * g + GT].rearrange("p o t -> p (o t)"), tt[:, u % 2, 0, :], tt[:, u % 2, 1, :],
                                      ALU.add).then_inc(s_mix, 1)
            dve.wait_ge(s_xin, 16)
            with dve.Fori(0, 4) as i:
                for u in range(6):
                    j, g = u // NG, u % NG
                    dve.wait_ge(s_rf, i * 6 + (u + 1))
                    add_gated(k, dve, xT, i * 2 + j, g, k.bank[u], 16, tmp, s_x, s_xs, i * 4 + 2 * j)


def ffn(k, xT, uT):
    nc = k.nc
    FK = FF // P
    wi_v = k.i["w_ffn_in"][0].rearrange("(k p) n -> p k n", p=P)
    wo_v = k.i["w_ffn_out"][0].rearrange("(k p) n -> p k n", p=P)
    s_wi, s_wo = [k.sem(f"s_f_wi{j}") for j in range(2)], [k.sem(f"s_f_wo{j}") for j in range(2)]
    s_hf, s_silu, s_h, s_yf, s_x, s_xs = (k.sem(f"s_f_{x}") for x in ("hf", "silu", "h", "yf", "x", "xs"))
    with ExitStack() as ctx:
        hT = k.sb("hT", [P, FK, TT], ctx=ctx)
        wi = k.sb("fwi", [P, 2, DK, 2, P], ctx=ctx)
        wo = k.sb("fwo", [P, 2, FK // 2, P], ctx=ctx)
        sl = k.sb("fsl", [P, 2, GT], ctx=ctx)
        tmp = k.sb("ftmp", [P, B], ctx=ctx)
        block = ctx.enter_context(nc.Block())
        HK = FK // 2

        @block.sync
        def _(sp):
            def load(m, j):
                for half in range(2):
                    sp.dma_start(wi[:, j, :, half, :], wi_v[:, :, bass.ds(m * P + FF * half, P)]).then_inc(s_wi[j], 16)

            load(0, 0)
            load(1, 1)
            for j in range(2):
                sp.dma_start(wo[:, j], wo_v[:, HK * j:HK * j + HK, 0:P]).then_inc(s_wo[j], 16)
            with sp.Fori(1, FK // 2) as i:
                for j in range(2):
                    sp.wait_ge(s_hf, i * 6 + (3 * j + 3 - 6))
                    load(i * 2 + j, j)
            with sp.Fori(1, DK) as c:
                for j in range(2):
                    sp.wait_ge(s_yf, c * 2 + (j + 1 - 2))
                    sp.dma_start(wo[:, j], wo_v[:, HK * j:HK * j + HK, bass.ds(c * P, P)]).then_inc(s_wo[j], 16)

        @block.tensor
        def _(pe):
            with pe.Fori(0, FK // 2) as i:
                for u in range(6):
                    j, g = u // NG, u % NG
                    if g == 0:
                        pe.wait_ge(s_wi[j], i * 32 + 32)
                    pe.wait_ge(s_h, i * 6 + (u + 1))
                    for half in range(2):
                        for kk in range(DK):
                            mm = pe.matmul(k.bank[2 * (u % 2) + half][:, 0:GT], wi[:, j, kk, half, :], uT[:, kk, GT * g:GT * g + GT],
                                           start=(kk == 0), stop=(kk == DK - 1))
                    mm.then_inc(s_hf, 1)
            pe.wait_ge(s_h, 3 * FK + 2)
            with pe.Fori(0, DK) as c:
                for j in range(2):
                    pe.wait_ge(s_wo[j], c * 16 + 16)
                    for g in range(NG):
                        if j == 0:
                            pe.wait_ge(s_x, c * NG)
                        for kk in range(HK):
                            mm = pe.matmul(k.bank[4 + g][:, 0:GT], wo[:, j, kk, :], hT[:, HK * j + kk, GT * g:GT * g + GT],
                                           start=(j == 0 and kk == 0), stop=(j == 1 and kk == HK - 1))
                    mm.then_inc(s_yf, 1)

        @block.scalar
        def _(act):
            with act.Fori(0, FK // 2) as i:
                for u in range(6):
                    act.wait_ge(s_hf, i * 6 + (u + 1))
                    act.wait_ge(s_h, i * 6 + (u + 1))
                    act.activation(sl[:, u % 2, :], k.bank[2 * (u % 2)][:, 0:GT], ACT.Silu).then_inc(s_silu, 1)

        @block.vector
        def _(dve):
            dve.memset(tmp[:, :], 0.0).then_inc(s_h, 2)
            with dve.Fori(0, FK // 2) as i:
                for u in range(6):
                    j, g = u // NG, u % NG
                    dve.wait_ge(s_silu, i * 6 + (u + 1))
                    dve.tensor_tensor(hT[:, bass.ds(i * 2 + j, 1), GT * g:GT * g + GT].rearrange("p o t -> p (o t)"), k.bank[2 * (u % 2) + 1][:, 0:GT],
                                      sl[:, u % 2, :], ALU.mult).then_inc(s_h, 1)
            with dve.Fori(0, DK) as c:
                for g in range(NG):
                    dve.wait_ge(s_yf, c * 2 + 2)
                    add_gated(k, dve, xT, c, g, k.bank[4 + g], 40, tmp, s_x, s_xs, c * 2)


def store_y(k, yT):
    nc = k.nc
    s_t, s_c, s_o = k.sem("s_y_t"), k.sem("s_y_c"), [k.sem(f"s_y_o{j}") for j in range(2)]
    with ExitStack() as ctx:
        yr = k.sb("yr", [P, 2, D], ctx=ctx)
        block = ctx.enter_context(nc.Block())

        @block.tensor
        def _(pe):
            for f in range(2 * (NTI + 1)):
                ti, half = f // 2, f % 2
                m = P if ti < NTI else B
                if f >= 4:
                    pe.wait_ge(s_c, f - 3)
                for q in range(4):
                    mm = pe.transpose(k.bank[f % 4][0:m, P * q:P * q + P], yT[:, 4 * half + q, P * ti:P * ti + m], k.ident[:, :])
                mm.then_inc(s_t, 1)

        @block.vector
        def _(dve):
            for f in range(2 * (NTI + 1)):
                ti, half = f // 2, f % 2
                m = P if ti < NTI else B
                dve.wait_ge(s_t, f + 1)
                if ti >= 2 and half == 0:
                    dve.wait_ge(s_o[ti % 2], 16 * (ti // 2))
                dve.tensor_copy(yr[0:m, ti % 2, 512 * half:512 * half + 512], k.bank[f % 4][0:m, :]).then_inc(s_c, 1)

        @block.sync
        def _(sp):
            for ti in range(NTI + 1):
                sp.wait_ge(s_c, 2 * ti + 2)
                if ti < NTI:
                    sp.dma_start(k.o["y_prompt"][0, P * ti:P * ti + P, :], yr[:, ti % 2, :]).then_inc(s_o[ti % 2], 16)
                else:
                    sp.dma_start(k.o["y_sample"].rearrange("b o d -> (b o) d"), yr[0:B, ti % 2, :]).then_inc(s_o[ti % 2], 16)
            sp.wait_ge(s_o[0], 16 * 5)
            sp.wait_ge(s_o[1], 16 * 4)


def reload_x(k, xT):
    nc = k.nc
    s_in = k.sem("s_rx")
    with nc.Block() as block:
        @block.sync
        def _(sp):
            sp.dma_start(xT[:, :, :], k.xT_d).then_inc(s_in, 16)
            sp.wait_ge(s_in, 16)


def build(nc, ins, outs):
    k = Core(nc, ins, outs)
    with k.ctx:
        shared_buffers(k)
        k.xT_d = k.dram("xT_d", (P, DK, TT))
        k.uT_d = k.dram("uT_d", (P, DK, TT))
        conditioning(k)
        k.stage_done()
        bias_tables(k)
        k.stage_done()
        cache_compress(k)
        k.stage_done()
        with ExitStack() as actx:
            k.hbT = k.sb("hbT", [P, MH, TT], ctx=actx)
            k.small = k.sb("small", [P, NTI, 32], ctx=actx)
            k.small_s = k.sb("small_s", [B, 32], ctx=actx)
            k.qTs = k.sb("qTs", [P, 4, B], ctx=actx)
            with ExitStack() as ctx:
                k.uT = k.sb("uT", [P, DK, TT], ctx=ctx)
                with ExitStack() as xctx:
                    xT = k.sb("xT", [P, DK, TT], ctx=xctx)
                    load_x(k, xT)
                    k.stage_done()
                    norm(k, "mix", xT, 0, k.uT, keep=k.xT_d, keep_dst=k.uT_d)
                    k.stage_done()
                k.qbT = k.sb("qbT", [P, MH, TT], ctx=ctx)
                k.kbT = k.sb("kbT", [P, MH, TT], ctx=ctx)
                k.kb = k.sb("kb", [P, NTI, 512], ctx=ctx)
                k.kb_s = k.sb("kb_s", [B, 512], ctx=ctx)
                k.vb = k.sb("vb", [P, NTI, MH, MD + 1], ctx=ctx)
                k.vb_s = k.sb("vb_s", [B, MH, MD + 1], ctx=ctx)
                mlstm_project(k)
                k.stage_done()
                mlstm_scan(k)
                k.stage_done()
                mlstm_decode(k)
                k.stage_done()
            k.oaT = k.sb("oaT", [P, 4, TT], ctx=actx)
            with ExitStack() as ctx:
                k.qT = k.sb("qT", [P, 4, TT], ctx=ctx)
                k.kv = k.sb("kv", [P, NTI, 768], ctx=ctx)
                k.ksT = k.sb("ksT", [P, T], ctx=ctx)
                k.kwT = k.sb("kwT", [P, T], ctx=ctx)
                k.kcpT = k.sb("kcpT", [P, T // STRIDE], ctx=ctx)
                k.vcp = k.sb("vcp", [T // STRIDE, P], ctx=ctx)
                nsa_project(k)
                k.stage_done()
                prompt_compress(k)
                k.stage_done()
                prompt_attention(k)
                k.stage_done()
            decode_attention(k)
            k.stage_done()
            merge(k)
            k.stage_done()
        with ExitStack() as ctx:
            xT = k.sb("xT2", [P, DK, TT], ctx=ctx)
            uT = k.sb("u2T", [P, DK, TT], ctx=ctx)
            reload_x(k, xT)
            k.stage_done()
            norm(k, "ffn", xT, 1, uT)
            k.stage_done()
            ffn(k, xT, uT)
            k.stage_done()
            norm(k, "final", xT, 2, uT)
            k.stage_done()
            store_y(k, uT)
            k.stage_done()


_INS = ["x_prompt", "x_sample", "c_prompt", "c_sample", "cache_nsa_kv", "cache_nsa_win", "state_mlstm_C",
        "state_mlstm_n", "state_mlstm_m", "page_table", "rel_bias", "w_ada", "b_ada", "norm_mix_g",
        "norm_ffn_g", "w_in", "mlstm_gate_b", "cmp_pe", "cmp_w1", "cmp_w2", "mlstm_norm_g", "w_branch_a",
        "w_branch_b", "w_out", "w_ffn_in", "w_ffn_out", "w_ada_final", "b_ada_final", "norm_final_g"]
_OUTS = [("y_prompt", (1, T, D)), ("y_sample", (B, 1, D)),
         ("kv_prompt", (1, 1, T, 4, G, HD)), ("kv_sample", (1, B, 1, 4, G, HD)),
         ("win_prompt", (1, 1, WIN, 2, G, HD)), ("win_sample", (1, B, WIN, 2, G, HD)),
         ("C_prompt", (1, 1, MH, MD, MD)), ("n_prompt", (1, 1, MH, MD)), ("m_prompt", (1, 1, MH)),
         ("C_sample", (1, B, MH, MD, MD)), ("n_sample", (1, B, MH, MD)), ("m_sample", (1, B, MH))]


def kernel(**inputs):
    import numpy as _np
    import concourse.bacc as _bacc
    from concourse import mybir as _mybir
    from concourse.bass_utils import run_bass_kernel_spmd as _run

    nc = _bacc.Bacc("TRN2", target_bir_lowering=False, num_devices=1)
    arrays, ins, outs = {}, {}, {}
    for name in _INS:
        a = _np.ascontiguousarray(inputs[name])
        arrays[f"in_{name}"] = a
        ins[name] = nc.dram_tensor(f"in_{name}", a.shape, _mybir.dt.from_np(a.dtype), kind="ExternalInput").ap()
    for name, shape in _OUTS:
        outs[name] = nc.dram_tensor(f"out_{name}", shape, F32, kind="ExternalOutput").ap()
    build(nc, ins, outs)
    r = _run(nc, [arrays], core_ids=[0])
    return tuple(r.results[0][f"out_{name}"] for name, _ in _OUTS)
```

```python
from contextlib import ExitStack

import numpy as np
import concourse.bass as bass
from concourse import mybir

F32 = mybir.dt.float32
F32R = mybir.dt.float32r
I32 = mybir.dt.int32
U32 = mybir.dt.uint32
ALU = mybir.AluOpType
ACT = mybir.ActivationFunctionType
AX = mybir.AxisListType

P = 128
D = 1024
T = 1024
B = 8
TT = T + B
DK = D // P
NTI = T // P
GT = TT // 3
NG = 3
H = 8
G = 2
HD = 64
PAST = 8192
PAGE = 128
NPAGES = PAST // PAGE
POOL = 640
STRIDE = 16
NPIECE = PAST // STRIDE
NCMP = NPIECE - 1
NCP = T // STRIDE - 1
CH = 256
SEL = 64
TOPN = 16
WIN = 512
MH = 4
MD = 128
FF = 2816
NBUCKET = 32
OFF_QA, OFF_KVA = 0, 512
OFF_GA = OFF_KVA + 768
OFF_QB = OFF_GA + 24
OFF_KB = OFF_QB + 512
OFF_VB = OFF_KB + 512
OFF_IFB = OFF_VB + 512
OFF_OB = OFF_IFB + 8
OFF_MG = OFF_OB + 512
NEG = -1e30
FLOOR = -1e20
EPS = 1e-6
BUCKET_START = [*range(16), 16, 21, 27, 35, 46, 59, 77, 99, 128, 166, 216, 280, 363, 470, 609, 790]
NREV = 8320
NFWD = 1152

VEC = {"b_ada": (0, 48), "b_ada_final": (48, 16), "norm_mix_g": (64, 8), "norm_ffn_g": (72, 8),
       "norm_final_g": (80, 8), "mlstm_norm_g": (88, 4)}
NVEC = 92


class Chain:

    def __init__(self, eng, sem, base=0):
        self.eng, self.sem, self.base, self.n, self.per = eng, sem, base, 0, None

    def start(self, i, per):
        self.i, self.per, self.n = i, per, 0

    def step(self, ins):
        ins.then_inc(self.sem, 1)
        self.n += 1

    def link(self, ins):
        self.step(ins)
        if self.per is None:
            self.eng.wait_ge(self.sem, self.base + self.n)
        else:
            self.eng.wait_ge(self.sem, self.i * self.per + self.base + self.n)

    def done(self):
        assert self.per == self.n, (self.per, self.n)


class Core:

    def __init__(self, nc, ins, outs):
        self.nc, self.i, self.o = nc, ins, outs
        self.ctx = ExitStack()
        self.stage_sems = []

    def sem(self, name, start=0):
        s = self.nc.alloc_semaphore(name=name)
        if start:
            self.nc.gpsimd.sem_inc(s, start)
        self.stage_sems.append(s)
        return s

    def lasting_sem(self, name):
        return self.nc.alloc_semaphore(name=name)

    def stage_done(self):
        self.nc.clear_and_free_semaphores(self.stage_sems)
        self.nc.all_engine_barrier()
        self.stage_sems = []

    def sb(self, name, shape, dt=F32, ctx=None):
        return (ctx or self.ctx).enter_context(self.nc.sbuf_tensor(name, shape, dt))

    def ps(self, name, shape):
        return self.ctx.enter_context(self.nc.psum_tensor(name, shape, F32))

    def dram(self, name, shape, dt=F32):
        return self.nc.dram_tensor(name, shape, dt).ap()


def shared_buffers(k):
    k.bank = [k.ps(f"bank{n}", [P, 512]) for n in range(8)]
    k.ident = k.sb("ident", [P, P])
    k.ones = k.sb("ones", [P, P])
    k.vecT = k.sb("vecT", [P, NVEC])
    k.modT = k.sb("modT", [P, 64, 9])
    k.modA = k.sb("modA", [P, 3, DK, 9])
    k.bias_cmp = k.sb("bias_cmp", [64, 512])
    k.bias_win = k.sb("bias_win", [64, 512])
    k.peb = k.sb("peb", [P, 2, 2])
    k.biasfwd_d = k.dram("biasfwd_d", (H, NFWD))
    k.biasrev_d = k.dram("biasrev_d", (B * H, NREV))
    k.smalltok_d = k.dram("smalltok_d", (B, 32))


def load_page(k, eng, i, page, kv):
    nt, q = page // 16, page % 16
    pages = k.i["cache_nsa_kv"][0].rearrange("q (n s) v g d -> q n s (v g d)", s=STRIDE)
    at = eng.value_load(k.pt[0:1, bass.ds(i * NPAGES + page, 1)], min_val=0, max_val=POOL - 1)
    eng.dma_start(k.raw[8 * q:8 * q + 8, kv, nt], pages[bass.ds(at, 1), :, :, P * kv:P * kv + P]
                  .rearrange("o n s c -> (o n) s c")).then_inc(k.s_page[kv][nt], 16)


def setup(k):
    nc = k.nc
    s_const, s_rows, s_vec, s_cT, s_cTs = (k.sem(x) for x in ("s_const", "s_rows", "s_vec", "s_cT", "s_cTs"))
    s_tab, s_rev, s_neg, s_fwd, s_store = k.sem("s_tab"), k.sem("s_rev"), k.sem("s_neg"), k.sem("s_fwd"), k.sem("s_bstore")
    with ExitStack() as ctx:
        crow = k.sb("crow", [9, D], ctx=ctx)
        vrow = k.sb("vrow", [NVEC, P], ctx=ctx)
        tab = k.sb("tab", [64, NBUCKET], ctx=ctx)
        rev = k.sb("rev", [64, NREV], ctx=ctx)
        fwd = k.sb("fwd", [H, NFWD], ctx=ctx)
        block = ctx.enter_context(nc.Block())
        ends = BUCKET_START[1:] + [PAST + 1]

        @block.sync
        def _(sp):
            sp.dma_start(k.pt[:, :], k.i["page_table"].rearrange("b n -> (b n)").rearrange("(o n) -> o n", o=1)).then_inc(k.s_pt, 16)
            sp.dma_start(crow[0:1, :], k.i["c_prompt"]).then_inc(s_rows, 16)
            sp.dma_start(crow[1:9, :], k.i["c_sample"]).then_inc(s_rows, 16)
            for name, (r, n) in VEC.items():
                a = k.i[name]
                a = a[0] if len(a.shape) == 2 else a
                sp.dma_start(vrow[r:r + n, :], a.rearrange("(r p) -> r p", p=P)).then_inc(s_vec, 16)
            sp.wait_ge(k.s_pt, 16)
            load_pages(k, sp, 0, 0, 0)

        @block.gpsimd
        def _(pool):
            pool.memset(k.ident[:, :], 0.0).then_inc(s_const, 1)
            pool.memset(k.ones[:, :], 1.0).then_inc(s_const, 1)
            pool.wait_ge(s_const, 2)
            pool.affine_select(out=k.ident[:, :], in_=k.ident[:, :], compare_op=ALU.not_equal, fill=1.0,
                               base=0, pattern=[[-1, P]], channel_multiplier=1).then_inc(s_const, 1)
            pool.wait_ge(k.s_pt, 16)
            load_pages(k, pool, 0, 0, 1)

        @block.tensor
        def _(pe):
            pe.wait_ge(s_const, 3)
            pe.wait_ge(s_rows, 32)
            for c in range(DK):
                mm = pe.transpose(k.bank[7][:, 9 * c:9 * c + 9], crow[:, P * c:P * c + P], k.ident[0:9, 0:9])
            mm.then_inc(s_cT, 1)
            pe.wait_ge(s_vec, 16 * len(VEC))
            pe.transpose(k.bank[6][:, 0:NVEC], vrow[:, :], k.ident[0:NVEC, 0:NVEC]).then_inc(s_cT, 1)

        @block.scalar
        def _(act):
            with nc.allow_non_contiguous_dma(reason="a 32 x 8 table, transposed"):
                for b in range(B):
                    act.dma_start(tab[8 * b:8 * b + 8, :], k.i["rel_bias"].rearrange("n h -> h n")).then_inc(s_tab, 16)
            load_cmp_weights(k, act, k.cw1, k.cw2, k.perow, (k.s_w1, k.s_w2, k.s_pe))
            for j in range(4):
                load_ada(k, act, 0, j)
            act.wait_ge(s_rev, NBUCKET)
            act.wait_ge(s_neg, 1)
            act.dma_start(k.biasrev_d, rev[:, :]).then_inc(s_store, 16)
            act.wait_ge(s_fwd, 3)
            act.dma_start(k.biasfwd_d, fwd[:, :]).then_inc(s_store, 16)
            act.wait_ge(s_store, 32)

        @block.vector
        def _(dve):
            dve.memset(rev[:, PAST + 1:NREV], NEG).then_inc(s_neg, 1)
            dve.wait_ge(s_cT, 1)
            dve.tensor_copy(k.cT[:, :, :], k.bank[7][:, 0:72].rearrange("p (c r) -> p c r", r=9)).then_inc(s_cTs, 1)
            dve.wait_ge(s_cT, 2)
            dve.tensor_copy(k.vecT[:, :], k.bank[6][:, 0:NVEC]).then_inc(s_cTs, 1)
            dve.wait_ge(s_tab, 16 * B)
            for n, (lo, hi) in enumerate(zip(BUCKET_START, ends)):
                dve.tensor_copy(rev[:, PAST - hi + 1:PAST - lo + 1],
                                tab[:, n:n + 1].to_broadcast([64, hi - lo])).then_inc(s_rev, 1)
            dve.wait_ge(s_rev, NBUCKET)
            dve.wait_ge(s_neg, 1)
            dve.tensor_copy(fwd[:, :], rev[0:H, PAST + 127:PAST + 127 - NFWD:-1]).then_inc(s_fwd, 1)
            dve.tensor_copy(k.bias_cmp[:, :], rev[:, 31:31 + 512 * STRIDE:STRIDE]).then_inc(s_fwd, 1)
            dve.tensor_copy(k.bias_win[:, :], rev[:, PAST - 511:PAST + 1]).then_inc(s_fwd, 1)


def load_pages(k, eng, i, kv, half):
    k.nc.disable_value_cache = True
    for page in range(NPAGES // 2 * half, NPAGES // 2 * (half + 1)):
        load_page(k, eng, i, page, kv)
    k.nc.disable_value_cache = False


def load_ada(k, act, m, j, final=False):
    w = k.i["w_ada_final"] if final else k.i["w_ada"][0]
    at = m * (4 * P) + (P * j - (48 * P if final else 0))
    act.dma_start(k.wada[:, j], w.rearrange("(k p) n -> p k n", p=P)[:, :, bass.ds(at, P)]).then_inc(k.s_ada[j], 16)


def load_cmp_weights(k, sp, w1, w2, perow, sems):
    for kv in range(2):
        sp.dma_start(w1[:, kv].rearrange("p r s f -> p (r s) f"),
                     k.i["cmp_w1"][0, kv].rearrange("(j s) d f -> (s d) j f", s=2)).then_inc(sems[0], 16)
        sp.dma_start(w2[:, kv], k.i["cmp_w2"][0, kv].rearrange("(c f) d -> f c d", f=P)).then_inc(sems[1], 16)
    sp.dma_start(perow[:, :], k.i["cmp_pe"][0].rearrange("v (j s) d -> (v j) (s d)", s=2)).then_inc(sems[2], 16)


def cache_compress(k):
    nc = k.nc
    k.kcT_d = k.dram("kcT_d", (P, B, NPIECE))
    k.vc_d = k.dram("vc_d", (P, B, 4, P))
    s_page, s_w1, s_w2, s_pe = k.s_page, k.s_w1, k.s_w2, k.s_pe
    raw, w1, w2, perow = k.raw, k.cw1, k.cw2, k.perow
    s_peT, s_peTs, s_peb = k.sem("s_peT"), k.sem("s_peTs"), k.sem("s_peb")
    s_kst = [k.sem(f"s_kst{kv}", start=1) for kv in range(2)]
    s_tr, s_xtv, s_xta = k.sem("s_tr"), k.sem("s_xtv"), k.sem("s_xta")
    s_hid, s_gelu, s_kc, s_kcs = (k.sem(x, start=1) for x in ("s_hid", "s_gelu", "s_kc", "s_kcs"))
    s_zero, s_mod, s_modA = k.sem("s_hzero"), k.sem("s_mod"), k.sem("s_modA")
    s_modT = k.sem("s_modT", start=1)
    with ExitStack() as ctx:
        kc_vc = k.sb("kc_vc", [P, 2, NPIECE], ctx=ctx)
        peT = k.sb("peT", [P, 32], ctx=ctx)
        xt = k.sb("xt", [P, 2, G, 8, NPIECE], ctx=ctx)
        hid = k.sb("hid", [P, 2, 2, NPIECE], ctx=ctx)
        block = ctx.enter_context(nc.Block())

        def pages(eng, half):
            load_pages(k, eng, 0, 1, half)
            with eng.Fori(1, B) as i:
                for kv in range(2):
                    eng.wait_ge(s_tr, i * 32 + (16 * kv + 16 - 32))
                    load_pages(k, eng, i, kv, half)

        @block.sync
        def _(sp):
            pages(sp, 0)
            for kv in range(2):
                sp.wait_ge(s_kst[kv], 16 * B + 1)

        @block.gpsimd
        def _(pool):
            pages(pool, 1)

        @block.tensor
        def _(pe):
            pe.wait_ge(s_pe, 16)
            pe.transpose(k.bank[0][:, 0:32], perow[:, :], k.ident[0:32, 0:32]).then_inc(s_peT, 1)
            pe.wait_ge(s_peTs, 1)
            pe.wait_ge(s_w1, 32)
            pe.wait_ge(s_w2, 32)
            for kv in range(2):
                for c in range(2):
                    for j in range(16):
                        mm = pe.matmul(k.bank[1][:, 2 * kv + c:2 * kv + c + 1], w1[:, kv, j // 8, j % 8, P * c:P * c + P],
                                       peT[:, 16 * kv + j:16 * kv + j + 1], start=(j == 0), stop=(j == 15))
            mm.then_inc(s_peT, 1)
            pe.wait_ge(s_peb, 1)

            def turn(i, kv, tokens, start=False):
                for s in tokens:
                    if s == 0:
                        for nt in range(4):
                            pe.wait_ge(s_page[kv][nt], i * 256 + 256)
                    if not (start and s < 4):
                        pe.wait_ge(s_xta if s % 2 else s_xtv, i * 16 + (8 * kv + s // 2 - 1))
                    for nt in range(4):
                        mm = pe.transpose(k.bank[s % 4][:, P * nt:P * nt + P], raw[:, kv, nt, s, :], k.ident[:, :])
                    mm.then_inc(s_tr, 1)

            def first(i, kv, n):
                g, c = n // 2, n % 2
                pe.wait_ge(s_gelu, i * 8 + (max(4 * kv + n - 1, 0) + 1))
                for j in range(16):
                    mm = pe.matmul(k.bank[4 + c][:, 0:NCMP], w1[:, kv, j // 8, j % 8, P * c:P * c + P],
                                   xt[:, kv, g, j % 8, j // 8:j // 8 + NCMP], start=(j == 0), stop=(j == 15))
                mm.then_inc(s_hid, 1)

            def second(i, kv, g):
                if g == 0:
                    pe.wait_ge(s_kcs, i * 2 + (kv + 1))
                pe.wait_ge(s_gelu, i * 8 + (4 * kv + 2 * g + 3))
                for nt in range(1 if kv == 0 else 4):
                    for c in range(2):
                        if kv == 0:
                            mm = pe.matmul(k.bank[7][HD * g:HD * g + HD, :], w2[:, 0, c, :], hid[:, g, c, :],
                                           start=(c == 0), stop=(c == 1))
                        else:
                            mm = pe.matmul(k.bank[7][:, P * nt + HD * g:P * nt + HD * g + HD],
                                           hid[:, g, c, P * nt:P * nt + P], w2[:, 1, c, :],
                                           start=(c == 0), stop=(c == 1))
                mm.then_inc(s_kc, 1)

            def modulation(i, kv, n):
                pe.wait_ge(k.s_ada[n], i * 32 + (16 * kv + 16))
                if n == 0:
                    pe.wait_ge(s_modT, i * 2 + (kv + 1))
                for c in range(DK):
                    mm = pe.matmul(k.bank[6][:, 9 * n:9 * n + 9], k.wada[:, n, c, :], k.cT[:, c, :], start=(c == 0), stop=(c == DK - 1))
                if n == 3:
                    mm.then_inc(s_mod, 1)

            def item(i, kv, following):
                pe.wait_ge(s_xtv, i * 16 + (8 * kv + 8))
                pe.wait_ge(s_xta, i * 16 + (8 * kv + 8))
                for n in range(4):
                    first(i, kv, n)
                    modulation(i, kv, n)
                    if n == 2:
                        second(i, kv, 0)
                    if following:
                        turn(*following, range(4 * n, 4 * n + 4))
                second(i, kv, 1)

            turn(0, 0, range(STRIDE), True)
            with pe.Fori(0, B - 1) as i:
                item(i, 0, (i, 1))
                item(i, 1, (i + 1, 0))
            item(B - 1, 0, (B - 1, 1))
            item(B - 1, 1, None)

        def copy(eng, i, kv, s, first=False):
            odd = s % 2
            if s < 2 and not first:
                eng.wait_ge(s_hid, i * 8 + (4 * kv - 3))
            eng.wait_ge(s_tr, i * 32 + (16 * kv + s + 1))
            for g in range(G):
                dst = xt[HD * odd:HD * odd + HD, kv, g, s // 2, :]
                src = k.bank[s % 4][HD * g:HD * g + HD, :]
                ins = eng.activation(dst, src, ACT.Copy) if odd else eng.tensor_copy(dst, src)
            ins.then_inc(s_xta if odd else s_xtv, 1)

        @block.vector
        def _(dve):
            def item(i, kv, following):
                if following:
                    for s in range(0, STRIDE, 2):
                        copy(dve, *following, s)
                dve.wait_ge(s_kst[kv], i * 16 + 1)
                dve.wait_ge(s_kc, i * 4 + (2 * kv + 3))
                dve.tensor_copy(kc_vc[:, kv, :], k.bank[7][:, :]).then_inc(s_kcs, 1)
                dve.wait_ge(s_mod, i * 2 + (kv + 1))
                m = bass.ds(i * 8 + 4 * kv, 4)
                dve.tensor_tensor(k.modT[:, m, :], k.bank[6][:, 0:36].rearrange("p (c r) -> p c r", r=9),
                                  k.vecT[:, m].unsqueeze(2).to_broadcast([P, 4, 9]), ALU.add).then_inc(s_modT, 1)

            dve.memset(hid[:, :, :, NCMP:NPIECE], 0.0).then_inc(s_zero, 1)
            dve.wait_ge(s_peT, 1)
            dve.tensor_copy(peT[:, :], k.bank[0][:, 0:32]).then_inc(s_peTs, 1)
            dve.wait_ge(s_peT, 2)
            dve.tensor_copy(k.peb[:, :, :], k.bank[1][:, 0:4].rearrange("p (v c) -> p v c", v=2)).then_inc(s_peb, 1)
            for s in range(0, STRIDE, 2):
                copy(dve, 0, 0, s, True)
            with dve.Fori(0, B - 1) as i:
                item(i, 0, (i, 1))
                item(i, 1, (i + 1, 0))
            item(B - 1, 0, (B - 1, 1))
            item(B - 1, 1, None)
            dve.wait_ge(s_modT, 2 * B + 1)
            for n, (lo, g) in enumerate(((8, 64), (32, 72), (56, 80))):
                dve.scalar_tensor_tensor(out=k.modA[:, n], in0=k.modT[:, lo:lo + 8, :], scalar=1.0,
                                         in1=k.vecT[:, g:g + 8].unsqueeze(2).to_broadcast([P, 8, 9]),
                                         op0=ALU.add, op1=ALU.mult).then_inc(s_modA, 1)

        @block.scalar
        def _(act):
            def item(i, kv, following, final=False):
                for n in range(4):
                    g, c = n // 2, n % 2
                    act.wait_ge(s_hid, i * 8 + (4 * kv + n + 2))
                    act.wait_ge(s_kc, i * 4 + (max(2 * kv + g - 1, 0) + 1))
                    act.activation(hid[:, g, c, 0:NCMP], k.bank[4 + c][:, 0:NCMP],
                                   ACT.Gelu_apprx_tanh, bias=k.peb[:, kv, c:c + 1]).then_inc(s_gelu, 1)
                    if following and n:
                        load_ada(k, act, i * 2 + (kv + 1), n - 1, final)
                    if following:
                        for s in range(4 * n + 1, 4 * n + 4, 2):
                            copy(act, *following, s)
                act.wait_ge(s_kcs, i * 2 + (kv + 2))
                if following:
                    load_ada(k, act, i * 2 + (kv + 1), 3, final)
                if kv == 0:
                    act.dma_start(k.kcT_d[:, bass.ds(i, 1), :].rearrange("p o n -> p (o n)"), kc_vc[:, 0, :]).then_inc(s_kst[0], 16)
                else:
                    act.dma_start(k.vc_d[:, bass.ds(i, 1), :, :].rearrange("p o t d -> p (o t d)"), kc_vc[:, 1, :]).then_inc(s_kst[1], 16)

            act.wait_ge(s_peb, 1)
            act.wait_ge(s_zero, 1)
            for s in range(1, STRIDE, 2):
                copy(act, 0, 0, s, True)
            NA = 48 // 8
            with act.Fori(0, NA - 1) as i:
                item(i, 0, (i, 1))
                item(i, 1, (i + 1, 0))
            item(NA - 1, 0, (NA - 1, 1))
            for i in range(NA - 1, B - 1):
                if i >= NA:
                    item(i, 0, (i, 1), True)
                item(i, 1, (i + 1, 0), True)
            item(B - 1, 0, (B - 1, 1), True)
            item(B - 1, 1, None)


def load_x(k, xT):
    nc = k.nc
    s_x, s_xt, s_xc = [k.sem(f"s_x{j}") for j in range(4)], k.sem("s_xt"), k.sem("s_xc")
    s_xs = k.sem("s_xs")
    with ExitStack() as ctx:
        xrow = k.sb("xrow", [P, 4, D], ctx=ctx)
        xsrow = k.sb("xsrow", [B, D], ctx=ctx)
        block = ctx.enter_context(nc.Block())

        @block.sync
        def _(sp):
            for ti in range(NTI):
                if ti >= 4:
                    sp.wait_ge(s_xt, 2 * (ti - 3))
                sp.dma_start(xrow[:, ti % 4], k.i["x_prompt"][0, P * ti:P * ti + P, :]).then_inc(s_x[ti % 4], 16)
                if ti == 0:
                    sp.dma_start(xsrow[:, :], k.i["x_sample"].rearrange("b o d -> (b o) d")).then_inc(s_xs, 16)
            w_v = k.i["w_in"][0].rearrange("(k p) n -> p k n", p=P)
            for u, off in enumerate((OFF_QB, OFF_KB)):
                sp.dma_start(k.mw[:, u], w_v[:, :, off:off + 512]).then_inc(k.s_mw[u], 16)

        @block.tensor
        def _(pe):
            for f in range(2 * NTI):
                ti, half = f // 2, f % 2
                pe.wait_ge(s_x[ti % 4], 16 * (ti // 4 + 1))
                if f >= 4:
                    pe.wait_ge(s_xc, f - 3)
                for q in range(4):
                    c = 4 * half + q
                    mm = pe.transpose(k.bank[f % 4][:, P * q:P * q + P], xrow[:, ti % 4, P * c:P * c + P], k.ident[:, :])
                mm.then_inc(s_xt, 1)
            pe.wait_ge(s_xs, 16)
            for c in range(DK):
                mm = pe.transpose(k.bank[4][:, B * c:B * c + B], xsrow[:, P * c:P * c + P], k.ident[0:B, 0:B])
            mm.then_inc(s_xt, 1)

        @block.vector
        def _(dve):
            for f in range(2 * NTI):
                ti, half = f // 2, f % 2
                dve.wait_ge(s_xt, f + 1)
                dve.tensor_copy(xT[:, 4 * half:4 * half + 4, P * ti:P * ti + P],
                                k.bank[f % 4][:, :].rearrange("p (q t) -> p q t", q=4)).then_inc(s_xc, 1)
            dve.wait_ge(s_xt, 2 * NTI + 1)
            dve.tensor_copy(xT[:, :, T:TT], k.bank[4][:, 0:B * DK].rearrange("p (c t) -> p c t", c=DK)).then_inc(s_xc, 1)


def norm(k, tag, src, n, dst, keep=None, keep_dst=None, load=None):
    nc = k.nc
    shift = (0, 24, 48)[n]
    s_sq, s_sum, s_ms, s_rt, s_rstd = (k.sem(f"{x}_{tag}") for x in ("s_sq", "s_sum", "s_ms", "s_rt", "s_rstd"))
    s_sqd, s_mul, s_out, s_smp = (k.sem(f"{x}_{tag}") for x in ("s_sqd", "s_mul", "s_nout", "s_smp"))
    s_keep, s_load = k.sem(f"s_keep_{tag}"), [k.sem(f"s_load{g}_{tag}") for g in range(NG)]
    with ExitStack() as ctx:
        sq = k.sb(f"sq_{tag}", [P, 4, GT], ctx=ctx)
        rs = k.sb(f"rs_{tag}", [P, NG, GT], ctx=ctx)
        tmp = k.sb(f"tmp_{tag}", [P, 4, GT], ctx=ctx)
        block = ctx.enter_context(nc.Block())

        if keep is not None:
            @block.sync
            def _(sp):
                sp.dma_start(keep, src[:, :, :]).then_inc(s_keep, 16)
                sp.wait_ge(s_out, NG * DK)
                sp.wait_ge(s_smp, DK + 1)
                sp.dma_start(keep_dst, dst[:, :, :]).then_inc(s_keep, 16)
                sp.wait_ge(s_keep, 32)

        if load is not None:
            @block.sync
            def _(sp):
                for g in range(NG):
                    sp.dma_start(src[:, :, GT * g:GT * g + GT], load[:, :, GT * g:GT * g + GT]).then_inc(s_load[g], 16)

        def squares(eng, g, odd, sem):
            if load is not None:
                eng.wait_ge(s_load[g], 16)
            for c in range(odd, DK, 2):
                f = g * DK + c
                x = src[:, c, GT * g:GT * g + GT]
                if f >= 4:
                    eng.wait_ge(s_sum, f - 3)
                ins = eng.tensor_tensor(sq[:, f % 4, :], x, x, ALU.mult) if odd else eng.activation(sq[:, f % 4, :], x, ACT.Square)
                ins.then_inc(sem, 1)

        @block.scalar
        def _(act):
            def root(g):
                act.wait_ge(s_ms, g + 1)
                act.activation(rs[:, g, :], rs[:, g, :], ACT.Sqrt).then_inc(s_rt, 1)

            def scale(g):
                w = GT if g < NG - 1 else T - GT * (NG - 1)
                for c in range(DK):
                    f = g * DK + c
                    act.wait_ge(s_mul, f + 1)
                    act.activation(dst[:, c, GT * g:GT * g + w], tmp[:, f % 4, 0:w], ACT.Identity, scale=k.modA[:, n, c, 0:1],
                                   bias=k.modT[:, shift + c, 0:1]).then_inc(s_out, 1)

            squares(act, 0, 0, s_sq)
            squares(act, 1, 0, s_sq)
            root(0)
            squares(act, 2, 0, s_sq)
            root(1)
            scale(0)
            root(2)
            scale(1)
            scale(2)

        @block.tensor
        def _(pe):
            for g in range(NG):
                for c in range(DK):
                    pe.wait_ge(s_sqd if c % 2 else s_sq, (g * DK + c) // 2 + 1)
                    pe.matmul(k.bank[g][:, 0:GT], k.ones[:, :], sq[:, (g * DK + c) % 4, :],
                              start=(c == 0), stop=(c == DK - 1)).then_inc(s_sum, 1)

        @block.vector
        def _(dve):
            def mean(g):
                dve.wait_ge(s_sum, DK * (g + 1))
                dve.tensor_scalar(rs[:, g, :], k.bank[g][:, 0:GT], 1.0 / D, EPS, ALU.mult, ALU.add).then_inc(s_ms, 1)

            def normed(g):
                dve.wait_ge(s_rt, g + 1)
                dve.reciprocal(rs[:, g, :], rs[:, g, :]).then_inc(s_rstd, 1)
                dve.wait_ge(s_rstd, g + 1)
                for c in range(DK):
                    f = g * DK + c
                    if f >= 4:
                        dve.wait_ge(s_out, f - 3)
                    if g == NG - 1 and c >= 4:
                        dve.wait_ge(s_smp, c - 3)
                    dve.tensor_tensor(tmp[:, f % 4, :], src[:, c, GT * g:GT * g + GT], rs[:, g, :], ALU.mult).then_inc(s_mul, 1)
                    if g == NG - 1:
                        dve.wait_ge(s_mul, f + 1)
                        dve.tensor_tensor(dst[:, c, T:TT], tmp[:, f % 4, GT - B:GT], k.modA[:, n, c, 1:9], ALU.mult).then_inc(s_smp, 1)

            squares(dve, 0, 1, s_sqd)
            squares(dve, 1, 1, s_sqd)
            mean(0)
            squares(dve, 2, 1, s_sqd)
            mean(1)
            normed(0)
            mean(2)
            normed(1)
            normed(2)
            dve.wait_ge(s_smp, DK)
            dve.tensor_tensor(dst[:, :, T:TT], dst[:, :, T:TT], k.modT[:, shift:shift + DK, 1:9], ALU.add).then_inc(s_smp, 1)


def mlstm_project(k):
    nc = k.nc
    w_v = k.i["w_in"][0].rearrange("(k p) n -> p k n", p=P)
    units = ((OFF_QB, k.qbT, 1.0), (OFF_KB, k.kbT, float(MD) ** -0.5))
    w, s_w, s_ws, s_gb = k.mw, k.s_mw, k.sem("s_mws"), k.sem("s_gb")
    s_fill, s_evT, s_evK, s_one = k.sem("s_mfill"), k.sem("s_mevT"), k.sem("s_mevK"), k.sem("s_mone")
    s_sm, s_gbb = k.sem("s_smallst"), k.sem("s_gbb")
    s_add = k.sem("s_madd")
    with ExitStack() as ctx:
        wsm = k.sb("mwsm", [P, DK, 32], ctx=ctx)
        gb = k.sb("gb", [1, 8], ctx=ctx)
        gbb = k.sb("gbb", [P, 8], ctx=ctx)
        block = ctx.enter_context(nc.Block())
        NT_FILLS = 2 * 4 * NG

        @block.sync
        def _(sp):
            sp.dma_start(wsm[:, :, 0:24], w_v[:, :, OFF_GA:OFF_QB]).then_inc(s_ws, 16)
            sp.dma_start(wsm[:, :, 24:32], w_v[:, :, OFF_IFB:OFF_OB]).then_inc(s_ws, 16)
            sp.dma_start(gb[:, :], k.i["mlstm_gate_b"]).then_inc(s_gb, 16)
            sp.wait_ge(s_fill, 4 * NG)
            sp.dma_start(w[:, 0], w_v[:, :, OFF_VB:OFF_VB + 512]).then_inc(s_w[0], 16)
            sp.wait_ge(s_add, 2)
            sp.dma_start(k.smalltok_d, k.small_s[:, :]).then_inc(s_sm, 16)
            sp.wait_ge(s_sm, 16)

        def tokens(ti):
            return slice(P * ti, P * ti + P) if ti < NTI else slice(T, TT)

        @block.tensor
        def _(pe):
            fill = 0

            def bank():
                if fill >= 8:
                    old = fill - 8
                    if old < NT_FILLS:
                        pe.wait_ge(s_evT, old + 1)
                    else:
                        pe.wait_ge(s_evK, old - NT_FILLS + 1)
                return k.bank[fill % 8]

            for u in range(2):
                pe.wait_ge(s_w[u], 16)
                for c in range(4):
                    for g in range(NG):
                        b = bank()
                        for kk in range(DK):
                            mm = pe.matmul(b[:, 0:GT], w[:, u, kk, P * c:P * c + P], k.uT[:, kk, GT * g:GT * g + GT],
                                           start=(kk == 0), stop=(kk == DK - 1))
                        mm.then_inc(s_fill, 1)
                        fill += 1
            pe.wait_ge(s_w[0], 32)
            pe.wait_ge(s_ws, 32)
            for src, n in ((w[:, 0], 512), (wsm, 32)):
                for ti in range(NTI + 1):
                    b = bank()
                    m = P if ti < NTI else B
                    for kk in range(DK):
                        mm = pe.matmul(b[0:m, 0:n], k.uT[:, kk, tokens(ti)], src[:, kk, :],
                                       start=(kk == 0), stop=(kk == DK - 1))
                    mm.then_inc(s_fill, 1)
                    fill += 1
            pe.wait_ge(s_evT, NT_FILLS)
            for ti in range(NTI + 1):
                b = bank()
                m = P if ti < NTI else B
                for h in range(MH):
                    mm = pe.transpose(b[0:m, P * h:P * h + P], k.kbT[:, h, tokens(ti)], k.ident[:, :])
                mm.then_inc(s_fill, 1)
                fill += 1
            b = bank()
            pe.wait_ge(s_gb, 16)
            pe.matmul(b[:, 0:8], k.ones[0:1, :], gb[0:1, :], start=True, stop=True).then_inc(s_fill, 1)

        @block.scalar
        def _(act):
            f = 0
            for _, dst, scale in units:
                for c in range(4):
                    for g in range(NG):
                        act.wait_ge(s_fill, f + 1)
                        act.activation(dst[:, c, GT * g:GT * g + GT], k.bank[f % 8][:, 0:GT], ACT.Copy, scale=scale).then_inc(s_evT, 1)
                        f += 1

        @block.vector
        def _(dve):
            dve.memset(k.vb[:, :, :, MD:MD + 1], 1.0).then_inc(s_one, 1)
            dve.memset(k.vb_s[:, :, MD:MD + 1], 1.0).then_inc(s_one, 1)
            f = NT_FILLS
            for kind in range(3):
                for ti in range(NTI + 1):
                    dve.wait_ge(s_fill, f + 1)
                    m = P if ti < NTI else B
                    n = 32 if kind == 1 else 512
                    b = k.bank[f % 8][0:m, 0:n]
                    if kind == 0:
                        dst = k.vb[:, ti, :, 0:MD] if ti < NTI else k.vb_s[:, :, 0:MD]
                        b = b.rearrange("p (h d) -> p h d", h=MH)
                    elif kind == 1:
                        dst = k.small[:, ti, :] if ti < NTI else k.small_s[:, :]
                    else:
                        dst = k.kb[:, ti, :] if ti < NTI else k.kb_s[:, :]
                    dve.tensor_copy(dst, b).then_inc(s_evK, 1)
                    f += 1
            dve.wait_ge(s_fill, f + 1)
            dve.tensor_copy(gbb[:, :], k.bank[f % 8][:, 0:8]).then_inc(s_gbb, 1)
            dve.wait_ge(s_gbb, 1)
            dve.wait_ge(s_evK, 18)
            dve.tensor_tensor(k.small[:, :, 24:32], k.small[:, :, 24:32], gbb[:, :].unsqueeze(1).to_broadcast([P, NTI, 8]), ALU.add).then_inc(s_add, 1)
            dve.tensor_tensor(k.small_s[:, 24:32], k.small_s[:, 24:32], gbb[0:B, :], ALU.add).then_inc(s_add, 1)


def mlstm_scan(k):
    nc = k.nc
    s_tri, s_chain, s_lf, s_bc, s_e = k.sem("s_tri"), k.sem("s_mchain"), k.sem("s_lf"), k.sem("s_bc"), k.sem("s_me")
    s_diag, s_crow, s_cmrow, s_q, s_S, s_B, s_A, s_swT = (k.sem(f"s_m_{x}") for x in ("diag", "crow", "cm", "q", "S", "B", "A", "swT"))
    s_E, s_w, s_swTs, s_kw, s_QC = (k.sem(f"s_m_{x}") for x in ("E", "w", "swTs", "kw", "QC"))
    s_U, s_sw, s_C = (k.sem(f"s_m_{x}", start=1) for x in ("U", "sw", "C"))
    s_hn, s_hT, s_hTs, s_st, s_init, s_hsq, s_hrt = (k.sem(f"s_m_{x}") for x in ("hn", "hT", "hTs", "st", "init", "hsq", "hrt"))
    NC = T // P
    W = MD + 1
    with ExitStack() as ctx:
        tri = k.sb("tri", [P, P], ctx=ctx)
        low = k.sb("low", [P, P], ctx=ctx)
        g1 = k.sb("mg1", [P, NC, MH], ctx=ctx)
        g2 = k.sb("mg2", [P, NC, MH], ctx=ctx)
        lf = k.sb("lf", [P, NC, MH], ctx=ctx)
        bc = k.sb("bcum", [P, NC, MH], ctx=ctx)
        bl = k.sb("blast", [P, NC, MH], ctx=ctx)
        cs = k.sb("cs", [P, NC, MH], ctx=ctx)
        diag = k.sb("mdiag", [P, MH, P], ctx=ctx)
        cm = k.sb("cm", [P, MH, P], ctx=ctx)
        ee = k.sb("ee", [P, MH, P], ctx=ctx)
        sw = k.sb("sw", [P, MH, P], ctx=ctx)
        swT = k.sb("swT", [P, MH, P], ctx=ctx)
        kw = k.sb("kw", [P, MH, P], ctx=ctx)
        qc = k.sb("qc", [P, MH, P], ctx=ctx)
        rmax = k.sb("rmax", [P, MH], ctx=ctx)
        cmax = k.sb("cmax", [P, MH], ctx=ctx)
        mx = k.sb("mx", [P, MH], ctx=ctx)
        nmx = k.sb("nmx", [P, MH], ctx=ctx)
        ml = k.sb("ml", [P, MH], ctx=ctx)
        mst = k.sb("mst", [P, MH], ctx=ctx)
        ein = k.sb("ein", [P, 4, MH], ctx=ctx)
        wx = k.sb("wx", [P, 4, MH], ctx=ctx)
        C = k.sb("Cst", [P, MH, W], ctx=ctx)
        num = k.sb("num", [P, MH, W], ctx=ctx)
        den = k.sb("den", [P, MH], ctx=ctx)
        hb = k.sb("hbuf", [P, NC * MH, P], ctx=ctx)
        mu = k.sb("mu", [P, NC * MH], ctx=ctx)
        var = k.sb("var", [P, NC * MH], ctx=ctx)
        PER = 16
        block = ctx.enter_context(nc.Block())

        @block.gpsimd
        def _(pool):
            pool.memset(tri[:, :], 1.0).then_inc(s_tri, 1)
            pool.memset(low[:, :], 0.0).then_inc(s_tri, 1)
            pool.wait_ge(s_tri, 2)
            pool.affine_select(out=tri[:, :], in_=tri[:, :], compare_op=ALU.is_ge, fill=0.0, base=0,
                               pattern=[[1, P]], channel_multiplier=-1).then_inc(s_tri, 1)
            pool.affine_select(out=low[:, :], in_=low[:, :], compare_op=ALU.is_ge, fill=NEG, base=0,
                               pattern=[[-1, P]], channel_multiplier=1).then_inc(s_tri, 1)

        @block.vector
        def _(dve):
            ch = Chain(dve, s_chain)
            f, i_ = k.small[:, :, 28:32], k.small[:, :, 24:28]
            dve.memset(mst[:, :], 0.0).then_inc(s_init, 1)
            dve.memset(C[:, :, :], 0.0).then_inc(s_init, 1)
            ch.link(dve.scalar_tensor_tensor(out=g1[:, :, :], in0=f, scalar=-1.0, in1=f, op0=ALU.mult, op1=ALU.max))
            dve.tensor_scalar(g2[:, :, :], f, 0.0, None, ALU.min).then_inc(s_lf, 1)
            dve.wait_ge(s_e, 2)
            dve.wait_ge(s_lf, 1)
            dve.tensor_tensor(lf[:, :, :], g2[:, :, :], g1[:, :, :], ALU.subtract).then_inc(s_lf, 1)
            dve.wait_ge(s_bc, 1)
            dve.tensor_copy(bc[:, :, :], k.bank[0][:, 0:NC * MH].rearrange("p (c h) -> p c h", h=MH)).then_inc(s_lf, 1)
            dve.tensor_copy(bl[:, :, :], k.bank[1][:, 0:NC * MH].rearrange("p (c h) -> p c h", h=MH)).then_inc(s_lf, 1)
            dve.wait_ge(s_lf, 4)
            ch.link(dve.tensor_tensor(cs[:, :, :], i_, bc[:, :, :], ALU.subtract))
            dve.wait_ge(s_init, 2)
            dve.wait_ge(s_tri, 4)
            base = ch.n

            with dve.Fori(0, NC) as i:
                ch.base = base
                ch.start(i, PER)
                csi = cs[:, bass.ds(i, 1), :].rearrange("p o h -> p (o h)")
                bci = bc[:, bass.ds(i, 1), :].rearrange("p o h -> p (o h)")
                dve.tensor_tensor(diag[:, :, :], k.ident[:, :].unsqueeze(1).to_broadcast([P, MH, P]),
                                  csi.unsqueeze(2).to_broadcast([P, MH, P]), ALU.mult).then_inc(s_diag, 1)
                crow = k.bank[0][:, :].rearrange("p (h s) -> p h s", h=MH)
                dve.wait_ge(s_crow, i + 1)
                dve.tensor_reduce(cmax[:, :], crow, AX.X, ALU.max).then_inc(s_cmrow, 1)
                ch.link(dve.tensor_tensor(cm[:, :, :], crow, low[:, :].unsqueeze(1).to_broadcast([P, MH, P]), ALU.add))
                ch.link(dve.tensor_reduce(rmax[:, :], cm[:, :, :], AX.X, ALU.max))
                dve.wait_ge(s_cmrow, i * 2 + 1)
                ch.link(dve.tensor_tensor(mx[:, :], rmax[:, :], mst[:, :], ALU.max))
                ch.link(dve.tensor_tensor(ml[:, :], cmax[:, :], mst[:, :], ALU.max))
                ch.link(dve.tensor_scalar(nmx[:, :], mx[:, :], -1.0, None, ALU.mult))
                ch.link(dve.tensor_tensor(ein[:, 0], mst[:, :], mx[:, :], ALU.subtract))
                ch.link(dve.tensor_tensor(ein[:, 1], nmx[:, :], bci, ALU.subtract))
                ch.link(dve.tensor_tensor(ein[:, 2], csi, ml[:, :], ALU.subtract))
                ch.link(dve.tensor_tensor(ein[:, 3], mst[:, :], ml[:, :], ALU.subtract))
                dve.tensor_tensor(mst[:, :], bl[:, bass.ds(i, 1), :].rearrange("p o h -> p (o h)"), ml[:, :], ALU.add).then_inc(s_cmrow, 1)
                dve.wait_ge(s_w, i + 1)
                dve.tensor_tensor(kw[:, :, :], k.kb[:, bass.ds(i, 1), :].rearrange("p o (h d) -> p (o h) d", h=MH),
                                  wx[:, 2].unsqueeze(2).to_broadcast([P, MH, P]), ALU.mult).then_inc(s_kw, 1)
                dve.wait_ge(s_E, i * 4 + 4)
                dve.wait_ge(s_S, i + 1)
                dve.tensor_tensor(sw[:, :, :], k.bank[1][:, :].rearrange("p (h s) -> p h s", h=MH), ee[:, :, :], ALU.mult).then_inc(s_sw, 1)
                dve.wait_ge(s_B, i + 1)
                for a in range(2):
                    last = dve.tensor_tensor(num[:, 2 * a:2 * a + 2, :], k.bank[5 + a][:, 0:2 * W].rearrange("p (h e) -> p h e", h=2),
                                             wx[:, 0, 2 * a:2 * a + 2].unsqueeze(2).to_broadcast([P, 2, W]), ALU.mult)
                    last.then_inc(s_QC, 1)
                ch.link(dve.tensor_tensor(C[:, :, :], C[:, :, :], wx[:, 3].unsqueeze(2).to_broadcast([P, MH, W]), ALU.mult))
                dve.wait_ge(s_QC, i * 2 + 2)
                dve.wait_ge(s_A, i + 1)
                for a in range(2):
                    ch.link(dve.tensor_tensor(num[:, 2 * a:2 * a + 2, :], num[:, 2 * a:2 * a + 2, :],
                                              k.bank[3 + a][:, 0:2 * W].rearrange("p (h e) -> p h e", h=2), ALU.add))
                dve.wait_ge(s_U, i + 2)
                for a in range(2):
                    dve.tensor_tensor(C[:, 2 * a:2 * a + 2, :], C[:, 2 * a:2 * a + 2, :],
                                      k.bank[5 + a][:, 0:2 * W].rearrange("p (h e) -> p h e", h=2), ALU.add).then_inc(s_C, 1)
                ch.link(dve.scalar_tensor_tensor(out=den[:, :].unsqueeze(2), in0=num[:, :, MD:W], scalar=-1.0, in1=num[:, :, MD:W],
                                                 op0=ALU.mult, op1=ALU.max))
                ch.link(dve.tensor_tensor(den[:, :], den[:, :], wx[:, 1], ALU.max))
                ch.link(dve.reciprocal(den[:, :], den[:, :]))
                ch.link(dve.tensor_tensor(hb[:, bass.ds(i * MH, MH), :], num[:, :, 0:MD],
                                          den[:, :].unsqueeze(2).to_broadcast([P, MH, MD]), ALU.mult))
                ch.done()
            ch.per, ch.base = None, base + NC * PER
            ch.n = 0
            n = NC * MH
            ch.link(dve.tensor_reduce(mu[:, :], hb[:, :, :], AX.X, ALU.add))
            ch.link(dve.tensor_scalar(mu[:, :], mu[:, :], 1.0 / MD, None, ALU.mult))
            for c in range(NC):
                s = slice(MH * c, MH * c + MH)
                dve.tensor_tensor(hb[:, s, :], hb[:, s, :], mu[:, s].unsqueeze(2).to_broadcast([P, MH, MD]), ALU.subtract).then_inc(s_hn, 1)
            for c in range(NC):
                dve.wait_ge(s_hsq, c + 1)
                dve.tensor_reduce(var[:, MH * c:MH * c + MH], (ee if c % 2 else cm)[:, :, :], AX.X, ALU.add).then_inc(s_hn, 1)
            dve.wait_ge(s_hn, 2 * NC)
            ch.link(dve.tensor_scalar(var[:, :], var[:, :], 1.0 / MD, EPS, ALU.mult, ALU.add))
            dve.wait_ge(s_hrt, 1)
            ch.link(dve.reciprocal(var[:, :], var[:, :]))
            for c in range(NC):
                s = slice(MH * c, MH * c + MH)
                dve.tensor_tensor(hb[:, s, :], hb[:, s, :], var[:, s].unsqueeze(2).to_broadcast([P, MH, MD]), ALU.mult).then_inc(s_hn, 1)
            for c in range(NC):
                dve.wait_ge(s_hT, c + 1)
                dve.tensor_tensor(k.hbT[:, :, P * c:P * c + P], k.bank[c % 4][:, :].rearrange("p (h t) -> p h t", h=MH),
                                  k.vecT[:, 88:92].unsqueeze(2).to_broadcast([P, MH, P]), ALU.mult).then_inc(s_hTs, 1)

        @block.scalar
        def _(act):
            act.wait_ge(s_chain, 1)
            act.activation(g1[:, :, :], g1[:, :, :], ACT.Exp, scale=-1.0).then_inc(s_e, 1)
            act.wait_ge(s_e, 1)
            act.activation(g1[:, :, :], g1[:, :, :], ACT.Ln, bias=1.0).then_inc(s_e, 1)
            with act.Fori(0, NC) as i:
                act.wait_ge(s_U, i + 1)
                act.activation(qc[:, :, :], k.qbT[:, :, bass.ds(i * P, P)], ACT.Copy).then_inc(s_q, 1)
                act.wait_ge(s_cmrow, i * 2 + 2)
                act.activation(wx[:, :, :], ein[:, :, :], ACT.Exp).then_inc(s_w, 1)
                for h in range(MH):
                    act.activation(ee[:, h, :], cm[:, h, :], ACT.Exp, bias=nmx[:, h:h + 1]).then_inc(s_E, 1)
                act.wait_ge(s_swT, i + 1)
                act.activation(swT[:, :, :], k.bank[2][:, :].rearrange("p (h s) -> p h s", h=MH), ACT.Copy).then_inc(s_swTs, 1)
            for c in range(NC):
                act.wait_ge(s_hn, c + 1)
                if c >= 2:
                    act.wait_ge(s_hn, NC + c - 1)
                act.activation((ee if c % 2 else cm)[:, :, :], hb[:, MH * c:MH * c + MH, :], ACT.Square).then_inc(s_hsq, 1)
            act.wait_ge(s_chain, 2 + NC * PER + 3)
            act.activation(var[:, :], var[:, :], ACT.Sqrt).then_inc(s_hrt, 1)

        @block.tensor
        def _(pe):
            pe.wait_ge(s_lf, 2)
            pe.wait_ge(s_tri, 4)
            pe.matmul(k.bank[0][:, 0:NC * MH], tri[:, :], lf[:, :, :].rearrange("p c h -> p (c h)"), start=True, stop=True)
            pe.matmul(k.bank[1][:, 0:NC * MH], k.ones[:, :], lf[:, :, :].rearrange("p c h -> p (c h)"), start=True, stop=True).then_inc(s_bc, 1)
            pe.wait_ge(s_lf, 4)
            with pe.Fori(0, NC) as i:
                pe.wait_ge(s_diag, i + 1)
                pe.matmul(k.bank[0][:, :], k.ones[:, :], diag[:, :, :].rearrange("p h s -> p (h s)"), start=True, stop=True).then_inc(s_crow, 1)
                pe.wait_ge(s_q, i + 1)
                pe.wait_ge(s_sw, i + 1)
                for h in range(MH):
                    mm = pe.matmul(k.bank[1][:, P * h:P * h + P], qc[:, h, :], k.kbT[:, h:h + 1, bass.ds(i * P, P)].rearrange("p o t -> p (o t)"),
                                   start=True, stop=True)
                mm.then_inc(s_S, 1)
                pe.wait_ge(s_C, i * 2 + 1)
                for h in range(MH):
                    mm = pe.matmul(k.bank[5 + h // 2][:, W * (h % 2):W * (h % 2) + W], qc[:, h, :], C[:, h, :], start=True, stop=True)
                mm.then_inc(s_B, 1)
                pe.wait_ge(s_sw, i + 2)
                for h in range(MH):
                    mm = pe.transpose(k.bank[2][:, P * h:P * h + P], sw[:, h, :], k.ident[:, :])
                mm.then_inc(s_swT, 1)
                pe.wait_ge(s_swTs, i + 1)
                v = k.vb[:, bass.ds(i, 1), :, :]
                for h in range(MH):
                    mm = pe.matmul(k.bank[3 + h // 2][:, W * (h % 2):W * (h % 2) + W], swT[:, h, :], v[:, :, h, :].rearrange("p o e -> p (o e)"),
                                   start=True, stop=True)
                mm.then_inc(s_A, 1)
                pe.wait_ge(s_QC, i * 2 + 2)
                for h in range(MH):
                    mm = pe.matmul(k.bank[5 + h // 2][:, W * (h % 2):W * (h % 2) + W], kw[:, h, :], v[:, :, h, :].rearrange("p o e -> p (o e)"),
                                   start=True, stop=True)
                mm.then_inc(s_U, 1)
            for c in range(NC):
                pe.wait_ge(s_hn, 2 * NC + c + 1)
                if c >= 4:
                    pe.wait_ge(s_hTs, c - 3)
                for h in range(MH):
                    mm = pe.transpose(k.bank[c % 4][:, P * h:P * h + P], hb[:, MH * c + h, :], k.ident[:, :])
                mm.then_inc(s_hT, 1)

        @block.sync
        def _(sp):
            sp.wait_ge(s_C, 2 * NC + 1)
            sp.dma_start(k.o["C_prompt"][0, 0].rearrange("h d e -> d h e"), C[:, :, 0:MD]).then_inc(s_st, 16)
            with nc.allow_non_contiguous_dma(reason="512 normalizer entries"):
                sp.dma_start(k.o["n_prompt"][0, 0].rearrange("h d -> d h"), C[:, :, MD:W].rearrange("p h o -> p (h o)")).then_inc(s_st, 16)
            sp.wait_ge(s_cmrow, 2 * NC)
            sp.dma_start(k.o["m_prompt"][0], mst[0:1, :]).then_inc(s_st, 16)
            sp.wait_ge(s_st, 48)


def mlstm_decode(k):
    nc = k.nc
    W = MD + 1
    BH = B * MH
    s_in, s_chain, s_e, s_bcp, s_bcs, s_km, s_U, s_C = (k.sem(f"s_d_{x}") for x in ("in", "chain", "e", "bcp", "bcs", "km", "U", "C"))
    s_nT, s_h, s_sum, s_rt, s_st, s_nrow = (k.sem(f"s_d_{x}") for x in ("nT", "h", "sum", "rt", "st", "nrow"))
    with ExitStack() as ctx:
        C = k.sb("Cs", [P, BH, W], ctx=ctx)
        n0 = k.sb("n0", [BH, P], ctx=ctx)
        nrow = k.sb("nrow", [BH, P], ctx=ctx)
        ncol = k.sb("ncol", [P, BH], ctx=ctx)
        m0 = k.sb("m0", [B, MH], ctx=ctx)
        g1 = k.sb("dg1", [B, MH], ctx=ctx)
        g2 = k.sb("dg2", [B, MH], ctx=ctx)
        mm_ = k.sb("dm", [B, MH], ctx=ctx)
        ein = k.sb("dein", [B, 3, MH], ctx=ctx)
        dg = k.sb("ddiag", [B, 2, B, MH], ctx=ctx)
        wb = k.sb("dwb", [P, 2, BH], ctx=ctx)
        kws = k.sb("kws", [B, 512], ctx=ctx)
        km = k.sb("km", [B, B, 512], ctx=ctx)
        prod = k.sb("dprod", [P, MH, B], ctx=ctx)
        hT = k.sb("dhT", [P, MH, B], ctx=ctx)
        t1 = k.sb("dt1", [P, MH, B], ctx=ctx)
        t2 = k.sb("dt2", [P, MH, B], ctx=ctx)
        block = ctx.enter_context(nc.Block())
        groups = [(a, min(3, BH - a)) for a in range(0, BH, 3)]
        i_, f = k.small_s[:, 24:28], k.small_s[:, 28:32]

        @block.sync
        def _(sp):
            sp.dma_start(m0[:, :], k.i["state_mlstm_m"][0]).then_inc(s_in, 16)
            sp.dma_start(n0[:, :], k.i["state_mlstm_n"][0].rearrange("b h d -> (b h) d")).then_inc(s_in, 16)
            sp.dma_start(C[:, :, 0:MD], k.i["state_mlstm_C"][0].rearrange("b h d e -> d (b h) e")).then_inc(s_in, 16)
            sp.wait_ge(s_C, 2 + len(groups))
            sp.dma_start(k.o["C_sample"][0].rearrange("b h d e -> d (b h) e"), C[:, :, 0:MD]).then_inc(s_st, 16)
            sp.wait_ge(s_chain, 4)
            sp.dma_start(k.o["m_sample"][0], mm_[:, :]).then_inc(s_st, 16)
            sp.wait_ge(s_nrow, 1)
            sp.dma_start(k.o["n_sample"][0].rearrange("b h d -> (b h) d"), nrow[:, :]).then_inc(s_st, 16)
            sp.wait_ge(s_st, 48)

        @block.vector
        def _(dve):
            ch = Chain(dve, s_chain)
            ch.link(dve.scalar_tensor_tensor(out=g1[:, :], in0=f, scalar=-1.0, in1=f, op0=ALU.mult, op1=ALU.max))
            dve.wait_ge(s_e, 2)
            dve.wait_ge(s_in, 48)
            ch.link(dve.scalar_tensor_tensor(out=g2[:, :], in0=f, scalar=0.0, in1=g1[:, :], op0=ALU.min, op1=ALU.subtract))
            ch.link(dve.tensor_tensor(g2[:, :], g2[:, :], m0[:, :], ALU.add))
            ch.link(dve.tensor_tensor(mm_[:, :], g2[:, :], i_, ALU.max))
            ch.link(dve.tensor_tensor(ein[:, 0], g2[:, :], mm_[:, :], ALU.subtract))
            ch.link(dve.tensor_scalar(ein[:, 1], mm_[:, :], -1.0, None, ALU.mult))
            ch.link(dve.tensor_tensor(ein[:, 2], i_, mm_[:, :], ALU.subtract))
            dve.wait_ge(s_e, 3)
            ch.link(dve.tensor_tensor(dg[:, :, :, :], k.ident[0:B, 0:B].unsqueeze(1).unsqueeze(3).to_broadcast([B, 2, B, MH]),
                                      ein[:, 0:2].unsqueeze(2).to_broadcast([B, 2, B, MH]), ALU.mult))
            ch.link(dve.tensor_tensor(kws[:, :].rearrange("b (h d) -> b h d", h=MH), k.kb_s[:, :].rearrange("b (h d) -> b h d", h=MH),
                                      ein[:, 2].unsqueeze(2).to_broadcast([B, MH, MD]), ALU.mult))
            for b in range(B):
                dve.tensor_scalar(km[:, b, :], kws[:, :], k.ident[0:B, b:b + 1], None, ALU.mult).then_inc(s_km, 1)
            dve.wait_ge(s_bcp, 1)
            dve.tensor_copy(wb[:, :, :], k.bank[7][:, 0:2 * BH].rearrange("p (a n) -> p a n", a=2)).then_inc(s_bcs, 1)
            dve.wait_ge(s_nT, 1)
            dve.tensor_copy(C[:, :, MD:W], k.bank[6][:, 0:BH].unsqueeze(2)).then_inc(s_C, 1)
            dve.wait_ge(s_bcs, 1)
            dve.wait_ge(s_C, 1)
            dve.tensor_tensor(C[:, :, :], C[:, :, :], wb[:, 0].unsqueeze(2).to_broadcast([P, BH, W]), ALU.mult).then_inc(s_C, 1)
            dve.wait_ge(s_C, 2)
            for n, (a, w) in enumerate(groups):
                dve.wait_ge(s_U, n + 1)
                dve.tensor_tensor(C[:, a:a + w, :], C[:, a:a + w, :],
                                  k.bank[n % 6][:, 0:w * W].rearrange("p (n e) -> p n e", n=w), ALU.add).then_inc(s_C, 1)
            dve.wait_ge(s_C, 2 + len(groups))
            ch.link(dve.tensor_copy(ncol[:, :], C[:, :, MD:W].rearrange("p n o -> p (n o)")))
            ch.link(dve.tensor_tensor(prod[:, :, :], ncol[:, :].rearrange("p (b h) -> p h b", h=MH), k.qbT[:, :, T:TT], ALU.mult))
            dve.wait_ge(s_h, 2)
            den = k.bank[1][:, 0:BH].rearrange("p (h b) -> p h b", h=MH)
            ch.link(dve.tensor_copy(t2[:, :, :], den))
            ch.link(dve.scalar_tensor_tensor(out=t1[:, :, :], in0=t2[:, :, :], scalar=-1.0, in1=t2[:, :, :], op0=ALU.mult, op1=ALU.max))
            ch.link(dve.tensor_tensor(t1[:, :, :], t1[:, :, :], wb[:, 1].rearrange("p (b h) -> p h b", h=MH), ALU.max))
            ch.link(dve.reciprocal(t1[:, :, :], t1[:, :, :]))
            ch.link(dve.tensor_tensor(hT[:, :, :], k.bank[0][:, 0:BH].rearrange("p (h b) -> p h b", h=MH), t1[:, :, :], ALU.mult))
            dve.wait_ge(s_sum, 1)
            ch.link(dve.scalar_tensor_tensor(out=hT[:, :, :], in0=k.bank[2][:, 0:BH].rearrange("p (h b) -> p h b", h=MH), scalar=-1.0 / MD,
                                             in1=hT[:, :, :], op0=ALU.mult, op1=ALU.add))
            ch.link(dve.tensor_tensor(t2[:, :, :], hT[:, :, :], hT[:, :, :], ALU.mult))
            dve.wait_ge(s_sum, 2)
            ch.link(dve.tensor_scalar(t1[:, :, :], k.bank[3][:, 0:BH].rearrange("p (h b) -> p h b", h=MH), 1.0 / MD, EPS, ALU.mult, ALU.add))
            dve.wait_ge(s_rt, 1)
            ch.link(dve.reciprocal(t1[:, :, :], t1[:, :, :]))
            ch.link(dve.tensor_tensor(hT[:, :, :], hT[:, :, :], t1[:, :, :], ALU.mult))
            ch.link(dve.tensor_tensor(k.hbT[:, :, T:TT], hT[:, :, :], k.vecT[:, 88:92].unsqueeze(2).to_broadcast([P, MH, B]), ALU.mult))
            dve.wait_ge(s_nT, 2)
            dve.tensor_copy(nrow[:, :], k.bank[5][0:BH, 0:P]).then_inc(s_nrow, 1)

        @block.scalar
        def _(act):
            act.wait_ge(s_chain, 1)
            act.activation(g1[:, :], g1[:, :], ACT.Exp, scale=-1.0).then_inc(s_e, 1)
            act.wait_ge(s_e, 1)
            act.activation(g1[:, :], g1[:, :], ACT.Ln, bias=1.0).then_inc(s_e, 1)
            act.wait_ge(s_chain, 7)
            act.activation(ein[:, :, :], ein[:, :, :], ACT.Exp).then_inc(s_e, 1)
            act.wait_ge(s_chain, 19)
            act.activation(t1[:, :, :], t1[:, :, :], ACT.Sqrt).then_inc(s_rt, 1)

        @block.tensor
        def _(pe):
            pe.wait_ge(s_in, 48)
            pe.transpose(k.bank[6][:, 0:BH], n0[:, :], k.ident[0:BH, 0:BH]).then_inc(s_nT, 1)
            pe.wait_ge(s_chain, 8)
            pe.matmul(k.bank[7][:, 0:2 * BH], k.ones[0:B, :], dg[:, :, :, :].rearrange("b a c h -> b (a c h)"), start=True, stop=True).then_inc(s_bcp, 1)
            pe.wait_ge(s_km, B)
            for n, (a, w) in enumerate(groups):
                if n >= 6:
                    pe.wait_ge(s_C, n - 3)
                for q in range(w):
                    b, h = (a + q) // MH, (a + q) % MH
                    mm = pe.matmul(k.bank[n % 6][:, q * W:q * W + W], km[:, b, P * h:P * h + P], k.vb_s[:, h, :], start=True, stop=True)
                mm.then_inc(s_U, 1)
            pe.wait_ge(s_C, 2 + len(groups))
            for b in range(B):
                for h in range(MH):
                    mm = pe.matmul(k.bank[0][:, h * B + b:h * B + b + 1], C[:, MH * b + h, 0:MD], k.qbT[:, h, T + b:T + b + 1], start=True, stop=True)
            mm.then_inc(s_h, 1)
            pe.wait_ge(s_chain, 10)
            pe.transpose(k.bank[5][0:BH, 0:P], ncol[:, :], k.ident[:, :]).then_inc(s_nT, 1)
            pe.wait_ge(s_chain, 11)
            pe.matmul(k.bank[1][:, 0:BH], k.ones[:, :], prod[:, :, :].rearrange("p h b -> p (h b)"), start=True, stop=True).then_inc(s_h, 1)
            pe.wait_ge(s_chain, 16)
            pe.matmul(k.bank[2][:, 0:BH], k.ones[:, :], hT[:, :, :].rearrange("p h b -> p (h b)"), start=True, stop=True).then_inc(s_sum, 1)
            pe.wait_ge(s_chain, 18)
            pe.matmul(k.bank[3][:, 0:BH], k.ones[:, :], t2[:, :, :].rearrange("p h b -> p (h b)"), start=True, stop=True).then_inc(s_sum, 1)


def nsa_project(k):
    nc = k.nc
    w_v = k.i["w_in"][0].rearrange("(k p) n -> p k n", p=P)
    s_wq, s_wk, s_fill, s_evq, s_evk, s_kT, s_out = (k.sem(f"s_n_{x}") for x in ("wq", "wk", "fill", "evq", "evk", "kT", "out"))
    s_kTs = k.sem("s_n_kTs")
    s_gate, s_u = k.sem("s_n_gate"), k.sem("s_n_u")
    with ExitStack() as ctx:
        uT = k.sb("nuT", [P, DK, TT], ctx=ctx)
        kv_s = k.sb("kv_s", [B, 768], ctx=ctx)
        wq = k.sb("nwq", [P, DK, 4, G, HD], ctx=ctx)
        wk = k.sb("nwk", [P, DK, 768], ctx=ctx)
        block = ctx.enter_context(nc.Block())
        NQ = 4 * NG

        @block.sync
        def _(sp):
            sp.dma_start(uT[:, :, :], k.uT_d).then_inc(s_u, 16)
            for c in range(DK):
                for g in range(G):
                    sp.dma_start(wq[:, c, :, g, :], w_v[:, c, 256 * g:256 * g + 256].rearrange("p (j d) -> p j d", j=4)).then_inc(s_wq, 16)
            sp.dma_start(wk[:, :, :], w_v[:, :, OFF_KVA:OFF_GA]).then_inc(s_wk, 16)
            win = k.o["win_sample"][0].rearrange("b w v g d -> b w (v g d)")
            old = k.i["cache_nsa_win"][0].rearrange("b w v g d -> b w (v g d)")
            sp.dma_start(win[:, 0:WIN - 1, :], old[:, 1:WIN, :]).then_inc(s_out, 16)
            sp.wait_ge(s_evk, 2 * (NTI + 1))
            kv = k.o["kv_prompt"][0, 0].rearrange("(c p) v g d -> p c (v g d)", p=P)
            sp.dma_start(kv, k.kv[:, :, 0:512]).then_inc(s_out, 16)
            wp = k.o["win_prompt"][0, 0].rearrange("(c p) v g d -> p c (v g d)", p=P)
            sp.dma_start(wp, k.kv[:, NTI - WIN // P:NTI, 512:768]).then_inc(s_out, 16)
            sp.dma_start(k.o["kv_sample"][0].rearrange("b o v g d -> b (o v g d)"), kv_s[:, 0:512]).then_inc(s_out, 16)
            sp.dma_start(win[:, WIN - 1, :], kv_s[:, 512:768]).then_inc(s_out, 16)
            sp.wait_ge(s_out, 80)

        @block.tensor
        def _(pe):
            fill = 0
            pe.wait_ge(s_u, 16)
            pe.wait_ge(s_wq, 16 * DK * G)
            for j in range(4):
                for g in range(NG):
                    if fill >= 8:
                        pe.wait_ge(s_evq, fill - 7)
                    for kk in range(DK):
                        mm = pe.matmul(k.bank[fill % 8][:, 0:GT], wq[:, kk, j].rearrange("p g d -> p (g d)"),
                                       uT[:, kk, GT * g:GT * g + GT], start=(kk == 0), stop=(kk == DK - 1))
                    mm.then_inc(s_fill, 1)
                    fill += 1
            pe.wait_ge(s_wk, 16)
            for ti in range(NTI + 1):
                m = P if ti < NTI else B
                for half in range(2):
                    old = fill - 8
                    if old < NQ:
                        pe.wait_ge(s_evq, old + 1)
                    else:
                        pe.wait_ge(s_evk, old - NQ + 1)
                    for kk in range(DK):
                        mm = pe.matmul(k.bank[fill % 8][0:m, 0:384], uT[:, kk, P * ti:P * ti + m],
                                       wk[:, kk, 384 * half:384 * half + 384], start=(kk == 0), stop=(kk == DK - 1))
                    mm.then_inc(s_fill, 1)
                    fill += 1
            pe.wait_ge(s_evk, 2 * (NTI + 1))
            for n in range(4):
                for q in range(4):
                    ti = 4 * (n % 2) + q
                    off = 256 if n < 2 else 512
                    mm = pe.transpose(k.bank[n][:, P * q:P * q + P], k.kv[:, ti, off:off + P], k.ident[:, :])
                mm.then_inc(s_kT, 1)

        @block.scalar
        def _(act):
            act.activation(k.small[:, :, 0:24], k.small[:, :, 0:24], ACT.Sigmoid).then_inc(s_gate, 1)
            for f in range(NQ):
                act.wait_ge(s_fill, f + 1)
                j, g = f // NG, f % NG
                act.activation(k.qT[:, j, GT * g:GT * g + GT], k.bank[f % 8][:, 0:GT], ACT.Copy, scale=float(HD) ** -0.5).then_inc(s_evq, 1)

        @block.vector
        def _(dve):
            for n in range(2 * (NTI + 1)):
                f = NQ + n
                ti, half = n // 2, n % 2
                dve.wait_ge(s_fill, f + 1)
                m = P if ti < NTI else B
                dst = k.kv[:, ti, 384 * half:384 * half + 384] if ti < NTI else kv_s[:, 384 * half:384 * half + 384]
                dve.tensor_copy(dst, k.bank[f % 8][0:m, 0:384]).then_inc(s_evk, 1)
            dve.wait_ge(s_evq, NQ)
            dve.tensor_copy(k.qTs[:, :, :], k.qT[:, :, T:TT]).then_inc(s_kTs, 1)
            for n in range(4):
                dve.wait_ge(s_kT, n + 1)
                dst = k.ksT if n < 2 else k.kwT
                dve.tensor_copy(dst[:, 512 * (n % 2):512 * (n % 2) + 512], k.bank[n][:, :]).then_inc(s_kTs, 1)


def prompt_compress(k):
    nc = k.nc
    NPP = T // STRIDE
    s_raw, s_w1, s_w2, s_pe = k.sem("s_pr_raw"), k.sem("s_pr_w1"), k.sem("s_pr_w2"), k.sem("s_pr_pe")
    s_tr, s_xt, s_hid, s_gelu, s_out, s_outs, s_zero = (k.sem(f"s_pr_{x}") for x in ("tr", "xt", "hid", "gelu", "o", "os", "z"))
    with ExitStack() as ctx:
        w1 = k.sb("pw1", [P, 2, 2, 8, CH], ctx=ctx)
        w2 = k.sb("pw2", [P, 2, 2, HD], ctx=ctx)
        perow = k.sb("pperow", [32, P], ctx=ctx)
        turned = k.sb("pturned", [NPP, G, STRIDE, HD], ctx=ctx)
        xt = k.sb("pxt", [P, 2, 8, G, NPP], ctx=ctx)
        hid = k.sb("phid", [P, 2, 2, G, NPP], ctx=ctx)
        block = ctx.enter_context(nc.Block())

        @block.sync
        def _(sp):
            load_cmp_weights(k, sp, w1, w2, perow, (s_w1, s_w2, s_pe))
            src = k.o["kv_prompt"][0, 0].rearrange("(n s) v g d -> n s v g d", s=STRIDE)
            for kv in range(2):
                if kv:
                    sp.wait_ge(s_tr, 2)
                for g in range(G):
                    sp.dma_start(turned[:, g], src[:, :, kv, g, :]).then_inc(s_raw, 16)
            sp.wait_ge(s_pe, 16)

        @block.gpsimd
        def _(pool):
            pool.memset(hid[:, :, :, :, NCP:NPP], 0.0).then_inc(s_zero, 1)

        @block.tensor
        def _(pe):
            for f in range(4):
                kv, half = f // 2, f % 2
                pe.wait_ge(s_raw, 32 * (kv + 1))
                for q in range(4):
                    for g in range(G):
                        s2 = 2 * (4 * half + q)
                        mm = pe.transpose(k.bank[f][:, NPP * (2 * q + g):NPP * (2 * q + g) + NPP],
                                          turned[:, g, s2:s2 + 2, :].rearrange("p s d -> p (s d)"), k.ident[0:NPP, 0:NPP])
                mm.then_inc(s_tr, 1)
            pe.wait_ge(s_w1, 32)
            pe.wait_ge(s_w2, 32)
            pe.wait_ge(s_xt, 4)
            for kv in range(2):
                for c in range(2):
                    for j in range(16):
                        mm = pe.matmul(k.bank[4 + 2 * kv + c][:, 0:2 * NCP], w1[:, kv, j // 8, j % 8, P * c:P * c + P],
                                       xt[:, kv, j % 8, :, j // 8:j // 8 + NCP], start=(j == 0), stop=(j == 15))
                    mm.then_inc(s_hid, 1)
            for kv in range(2):
                pe.wait_ge(s_gelu, 2 * kv + 2)
                for g in range(G):
                    for c in range(2):
                        if kv == 0:
                            mm = pe.matmul(k.bank[0][HD * g:HD * g + HD, 0:NPP], w2[:, 0, c, :], hid[:, 0, c, g, :],
                                           start=(c == 0), stop=(c == 1))
                        else:
                            mm = pe.matmul(k.bank[1][0:NPP, HD * g:HD * g + HD], hid[:, 1, c, g, :], w2[:, 1, c, :],
                                           start=(c == 0), stop=(c == 1))
                mm.then_inc(s_out, 1)

        @block.vector
        def _(dve):
            for f in range(4):
                kv, half = f // 2, f % 2
                dve.wait_ge(s_tr, f + 1)
                dve.tensor_copy(xt[:, kv, 4 * half:4 * half + 4].rearrange("p q g n -> p (q g n)"), k.bank[f][:, :]).then_inc(s_xt, 1)
            dve.wait_ge(s_out, 1)
            dve.tensor_copy(k.kcpT[:, :], k.bank[0][:, 0:NPP]).then_inc(s_outs, 1)
            dve.wait_ge(s_out, 2)
            dve.tensor_copy(k.vcp[:, :], k.bank[1][0:NPP, 0:P]).then_inc(s_outs, 1)

        @block.scalar
        def _(act):
            act.wait_ge(s_zero, 1)
            for kv in range(2):
                for c in range(2):
                    act.wait_ge(s_hid, 2 * kv + c + 1)
                    act.activation(hid[:, kv, c, :, 0:NCP], k.bank[4 + 2 * kv + c][:, 0:2 * NCP].rearrange("p (g n) -> p g n", g=G),
                                   ACT.Gelu_apprx_tanh, bias=k.peb[:, kv, c:c + 1]).then_inc(s_gelu, 1)


def prompt_attention(k):
    nc = k.nc
    assert T // SEL <= TOPN
    s_strip = [k.sem(f"s_pa_strip{g}") for g in range(G)]
    s_q, s_wf, s_sc, s_nm, s_ch = (k.sem(f"s_pa_{x}") for x in ("q", "wf", "sc", "nm", "ch"))
    s_add, s_exp, s_T, s_pta, s_ptd, s_pv, s_o = (k.sem(f"s_pa_{x}", start=1) for x in ("add", "exp", "T", "pta", "ptd", "pv", "o"))
    s_oT, s_oTs, s_mz = (k.sem(f"s_pa_{x}") for x in ("oT", "oTs", "mz"))
    NU = G * NTI
    units = [(g, ti) for g in range(G) for ti in range(NTI)]
    GATE = (1, 2, 0)
    WOFF, COFF, SW = T, T + 5 * P, T + 5 * P + 64

    def ptiles(ti):
        sel = [(P * s, P) for s in range(ti + 1)]
        nw = min(ti + 1, 5)
        win = [(WOFF + P * s, P) for s in range(5 - nw, 5)]
        return sel, win, [(COFF, min(8 * ti + 7, NCP))]

    fills = []
    for u, (g, ti) in enumerate(units):
        n = sum(len(x) for x in ptiles(ti))
        a = m = 0
        while a < n:
            w = min(4, n - a) - (n - a == 5)
            fills.append((u, a, w, m))
            a, m = a + w, m + 1
    NFA = sum(1 for f in fills if f[3] % 2 == 0)
    NFD = len(fills) - NFA

    def copied(upto, odd):
        return sum(1 for f in fills[:upto] if f[3] % 2 == odd)

    with ExitStack() as ctx:
        strip = k.sb("strip", [P, G, T], ctx=ctx)
        wf = k.sb("wfirst", [P, G, P], ctx=ctx)
        qh = k.sb("qh", [P, T], ctx=ctx)
        S = k.sb("Sp", [P, 2, SW], ctx=ctx)
        E = k.sb("Ep", [P, 2, SW], ctx=ctx)
        PT = k.sb("PTp", [P, 2, 14, P], ctx=ctx)
        mxp = k.sb("mxp", [P, 3, 2], ctx=ctx)
        mx3 = k.sb("mx3", [P, 3], ctx=ctx)
        nm = k.sb("nm", [P, 2, 3], ctx=ctx)
        ls = k.sb("ls", [P, 4, 3], ctx=ctx)
        rr = k.sb("rr", [P, 3], ctx=ctx)
        ob = k.sb("ob", [P, 3, HD], ctx=ctx)
        oA = k.sb("oA", [P, NTI, 4, G, HD], ctx=ctx)
        block = ctx.enter_context(nc.Block())

        @block.sync
        def _(sp):
            def load(i, g):
                h_off = (i + 4 * g) * NFWD
                src = bass.AP(k.biasfwd_d.tensor, h_off, [[1, P], [1, T]])
                sp.dma_start(strip[:, g, :], src).then_inc(s_strip[g], 16)

            load(0, 0)
            load(0, 1)
            sp.dma_start(k.kcT[:, :, :], k.kcT_d).then_inc(k.s_kcv, 16)
            sp.dma_start(k.vc[:, :, :, :], k.vc_d).then_inc(k.s_kcv, 16)
            with sp.Fori(1, 4) as i:
                for g in range(G):
                    sp.wait_ge(s_add, i * NU + (NTI * (g + 1) - NU + 1))
                    load(i, g)

        @block.gpsimd
        def _(pool):
            def prepare(i, g):
                half = slice(HD * g, HD * g + HD)
                if i:
                    pool.wait_ge(s_sc, i * NU + (NTI * (g + 1) - NU))
                if i or g:
                    pool.wait_ge(s_wf, i * G + g)
                if i:
                    pool.tensor_copy(qh[half, :], k.qT[half, i, 0:T]).then_inc(s_q, 1)
                pool.wait_ge(s_q, i * G + (g + 1))
                pool.wait_ge(s_strip[g], i * 16 + 16)
                pool.affine_select(out=wf[:, g, :], in_=strip[:, g, 5 * P - 1:4 * P - 1:-1], compare_op=ALU.is_ge, fill=NEG,
                                   base=-1, pattern=[[1, P]], channel_multiplier=-1).then_inc(s_wf, 1)

            for i in range(4):
                prepare(i, 0)
                prepare(i, 1)

        @block.tensor
        def _(pe):
            def scores(i, u):
                g, ti = units[u]
                half = slice(HD * g, HD * g + HD)
                q = qh[half, P * ti:P * ti + P]
                if ti == 0:
                    pe.wait_ge(s_q, i * G + (g + 1))
                pe.wait_ge(s_add, i * NU + (u + 1))
                n = P * (ti + 1)
                for a in range(0, n, 512):
                    pe.matmul(k.bank[a // 512][:, 0:min(512, n - a)], q, k.ksT[half, a:min(a + 512, n)], start=True, stop=True)
                if ti >= 4:
                    pe.matmul(k.bank[2][:, 0:P], q, k.kwT[half, P * (ti - 4):P * (ti - 3)], start=True, stop=True)
                lo = P * max(ti - 3, 0)
                pe.matmul(k.bank[3][:, 0:n - lo], q, k.kwT[half, lo:n], start=True, stop=True)
                nn = min(8 * ti + 7, NCP)
                pe.matmul(k.bank[2][:, P:P + nn], q, k.kcpT[half, 0:nn], start=True, stop=True).then_inc(s_sc, 1)

            def turn(i, u):
                g, ti = units[u]
                tiles = [t for x in ptiles(ti) for t in x]
                pe.wait_ge(s_exp, i * NU + (u + 2))
                for n, (uu, a, w, m) in enumerate(fills):
                    if uu != u:
                        continue
                    if m == 3:
                        pe.wait_ge(s_pta, i * NFA + (copied(n - 2, 0) + 1))
                    elif m == 0:
                        pe.wait_ge(s_pta, i * NFA + (copied(n, 0) + 1))
                        pe.wait_ge(s_ptd, i * NFD + (copied(n, 1) + 1))
                    for q in range(w):
                        col, kk = tiles[a + q]
                        mm = pe.transpose(k.bank[4 + m % 3][0:kk, P * q:P * q + P], E[:, u % 2, col:col + kk], k.ident[:, :])
                    mm.then_inc(s_T, 1)

            def products(i, u):
                g, ti = units[u]
                n = max(m for m, f in enumerate(fills) if f[0] == u) + 1
                pe.wait_ge(s_pta, i * NFA + (copied(n, 0) + 1))
                pe.wait_ge(s_ptd, i * NFD + (copied(n, 1) + 1))
                pe.wait_ge(s_o, i * NU + (u + 1))
                t = 0
                for br, tl in enumerate(ptiles(ti)):
                    for m in range(len(tl)):
                        if br == 0:
                            v = k.kv[:, m, 384 + HD * g:384 + HD * g + HD]
                        elif br == 1:
                            v = k.kv[:, ti + 1 - len(tl) + m, 640 + HD * g:640 + HD * g + HD]
                        else:
                            v = k.vcp[0:tl[0][1], HD * g:HD * g + HD]
                        mm = pe.matmul(k.bank[7][:, HD * GATE[br]:HD * GATE[br] + HD], PT[0:tl[m][1], u % 2, t, :], v,
                                       start=(m == 0), stop=(m == len(tl) - 1))
                        t += 1
                mm.then_inc(s_pv, 1)

            with pe.Fori(0, 4) as i:
                scores(i, 0)
                for u in range(NU):
                    if u + 1 < NU:
                        scores(i, u + 1)
                    turn(i, u)
                    if u:
                        products(i, u - 1)
                products(i, NU - 1)
            pe.wait_ge(s_o, 4 * NU + 1)
            for ti in range(NTI):
                if ti >= 4:
                    pe.wait_ge(s_oTs, ti - 3)
                for j in range(4):
                    mm = pe.transpose(k.bank[ti % 4][:, P * j:P * j + P], oA[:, ti, j].rearrange("p g d -> p (g d)"), k.ident[:, :])
                mm.then_inc(s_oT, 1)

        def copies(eng, i, u, odd, sem):
            for n, (uu, a, w, m) in enumerate(fills):
                if uu != u or m % 2 != odd:
                    continue
                g, ti = units[u]
                eng.wait_ge(s_T, i * len(fills) + (n + 2))
                if m < 2:
                    eng.wait_ge(s_pv, i * NU + (max(u - 1, 0) + 1))
                tiles = [t for x in ptiles(ti) for t in x]
                full = [x for x in tiles[a:a + w] if x[1] == P]
                parts = []
                if full:
                    parts.append((PT[:, u % 2, a:a + len(full), :], k.bank[4 + m % 3][:, 0:P * len(full)].rearrange("p (q t) -> p q t", t=P)))
                if len(full) < w:
                    kk = tiles[a + w - 1][1]
                    parts.append((PT[0:kk, u % 2, a + w - 1, :], k.bank[4 + m % 3][0:kk, P * (w - 1):P * w]))
                for dst, src in parts:
                    ins = eng.tensor_copy(dst, src) if odd else eng.activation(dst, src, ACT.Copy)
                ins.then_inc(sem, 1)

        @block.vector
        def _(dve):
            ch = Chain(dve, s_ch)
            PER = 6 * NU

            def addmax(i, u):
                g, ti = units[u]
                if ti == 0:
                    dve.wait_ge(s_strip[g], i * 16 + 16)
                    dve.wait_ge(s_wf, i * G + (g + 1))
                if u >= 2:
                    dve.wait_ge(s_exp, i * NU + u)
                else:
                    dve.wait_ge(s_exp, i * NU + 1)
                dve.wait_ge(s_sc, i * NU + (u + 1))
                nn = min(8 * ti + 7, NCP)
                dve.tensor_tensor(S[:, u % 2, COFF:COFF + nn], k.bank[2][:, P:P + nn], strip[:, g, P * ti + 96:(P * ti + 96 - STRIDE * nn if P * ti + 96 >= STRIDE * nn else None):-STRIDE],
                                  ALU.add).then_inc(s_mz, 1)
                n = P * (ti + 1)
                parts = []
                x0 = P * ti + P - 1
                for a in range(0, n, 512):
                    w = min(512, n - a)
                    lo = x0 - a - w
                    parts.append((0, a // 512, a, w, a // 512, 0, strip[:, g, x0 - a:lo if lo >= 0 else None:-1]))
                lo = P * max(ti - 3, 0)
                w = n - lo
                parts.append((1, 0, WOFF + 5 * P - w, w, 3, 0, strip[:, g, w - 1::-1]))
                if ti >= 4:
                    parts.append((1, 1, WOFF, P, 2, 0, wf[:, g, :]))
                for m, (br, sl, col, w, bank, bc, bias) in enumerate(parts):
                    dve.tensor_tensor_reduce(S[:, u % 2, col:col + w], k.bank[bank][:, bc:bc + w], bias, 1.0, NEG,
                                             ALU.add, ALU.max, mxp[:, br, sl:sl + 1]).then_inc(s_add if m == len(parts) - 1 else s_mz, 1)

            mz = [sum(4 if t >= 4 else 2 for _, t in units[:u + 1]) for u in range(NU)]

            def bounds(i, u):
                g, ti = units[u]
                dve.wait_ge(s_mz, i * mz[-1] + (mz[u] + 1))
                dve.wait_ge(s_add, i * NU + (u + 2))
                ch.step(dve.tensor_reduce(mx3[:, 0:2], mxp[:, 0:2, 0:2 if ti >= 4 else 1], AX.X, ALU.max))
                ch.link(dve.tensor_reduce(mx3[:, 2:3], S[:, u % 2, COFF:COFF + min(8 * ti + 7, NCP)], AX.X, ALU.max))
                dve.tensor_scalar(nm[:, u % 2, :], mx3[:, :], FLOOR, -1.0, ALU.max, ALU.mult).then_inc(s_nm, 1)

            def output(i, u):
                g, ti = units[u]
                ch.link(dve.tensor_scalar(rr[:, :], ls[:, u % 4, :], 1e-30, None, ALU.max))
                ch.link(dve.reciprocal(rr[:, :], rr[:, :]))
                ch.link(dve.tensor_tensor(rr[:, :], rr[:, :], k.small[:, ti, bass.ds(i * 3 + 12 * g, 3)], ALU.mult))
                dve.wait_ge(s_pv, i * NU + (u + 2))
                ch.link(dve.tensor_tensor(ob[:, :, :], k.bank[7][:, 0:3 * HD].rearrange("p (b d) -> p b d", b=3),
                                          rr[:, :].unsqueeze(2).to_broadcast([P, 3, HD]), ALU.mult))
                dve.tensor_reduce(oA[:, ti, bass.ds(i, 1), g, :].rearrange("p o d -> p (o d)"), ob[:, :, :].rearrange("p b d -> p d b"),
                                  AX.X, ALU.add).then_inc(s_o, 1)
                dve.wait_ge(s_o, i * NU + (u + 2))

            dve.memset(mxp[:, :, :], NEG).then_inc(s_mz, 1)
            dve.wait_ge(s_mz, 1)
            with dve.Fori(0, 4) as i:
                ch.start(i, 6 * NU)
                addmax(i, 0)
                bounds(i, 0)
                for u in range(NU):
                    if u + 1 < NU:
                        addmax(i, u + 1)
                        bounds(i, u + 1)
                    copies(dve, i, u, 1, s_ptd)
                    if u:
                        output(i, u - 1)
                output(i, NU - 1)
                ch.done()
            for ti in range(NTI):
                dve.wait_ge(s_oT, ti + 1)
                dve.tensor_copy(k.oaT[:, :, P * ti:P * ti + P], k.bank[ti % 4][:, :].rearrange("p (j t) -> p j t", j=4)).then_inc(s_oTs, 1)

        @block.scalar
        def _(act):
            def exps(i, u):
                g, ti = units[u]
                act.wait_ge(s_nm, i * NU + (u + 1))
                act.wait_ge(s_T, i * len(fills) + (sum(1 for f in fills if f[0] < u - 1) + 1))
                act.wait_ge(s_o, i * NU + (max(u - 3, 0) + 1))
                nn = min(8 * ti + 7, NCP)
                nw = P * min(ti + 1, 5)
                for br, (col, w) in enumerate(((0, P * (ti + 1)), (WOFF + 5 * P - nw, nw), (COFF, nn))):
                    ins = act.activation(E[:, u % 2, col:col + w], S[:, u % 2, col:col + w], ACT.Exp,
                                         bias=nm[:, u % 2, br:br + 1], accum_out=ls[:, u % 4, GATE[br]:GATE[br] + 1])
                ins.then_inc(s_exp, 1)

            for g in range(G):
                half = slice(HD * g, HD * g + HD)
                act.activation(qh[half, :], k.qT[half, 0, 0:T], ACT.Copy).then_inc(s_q, 1)
            with act.Fori(0, 4) as i:
                exps(i, 0)
                for u in range(NU):
                    copies(act, i, u, 0, s_pta)
                    if u + 1 < NU:
                        exps(i, u + 1)


def decode_attention(k):
    nc = k.nc
    BG = B * G
    NSELK = TOPN * SEL
    s_q0, s_qp, s_win, s_pt, s_gt = (k.sem(f"s_da_{x}") for x in ("q0", "qp", "win", "pt", "gt"))
    s_new = [k.sem(f"s_da_new{j}") for j in range(2)]
    s_const, s_kT, s_kTs, s_sc, s_ch = (k.sem(f"s_da_{x}") for x in ("const", "kT", "kTs", "sc", "ch"))
    s_exp, s_imp, s_tb, s_idx, s_bidx, s_bg, s_rows = (k.sem(f"s_da_{x}") for x in ("exp", "imp", "tb", "idx", "bidx", "bg", "rows"))
    s_ga = [k.sem(f"s_da_ga{j}") for j in range(2)]
    s_sT, s_sTs, s_vs, s_ssc, s_pT, s_pTs, s_o, s_od = (k.sem(f"s_da_{x}") for x in ("sT", "sTs", "vs", "ssc", "pT", "pTs", "o", "od"))
    s_sig, s_kcv, kcT, vc = k.sem("s_da_sig"), k.s_kcv, k.kcT, k.vc
    rows = k.i["cache_nsa_kv"][0].rearrange("q t (s v) g d -> (q t s) (v g d)", s=2)
    brow = k.biasrev_d.rearrange("h (n r) -> (h n) r", r=SEL)
    NBR = NREV // SEL
    with ExitStack() as ctx:
        qp = k.sb("qpad", [P, 8 * 72], ctx=ctx)
        win = k.sb("dwin", [P, B, 4, 256], ctx=ctx)
        wT = k.sb("dwT", [P, 2, WIN], ctx=ctx)
        S = k.sb("dS", [64, 2 * 512 + NSELK], ctx=ctx)
        mx = k.sb("dmx", [64, 4], ctx=ctx)
        nm = k.sb("dnm", [64, 4], ctx=ctx)
        ls = k.sb("dls", [64, 4], ctx=ctx)
        gt = k.sb("dgt", [64, 3], ctx=ctx)
        gsel = k.sb("gsel", [64, BG], ctx=ctx)
        gselT = k.sb("gselT", [BG, 64], ctx=ctx)
        iota = k.sb("diota", [BG, P], ctx=ctx)
        coli = k.sb("dcoli", [P, 1], I32, ctx=ctx)
        colf = k.sb("dcolf", [P, 1], ctx=ctx)
        hrow = k.sb("dhrow", [64, 1], ctx=ctx)
        prow = k.sb("dprow", [P, 1], ctx=ctx)
        iti = k.sb("diti", [P, P], I32, ctx=ctx)
        pti = k.sb("dpti", [BG, NPAGES], I32, ctx=ctx)
        tokb = k.sb("dtokb", [BG, NPAGES, 2], ctx=ctx)
        imp = k.sb("dimp", [BG, P], ctx=ctx)
        imp2 = k.sb("dimp2", [BG, P], ctx=ctx)
        v8 = k.sb("dv8", [BG, TOPN], ctx=ctx)
        ix = k.sb("dix", [BG, TOPN], U32, ctx=ctx)
        ixf = k.sb("dixf", [BG, TOPN], ctx=ctx)
        tb = k.sb("dtb", [BG, TOPN], ctx=ctx)
        hit = k.sb("dhit", [BG, 2, P], ctx=ctx)
        tbd = k.sb("dtbd", [BG, BG, TOPN], ctx=ctx)
        gidx = k.sb("dgidx", [P, BG, 8], U32, ctx=ctx)
        bidx = k.sb("dbidx", [64, TOPN], U32, ctx=ctx)
        bsel = k.sb("dbsel", [64, NSELK], ctx=ctx)
        kvs = k.sb("dkvs", [P, 2, 8, 256], ctx=ctx)
        sT = k.sb("dsT", [P, 2, NSELK], ctx=ctx)
        vsel = k.sb("dvsel", [P, BG, 8, HD], ctx=ctx)
        pT = k.sb("dpT", [P, 16, 64], ctx=ctx)
        block = ctx.enter_context(nc.Block())

        @block.sync
        def _(sp):
            for b in range(B):
                sp.dma_start(win[:, b], k.o["win_sample"][0, b].rearrange("(c p) v g d -> p c (v g d)", p=P)).then_inc(s_win, 16)
            for bg in range(BG):
                sp.dma_start(pti[bg:bg + 1, :], k.i["page_table"][bg // G:bg // G + 1, :]).then_inc(s_pt, 16)
            for b in range(B):
                sp.dma_start(gt[8 * b:8 * b + 8, :], k.smalltok_d[b, 0:24].rearrange("(h r) -> h r", r=3)).then_inc(s_gt, 16)
            new = k.o["kv_sample"][0].rearrange("b o v g d -> b (o v g d)")
            for bg in range(BG):
                sp.wait_ge(s_ga[bg % 2], 128 * (bg // 2 + 1))
                sp.dma_start(kvs[64:65, bg % 2, 7, :], new[bg // 2:bg // 2 + 1, 256:512]).then_inc(s_new[bg % 2], 16)
            for j in range(2):
                sp.wait_ge(s_new[j], 8 * BG)

        @block.gpsimd
        def _(pool):
            pool.memset(qp[:, :], 0.0).then_inc(s_q0, 1)
            pool.memset(gsel[:, :], 1.0).then_inc(s_const, 1)
            pool.memset(gselT[:, :], 1.0).then_inc(s_const, 1)
            pool.iota(iti[:, :], pattern=[[1, P]], base=0, channel_multiplier=0).then_inc(s_const, 1)
            pool.iota(coli[:, :], pattern=[[0, 1]], base=0, channel_multiplier=1).then_inc(s_const, 1)
            pool.wait_ge(s_const, 4)
            pool.affine_select(out=gsel[:, :], in_=gsel[:, :], compare_op=ALU.is_ge, fill=0.0, base=0,
                               pattern=[[-4, BG]], channel_multiplier=1).then_inc(s_const, 1)
            pool.affine_select(out=gselT[:, :], in_=gselT[:, :], compare_op=ALU.is_ge, fill=0.0, base=0,
                               pattern=[[1, 64]], channel_multiplier=-4).then_inc(s_const, 1)
            pool.wait_ge(s_const, 6)
            pool.affine_select(out=gsel[:, :], in_=gsel[:, :], compare_op=ALU.is_ge, fill=0.0, base=3,
                               pattern=[[4, BG]], channel_multiplier=-1).then_inc(s_const, 1)
            pool.affine_select(out=gselT[:, :], in_=gselT[:, :], compare_op=ALU.is_ge, fill=0.0, base=3,
                               pattern=[[-1, 64]], channel_multiplier=4).then_inc(s_const, 1)
            pool.wait_ge(s_bidx, 1)
            for n in range(TOPN):
                pool.indirect_dma_start(out=bsel[:, SEL * n:SEL * n + SEL], out_offset=None, in_=brow,
                                        in_offset=bass.IndirectOffsetOnAxis(ap=bidx[:, n:n + 1], axis=0)).then_inc(s_bg, 16)
            pool.wait_ge(s_idx, 2)
            for bg in range(BG):
                if bg >= 2:
                    pool.wait_ge(s_sT, 2 * (bg - 1))
                    pool.wait_ge(s_vs, bg - 1)
                for m in range(8):
                    pool.indirect_dma_start(out=kvs[:, bg % 2, m, :], out_offset=None, in_=rows,
                                            in_offset=bass.IndirectOffsetOnAxis(ap=gidx[:, bg, m:m + 1], axis=0)).then_inc(s_ga[bg % 2], 16)

        @block.vector
        def _(dve):
            ch = Chain(dve, s_ch)
            dve.wait_ge(s_q0, 1)
            for g in range(G):
                half = slice(HD * g, HD * g + HD)
                dve.tensor_copy(qp[half, :].rearrange("p (b x) -> p b x", x=72)[:, :, 4 * g:4 * g + 4],
                                k.qTs[half, :, :].rearrange("p j b -> p b j")).then_inc(s_qp, 1)
            for b in range(B):
                dve.wait_ge(s_kT, b + 1)
                if b >= 2:
                    dve.wait_ge(s_sc, b - 1 + 1)
                dve.tensor_copy(wT[:, b % 2, :], k.bank[2 + b % 2][:, :]).then_inc(s_kTs, 1)
            dve.wait_ge(s_sc, 1)
            ch.link(dve.tensor_tensor_reduce(S[:, 0:512], k.bank[0][0:64, :], k.bias_cmp[:, :], 1.0, NEG, ALU.add, ALU.max, mx[:, 0:1]))
            ch.link(dve.tensor_scalar(nm[:, 0:1], mx[:, 0:1], FLOOR, -1.0, ALU.max, ALU.mult))
            dve.wait_ge(s_exp, 1)
            ch.link(dve.tensor_scalar(mx[:, 0:1], ls[:, 0:1], 1e-30, None, ALU.max))
            ch.link(dve.reciprocal(mx[:, 0:1], mx[:, 0:1]))
            ch.link(dve.tensor_scalar(S[:, 0:512], S[:, 0:512], mx[:, 0:1], None, ALU.mult))
            dve.wait_ge(s_imp, 1)
            ch.link(dve.tensor_reduce(imp[:, :], k.bank[4][0:BG, :].rearrange("p (j r) -> p j r", r=4), AX.X, ALU.add))
            ch.link(dve.tensor_tensor(imp[:, 1:P], imp[:, 1:P], k.bank[4][0:BG, 3:3 + 4 * (P - 1):4], ALU.add))
            ch.link(dve.memset(imp[:, 0:1], 1e9))
            ch.link(dve.memset(imp[:, P - 1:P], 1e9))
            ch.link(dve.max(v8[:, 0:8], imp[:, :]))
            ch.link(dve.max_index(ix[:, 0:8], v8[:, 0:8], imp[:, :]))
            ch.link(dve.match_replace(imp2[:, :], v8[:, 0:8], imp[:, :], NEG))
            ch.link(dve.max(v8[:, 8:16], imp2[:, :]))
            ch.link(dve.max_index(ix[:, 8:16], v8[:, 8:16], imp2[:, :]))
            ch.link(dve.tensor_copy(ixf[:, :], ix[:, :]))
            dve.wait_ge(s_const, 8)
            ch.link(dve.tensor_copy(iota[:, :], iti[0:BG, :]))
            dve.wait_ge(s_pt, 16 * BG)
            for r in range(2):
                ch.link(dve.tensor_scalar(tokb[:, :, r], pti[:, :], 2.0 * PAGE, 2.0 * SEL * r, ALU.mult, ALU.add))
            for n in range(TOPN):
                if n >= 2:
                    dve.wait_ge(s_tb, n - 1)
                dve.scalar_tensor_tensor(out=hit[:, n % 2, :], in0=iota[:, :], scalar=ixf[:, n:n + 1],
                                         in1=tokb[:, :, :].rearrange("p a r -> p (a r)"), op0=ALU.is_equal, op1=ALU.mult).then_inc(s_rows, 1)
                dve.wait_ge(s_rows, n + 1)
                dve.tensor_reduce(tb[:, n:n + 1], hit[:, n % 2, :], AX.X, ALU.add).then_inc(s_tb, 1)
            dve.wait_ge(s_tb, TOPN)
            ch.link(dve.tensor_tensor(tbd[:, :, :], k.ident[0:BG, 0:BG].unsqueeze(2).to_broadcast([BG, BG, TOPN]),
                                      tb[:, :].unsqueeze(1).to_broadcast([BG, BG, TOPN]), ALU.mult))
            ch.link(dve.memset(ixf[:, TOPN - 1:TOPN], float(PAST // SEL)))
            ch.link(dve.tensor_copy(colf[:, :], coli[:, :]))
            ch.link(dve.tensor_scalar(hrow[:, :], colf[0:64, :], float(NBR), None, ALU.mult))
            ch.link(dve.tensor_scalar(prow[:, :], colf[:, :], 2.0, 1.0, ALU.mult, ALU.add))
            ch.link(dve.tensor_scalar(prow[64:P, :], prow[64:P, :], -2.0 * SEL, None, ALU.add))
            dve.wait_ge(s_imp, 2)
            dve.tensor_scalar(bidx[:, :], k.bank[5][0:64, 0:TOPN], hrow[:, :], None, ALU.add).then_inc(s_bidx, 1)
            dve.wait_ge(s_imp, 3)
            for r in range(2):
                half = slice(64 * r, 64 * r + 64)
                dve.tensor_scalar(gidx[half, :, :], k.bank[6][half, 0:BG * TOPN].rearrange("p (n m r) -> p n m r", m=8, r=2)[:, :, :, r],
                                  prow[half, :], None, ALU.add).then_inc(s_idx, 1)
            dve.wait_ge(s_sc, 1 + B)
            ch.link(dve.tensor_tensor_reduce(S[:, 512:1024], k.bank[1][0:64, :], k.bias_win[:, :], 1.0, NEG, ALU.add, ALU.max, mx[:, 1:2]))
            ch.link(dve.tensor_scalar(nm[:, 1:2], mx[:, 1:2], FLOOR, -1.0, ALU.max, ALU.mult))
            for bg in range(BG):
                g = bg % 2
                half = slice(HD * g, HD * g + HD)
                for a in range(2):
                    dve.wait_ge(s_sT, 2 * bg + a + 1)
                    if a == 0 and bg >= 2:
                        dve.wait_ge(s_ssc, bg - 1)
                    dve.tensor_copy(sT[half, bg % 2, 512 * a:512 * a + 512], k.bank[2 + a][half, :]).then_inc(s_sTs, 1)
            dve.wait_ge(s_ssc, BG)
            dve.wait_ge(s_bg, 16 * TOPN)
            for a in range(2):
                ch.link(dve.tensor_tensor_reduce(S[:, 1024 + 512 * a:1536 + 512 * a], k.bank[5 + a][0:64, :],
                                                 bsel[:, 512 * a:512 * a + 512], 1.0, NEG, ALU.add, ALU.max, mx[:, 2 + a:3 + a]))
            ch.link(dve.tensor_tensor(mx[:, 2:3], mx[:, 2:3], mx[:, 3:4], ALU.max))
            ch.link(dve.tensor_scalar(nm[:, 2:3], mx[:, 2:3], FLOOR, -1.0, ALU.max, ALU.mult))
            dve.wait_ge(s_exp, 3)
            dve.wait_ge(s_sig, 1)
            ch.link(dve.tensor_scalar(ls[:, 1:3], ls[:, 1:3], 1e-30, None, ALU.max))
            ch.link(dve.reciprocal(ls[:, 1:3], ls[:, 1:3]))
            ch.link(dve.memset(ls[:, 0:1], 1.0))
            ch.link(dve.tensor_tensor(mx[:, 0:1], gt[:, 0:1], ls[:, 0:1], ALU.mult))
            ch.link(dve.tensor_tensor(mx[:, 1:2], gt[:, 2:3], ls[:, 1:2], ALU.mult))
            ch.link(dve.tensor_tensor(mx[:, 2:3], gt[:, 1:2], ls[:, 2:3], ALU.mult))
            dve.wait_ge(s_imp, 3)
            ch.link(dve.tensor_scalar(S[:, 0:512], S[:, 0:512], mx[:, 0:1], None, ALU.mult))
            ch.link(dve.tensor_scalar(S[:, 512:1024], S[:, 512:1024], mx[:, 1:2], None, ALU.mult))
            ch.link(dve.tensor_scalar(S[:, 1024:2048], S[:, 1024:2048], mx[:, 2:3], None, ALU.mult))
            for a in range(2):
                dve.wait_ge(s_pT, a + 1)
                dve.tensor_copy(pT[:, 8 * a:8 * a + 8, :], k.bank[2 + a][:, :].rearrange("p (t r) -> p t r", t=8)).then_inc(s_pTs, 1)
            dve.wait_ge(s_o, 1)
            dve.tensor_copy(k.oaT[:, :, T:TT], k.bank[0][:, 0:32].rearrange("p (b j) -> p j b", j=4)).then_inc(s_od, 1)

        @block.scalar
        def _(act):
            act.wait_ge(s_gt, 16 * B)
            act.activation(gt[:, :], gt[:, :], ACT.Sigmoid).then_inc(s_sig, 1)
            act.wait_ge(s_ch, 2)
            act.activation(S[:, 0:512], S[:, 0:512], ACT.Exp, bias=nm[:, 0:1], accum_out=ls[:, 0:1]).then_inc(s_exp, 1)
            act.wait_ge(s_ch, 26)
            act.activation(S[:, 512:1024], S[:, 512:1024], ACT.Exp, bias=nm[:, 1:2], accum_out=ls[:, 1:2]).then_inc(s_exp, 1)
            for bg in range(BG):
                g = bg % 2
                act.wait_ge(s_new[bg % 2], 16 * (bg // 2 + 1))
                act.activation(vsel[:, bg], kvs[:, bg % 2, :, P + HD * g:P + HD * g + HD], ACT.Copy).then_inc(s_vs, 1)
            act.wait_ge(s_ch, 30)
            act.activation(S[:, 1024:2048], S[:, 1024:2048], ACT.Exp, bias=nm[:, 2:3], accum_out=ls[:, 2:3]).then_inc(s_exp, 1)

        @block.tensor
        def _(pe):
            pe.wait_ge(s_qp, 2)
            pe.wait_ge(s_kcv, 32)
            for b in range(B):
                mm = pe.matmul(k.bank[0][0:64, :], qp[:, 64 * b:64 * b + 64], kcT[:, b, :], start=(b == 0), stop=(b == B - 1))
            mm.then_inc(s_sc, 1)
            pe.wait_ge(s_win, 16 * B)

            def win_turn(b):
                if b >= 2:
                    pe.wait_ge(s_kTs, b - 1)
                for c in range(4):
                    mm = pe.transpose(k.bank[2 + b % 2][:, P * c:P * c + P], win[:, b, c, 0:P], k.ident[:, :])
                mm.then_inc(s_kT, 1)

            win_turn(0)
            for b in range(B):
                if b + 1 < B:
                    win_turn(b + 1)
                pe.wait_ge(s_kTs, b + 1)
                pe.matmul(k.bank[1][0:64, :], qp[:, 64 * b:64 * b + 64], wT[:, b % 2, :], start=(b == 0), stop=(b == B - 1)).then_inc(s_sc, 1)
            pe.wait_ge(s_const, 8)
            pe.wait_ge(s_ch, 5)
            pe.matmul(k.bank[4][0:BG, :], gsel[:, :], S[:, 0:512], start=True, stop=True).then_inc(s_imp, 1)
            pe.wait_ge(s_ch, 20)
            pe.matmul(k.bank[5][0:64, 0:TOPN], gselT[:, :], ixf[:, :], start=True, stop=True).then_inc(s_imp, 1)
            pe.matmul(k.bank[6][:, 0:BG * TOPN], k.ones[0:BG, :], tbd[:, :, :].rearrange("p n m -> p (n m)"), start=True, stop=True).then_inc(s_imp, 1)
            pe.wait_ge(s_idx, 2)
            pe.wait_ge(s_bidx, 1)

            def sel_turn(bg):
                pe.wait_ge(s_new[bg % 2], 16 * (bg // 2 + 1))
                pe.wait_ge(s_sTs, 2 * bg)
                for a in range(2):
                    for q in range(4):
                        mm = pe.transpose(k.bank[2 + a][:, P * q:P * q + P], kvs[:, bg % 2, 4 * a + q, 0:P], k.ident[:, :])
                    mm.then_inc(s_sT, 1)

            def sel_scores(bg):
                b, g = bg // 2, bg % 2
                half = slice(HD * g, HD * g + HD)
                pe.wait_ge(s_sTs, 2 * bg + 2)
                if bg:
                    pe.wait_ge(s_ssc, bg)
                for a in range(2):
                    mm = pe.matmul(k.bank[5 + a][0:64, :], qp[half, 64 * b:64 * b + 64], sT[half, bg % 2, 512 * a:512 * a + 512],
                                   start=(bg == 0), stop=(bg == BG - 1), skip_group_check=True)
                mm.then_inc(s_ssc, 1)

            for bg in range(BG):
                sel_turn(bg)
                if bg:
                    sel_scores(bg - 1)
            sel_scores(BG - 1)
            pe.wait_ge(s_ch, 39)
            for a in range(2):
                for q in range(8):
                    t = 8 * a + q
                    mm = pe.transpose(k.bank[2 + a][:, 64 * q:64 * q + 64], S[:, P * t:P * t + P], k.ident[0:64, 0:64])
                mm.then_inc(s_pT, 1)
            pe.wait_ge(s_pTs, 2)
            pe.wait_ge(s_vs, BG)
            for g in range(G):
                for b in range(B):
                    bg = G * b + g
                    col = slice(8 * b + 4 * g, 8 * b + 4 * g + 4)
                    vals = ([(vc[:, b, t, HD * g:HD * g + HD], t) for t in range(4)]
                            + [(win[:, b, c, P + HD * g:P + HD * g + HD], 4 + c) for c in range(4)]
                            + [(vsel[:, bg, m, :], 8 + m) for m in range(8)])
                    for n, (v, t) in enumerate(vals):
                        mm = pe.matmul(k.bank[0][HD * g:HD * g + HD, 4 * b:4 * b + 4], v, pT[:, t, col], start=(n == 0), stop=(n == 15))
            mm.then_inc(s_o, 1)


def add_gated(k, dve, xT, c, g, bank, gate, tmp, sem_x, sem_t, n_t):
    w = GT if g < NG - 1 else T - GT * (NG - 1)
    cs = c if isinstance(c, slice) else bass.ds(c, 1)
    if w < GT:
        dve.wait_ge(sem_t, n_t)
        dve.tensor_tensor(tmp[:, :], bank[:, w:GT], k.modT[:, bass.ds(gate + c, 1), 1:9].rearrange("p o b -> p (o b)"), ALU.mult).then_inc(sem_t, 1)
        dve.wait_ge(sem_t, n_t + 1)
        dve.tensor_tensor(xT[:, cs, T:TT].rearrange("p o b -> p (o b)"), xT[:, cs, T:TT].rearrange("p o b -> p (o b)"), tmp[:, :], ALU.add).then_inc(sem_t, 1)
    x = xT[:, cs, GT * g:GT * g + w].rearrange("p o t -> p (o t)")
    dve.scalar_tensor_tensor(out=x, in0=bank[:, 0:w], scalar=k.modT[:, bass.ds(gate + c, 1), 0:1].rearrange("p o b -> p (o b)"),
                             in1=x, op0=ALU.mult, op1=ALU.add).then_inc(sem_x, 1)


def mm3(pe, out, a, b, start, stop):
    for n, (x, y) in enumerate(((0, 0), (0, 1), (1, 0))):
        mm = pe.matmul(out, a[x], b[y], start=start and n == 0, stop=stop and n == 2)
    return mm


def merge(k, mixT):
    nc = k.nc
    w_v = k.i["w_in"][0].rearrange("(k p) n -> p k n", p=P)
    wa_v = k.i["w_branch_a"][0].rearrange("(g j d) n -> g d j n", g=G, j=4)
    wb_v = k.i["w_branch_b"][0].rearrange("(k p) n -> p k n", p=P)
    s_uh, s_ul, s_wh, s_wl = (k.sem(f"s_g_{x}") for x in ("uh", "ul", "wh", "wl"))
    s_ux = [k.sem(f"s_g_ux{g}") for g in range(NG)]
    s_wg, s_wb = [k.sem(f"s_g_wg{j}") for j in range(2)], [k.sem(f"s_g_wb{j}") for j in range(2)]
    s_mf, s_sig, s_t = (k.sem(f"s_g_{x}") for x in ("mf", "sig", "t"))
    s_mix = k.sem("s_g_mix", start=2)
    with ExitStack() as ctx:
        uT = k.sb("guT", [P, DK, TT], ctx=ctx)
        uH = k.sb("guH", [P, DK, TT], F32R, ctx=ctx)
        uL = uT[:, :, :].bitcast(F32R)
        wg = k.sb("gwg", [P, 2, DK, P], ctx=ctx)
        wgH = k.sb("gwgH", [P, 2, 2, DK, P], F32R, ctx=ctx)
        wgL = k.sb("gwgL", [P, 2, 2, DK, P], F32R, ctx=ctx)
        wb = k.sb("gwb", [P, 2, 2, 4, P], ctx=ctx)
        sig = k.sb("gsig", [P, 2, 2, GT], ctx=ctx)
        tt = k.sb("gtt", [P, 2, 2, GT], ctx=ctx)
        block = ctx.enter_context(nc.Block())

        @block.sync
        def _(sp):
            def load_blocks(e, cols, first=False):
                for br in range(2):
                    if not first:
                        sp.wait_ge(s_wl, e * 2 + (br - 1))
                    sp.dma_start(wg[:, br], w_v[:, :, cols[br]]).then_inc(s_wg[br], 16)

            def load_branches(c, j):
                for g in range(G):
                    sp.dma_start(wb[HD * g:HD * g + HD, j, 0], wa_v[g, :, :, bass.ds(c * P, P)]).then_inc(s_wb[j], 16)
                sp.dma_start(wb[:, j, 1], wb_v[:, :, bass.ds(c * P, P)]).then_inc(s_wb[j], 16)

            for e in range(2):
                load_blocks(e, [slice(OFF_OB + P * (2 * e + br), OFF_OB + P * (2 * e + br + 1)) for br in range(2)], e == 0)
                if e == 0:
                    for g in range(NG):
                        sp.dma_start(uT[:, :, GT * g:GT * g + GT], k.uT_d[:, :, GT * g:GT * g + GT]).then_inc(s_ux[g], 16)
                load_branches(e, e)
            def gates(i, j):
                load_blocks(i * 2 + (2 + j), [bass.ds(i * (2 * P) + (OFF_MG + D * br + P * j), P) for br in range(2)])

            gates(0, 0)
            gates(0, 1)
            with sp.Fori(1, 4) as i:
                for j in range(2):
                    gates(i, j)
                    sp.wait_ge(s_mf, i * 6 + (3 * j + 3))
                    load_branches(i * 2 + j, j)

        @block.tensor
        def _(pe):
            def blocks(g, slot, first):
                t = slice(GT * g, GT * g + GT)
                for br in range(2):
                    for kk in range(DK):
                        mm = mm3(pe, k.bank[first + br][:, 0:GT], (wgH[:, slot, br, kk, :], wgL[:, slot, br, kk, :]),
                                 (uH[:, kk, t], uL[:, kk, t]), kk == 0, kk == DK - 1)
                return mm

            for u in range(6):
                e, g = u // NG, u % NG
                pe.wait_ge(s_wl, 2 * e + 2)
                pe.wait_ge(s_ul, DK * (g + 1))
                pe.wait_ge(s_mix, u + 1)
                blocks(g, e, 4 * (u % 2)).then_inc(s_mf, 1)
            with pe.Fori(0, 4) as i:
                for u in range(6):
                    j, g = u // NG, u % NG
                    b = 4 * (u % 2)
                    t = slice(GT * g, GT * g + GT)
                    if g == 0:
                        pe.wait_ge(s_wl, i * 4 + (4 + 2 * j + 2))
                        pe.wait_ge(s_wb[j], i * 48 + 48)
                    pe.wait_ge(s_mix, i * 6 + (6 + u + 1))
                    blocks(g, j, b)
                    if u == 0:
                        pe.wait_ge(s_mix, i * 6 + (6 + 2))
                    for br, src in ((0, k.oaT), (1, k.hbT)):
                        for kk in range(4):
                            mm = pe.matmul(k.bank[b + 2 + br][:, 0:GT], wb[:, j, br, kk, :], src[:, kk, t], start=(kk == 0), stop=(kk == 3))
                    mm.then_inc(s_mf, 1)

        @block.scalar
        def _(act):
            def round_block(e, slot, br):
                act.wait_ge(s_wg[br], e * 16 + 16)
                act.activation(wgH[:, slot, br], wg[:, br], ACT.Copy).then_inc(s_wh, 1)

            def unit(i, u, base, last=False):
                j, g = u // NG, u % NG
                act.wait_ge(s_mix, i * 6 + (base + u + 1))
                act.wait_ge(s_mf, i * 6 + (base + u + 1))
                for br in range(2):
                    act.activation(sig[:, u % 2, br, :], k.bank[4 * (u % 2) + br][:, 0:GT], ACT.Sigmoid).then_inc(s_sig, 1)
                if g < 2 and not (last and j == 1):
                    round_block(i * 2 + (base // 3 + j + 1), 1 - j, g)

            for br in range(2):
                round_block(0, 0, br)
            for g in range(NG):
                act.wait_ge(s_ux[g], 16)
                for c in range(DK):
                    act.activation(uH[:, c, GT * g:GT * g + GT], uT[:, c, GT * g:GT * g + GT], ACT.Copy).then_inc(s_uh, 1)
            for u in range(6):
                unit(0, u, 0)
            with act.Fori(0, 3) as i:
                for u in range(6):
                    unit(i, u, 6)
            for u in range(6):
                unit(3, u, 6, True)

        @block.vector
        def _(dve):
            def rest_block(e, slot, br):
                dve.wait_ge(s_wh, e * 2 + (br + 1))
                dve.tensor_tensor(wgL[:, slot, br], wg[:, br], wgH[:, slot, br], ALU.subtract).then_inc(s_wl, 1)

            def unit(i, u, last=False):
                j, g = u // NG, u % NG
                b = 4 * (u % 2)
                dve.wait_ge(s_sig, i * 12 + (12 + 2 * u + 2))
                dve.wait_ge(s_mix, i * 6 + (6 + u + 1))
                for br in range(2):
                    dve.tensor_tensor(tt[:, u % 2, br, :], k.bank[b + 2 + br][:, 0:GT], sig[:, u % 2, br, :], ALU.mult).then_inc(s_t, 1)
                dve.wait_ge(s_t, i * 12 + (2 * u + 2))
                dve.tensor_tensor(mixT[:, bass.ds(i * 2 + j, 1), GT * g:GT * g + GT].rearrange("p o t -> p (o t)"), tt[:, u % 2, 0, :], tt[:, u % 2, 1, :],
                                  ALU.add).then_inc(s_mix, 1)
                if g < 2 and not (last and j == 1):
                    rest_block(i * 2 + (3 + j), 1 - j, g)

            for br in range(2):
                rest_block(0, 0, br)
            for g in range(NG):
                for c in range(DK):
                    t = slice(GT * g, GT * g + GT)
                    dve.wait_ge(s_uh, DK * g + c + 1)
                    dve.tensor_tensor(uL[:, c, t], uT[:, c, t], uH[:, c, t], ALU.subtract).then_inc(s_ul, 1)
            for u in range(6):
                e, g = u // NG, u % NG
                dve.wait_ge(s_sig, 2 * u + 2)
                for br in range(2):
                    h = k.hbT[:, 2 * e + br, GT * g:GT * g + GT]
                    ins = dve.tensor_tensor(h, h, sig[:, u % 2, br, :], ALU.mult)
                ins.then_inc(s_mix, 1)
                if g < 2:
                    rest_block(e + 1, 1 - e, g)
            with dve.Fori(0, 3) as i:
                for u in range(6):
                    unit(i, u)
            for u in range(6):
                unit(3, u, True)


def mix_out(k, mixT):
    nc = k.nc
    wo_v = k.i["w_out"][0].rearrange("(k p) n -> p k n", p=P)
    s_xin, s_xst, s_mh, s_ml, s_wh, s_wl, s_rf, s_xs = (k.sem(f"s_o_{x}") for x in ("xin", "xst", "mh", "ml", "wh", "wl", "rf", "xs"))
    s_x = k.sem("s_o_x", start=4)
    s_wr = [k.sem(f"s_o_wr{j}") for j in range(2)]
    with ExitStack() as ctx:
        xT = k.sb("oxT", [P, DK, TT], ctx=ctx)
        mH = k.sb("omH", [P, DK, TT], F32R, ctx=ctx)
        mL = k.sb("omL", [P, DK, TT], F32R, ctx=ctx)
        wr = k.sb("owr", [P, 2, DK, P], ctx=ctx)
        wrH = k.sb("owrH", [P, 2, DK, P], F32R, ctx=ctx)
        wrL = k.sb("owrL", [P, 2, DK, P], F32R, ctx=ctx)
        tmp = k.sb("otmp", [P, B], ctx=ctx)
        block = ctx.enter_context(nc.Block())

        @block.sync
        def _(sp):
            for c in range(2):
                sp.dma_start(wr[:, c], wo_v[:, :, P * c:P * c + P]).then_inc(s_wr[c], 16)
            sp.dma_start(xT[:, :, :], k.xT_d).then_inc(s_xin, 16)
            for c in range(2, DK):
                sp.wait_ge(s_wl, c - 1)
                sp.dma_start(wr[:, c % 2], wo_v[:, :, P * c:P * c + P]).then_inc(s_wr[c % 2], 16)
            for c in range(DK):
                sp.wait_ge(s_x, 4 + NG * (c + 1))
                sp.wait_ge(s_xs, 2 * (c + 1))
                sp.dma_start(k.xT_d[:, c, :], xT[:, c, :]).then_inc(s_xst, 16)
            sp.wait_ge(s_xst, 16 * DK)

        @block.tensor
        def _(pe):
            for c in range(DK):
                pe.wait_ge(s_wl, c + 1)
                for g in range(NG):
                    t = slice(GT * g, GT * g + GT)
                    if c == 0:
                        pe.wait_ge(s_ml, DK * (g + 1))
                    pe.wait_ge(s_x, 3 * c + g - 1 if c >= 2 else 1)
                    for kk in range(DK):
                        mm = mm3(pe, k.bank[3 * (c % 2) + g][:, 0:GT], (wrH[:, c % 2, kk, :], wrL[:, c % 2, kk, :]),
                                 (mH[:, kk, t], mL[:, kk, t]), kk == 0, kk == DK - 1)
                    mm.then_inc(s_rf, 1)

        @block.scalar
        def _(act):
            def round_w(c):
                act.wait_ge(s_wr[c % 2], 16 * (c // 2 + 1))
                if c >= 2:
                    act.wait_ge(s_rf, NG * (c - 1))
                act.activation(wrH[:, c % 2], wr[:, c % 2], ACT.Copy).then_inc(s_wh, 1)

            round_w(0)
            for g in range(NG):
                for c in range(DK):
                    act.activation(mH[:, c, GT * g:GT * g + GT], mixT[:, c, GT * g:GT * g + GT], ACT.Copy).then_inc(s_mh, 1)
            for c in range(1, DK):
                round_w(c)

        @block.vector
        def _(dve):
            def rest_w(c):
                dve.wait_ge(s_wh, c + 1)
                dve.tensor_tensor(wrL[:, c % 2], wr[:, c % 2], wrH[:, c % 2], ALU.subtract).then_inc(s_wl, 1)

            rest_w(0)
            for g in range(NG):
                for c in range(DK):
                    t = slice(GT * g, GT * g + GT)
                    dve.wait_ge(s_mh, DK * g + c + 1)
                    dve.tensor_tensor(mL[:, c, t], mixT[:, c, t], mH[:, c, t], ALU.subtract).then_inc(s_ml, 1)
            rest_w(1)
            dve.wait_ge(s_xin, 16)
            for c in range(DK):
                for g in range(NG):
                    dve.wait_ge(s_rf, NG * c + g + 1)
                    add_gated(k, dve, xT, c, g, k.bank[3 * (c % 2) + g], 16, tmp, s_x, s_xs, 2 * c)
                if c + 2 < DK:
                    rest_w(c + 2)


def split(k, u, uH, uL):
    nc = k.nc
    s_h, s_l = k.sem("s_sp_h"), k.sem("s_sp_l")
    with nc.Block() as block:
        @block.scalar
        def _(act):
            for c in range(DK):
                act.activation(uH[:, c], u[:, c], ACT.Copy).then_inc(s_h, 1)

        @block.vector
        def _(dve):
            for c in range(DK):
                dve.wait_ge(s_h, c + 1)
                dve.tensor_tensor(uL[:, c], u[:, c], uH[:, c], ALU.subtract).then_inc(s_l, 1)
            dve.wait_ge(s_l, DK)


def ffn(k, xT, uH, uL):
    nc = k.nc
    FK = FF // P
    NS = FK // 2
    wi_v = k.i["w_ffn_in"][0].rearrange("(k p) n -> p k n", p=P)
    wo_v = k.i["w_ffn_out"][0].rearrange("(k p) n -> k p n", p=P)
    s_wi, s_wo = [k.sem(f"s_f_wi{j}") for j in range(2)], [k.sem(f"s_f_wo{j}") for j in range(2)]
    s_wh, s_wl, s_oh, s_ol = (k.sem(f"s_f_{x}") for x in ("wh", "wl", "oh", "ol"))
    s_hf, s_silu, s_hh, s_yf = (k.sem(f"s_f_{x}") for x in ("hf", "silu", "hh", "yf"))
    s_hm = k.sem("s_f_hm", start=2)
    s_hl, s_x, s_xs = (k.sem(f"s_f_{x}", start=1) for x in ("hl", "x", "xs"))
    with ExitStack() as ctx:
        hH = k.sb("fhH", [P, 2, TT], F32R, ctx=ctx)
        hL = k.sb("fhL", [P, 2, TT], F32R, ctx=ctx)
        wi = k.sb("fwi", [P, 2, DK, P], ctx=ctx)
        wiH = k.sb("fwiH", [P, 2, 2, DK, P], F32R, ctx=ctx)
        wiL = k.sb("fwiL", [P, 2, 2, DK, P], F32R, ctx=ctx)
        wo = k.sb("fwo", [P, 2, D], ctx=ctx)
        woH = k.sb("fwoH", [P, 2, D], F32R, ctx=ctx)
        woL = k.sb("fwoL", [P, 2, D], F32R, ctx=ctx)
        sl = k.sb("fsl", [P, 2, GT], ctx=ctx)
        hm = k.sb("fhm", [P, 2, GT], ctx=ctx)
        tmp = k.sb("ftmp", [P, B], ctx=ctx)
        block = ctx.enter_context(nc.Block())

        @block.sync
        def _(sp):
            def load_in(n, half):
                sp.dma_start(wi[:, half], wi_v[:, :, bass.ds(n * P + FF * half, P)]).then_inc(s_wi[half], 16)

            def load_out(n, j):
                sp.dma_start(wo[:, j], wo_v[bass.ds(n, 1), :, :].rearrange("o p n -> (o p) n")).then_inc(s_wo[j], 16)

            for half in range(2):
                load_in(0, half)
            for j in range(2):
                load_out(j, j)
            for half in range(2):
                sp.wait_ge(s_wl, half + 1)
                load_in(1, half)
            with sp.Fori(1, NS) as i:
                for half in range(2):
                    sp.wait_ge(s_wl, i * 4 + (half - 1))
                    load_in(i * 2, half)
                sp.wait_ge(s_ol, i * 2 - 1)
                load_out(i * 2, 0)
                for half in range(2):
                    sp.wait_ge(s_wl, i * 4 + (half + 1))
                    load_in(i * 2 + 1, half)
                sp.wait_ge(s_ol, i * 2)
                load_out(i * 2 + 1, 1)

        @block.tensor
        def _(pe):
            with pe.Fori(0, NS) as i:
                for u in range(6):
                    j, g = u // NG, u % NG
                    t = slice(GT * g, GT * g + GT)
                    if g == 0:
                        pe.wait_ge(s_wl, i * 4 + (2 * j + 2))
                    pe.wait_ge(s_hm, i * 6 + (u + 1))
                    for half in range(2):
                        for kk in range(DK):
                            mm = mm3(pe, k.bank[2 * (u % 2) + half][:, 0:GT], (wiH[:, j, half, kk, :], wiL[:, j, half, kk, :]),
                                     (uH[:, kk, t], uL[:, kk, t]), kk == 0, kk == DK - 1)
                    mm.then_inc(s_hf, 1)
                pe.wait_ge(s_ol, i * 2 + 2)
                for g in range(NG):
                    t = slice(GT * g, GT * g + GT)
                    pe.wait_ge(s_hl, i * 6 + (NG + g + 2))
                    for c in range(DK):
                        n = DK * g + c
                        pe.wait_ge(s_x, i * 24 + (max(n - 3, 0) + 1))
                        for j in range(2):
                            mm = mm3(pe, k.bank[4 + n % 4][:, 0:GT], (woH[:, j, P * c:P * c + P], woL[:, j, P * c:P * c + P]),
                                     (hH[:, j, t], hL[:, j, t]), j == 0, j == 1)
                        mm.then_inc(s_yf, 1)

        @block.scalar
        def _(act):
            def round_in(n, slot, half):
                act.wait_ge(s_wi[half], n * 16 + 16)
                act.activation(wiH[:, slot, half], wi[:, half], ACT.Copy).then_inc(s_wh, 1)

            def segment(i, last):
                for u in range(6):
                    j, g = u // NG, u % NG
                    act.wait_ge(s_hm, i * 6 + (u + 1))
                    act.wait_ge(s_hf, i * 6 + (u + 1))
                    act.activation(sl[:, u % 2, :], k.bank[2 * (u % 2)][:, 0:GT], ACT.Silu).then_inc(s_silu, 1)
                    if g < 2 and not (last and j == 1):
                        round_in(i * 2 + (j + 1), 1 - j, g)
                    if u in (2, 3):
                        act.wait_ge(s_wo[u - 2], i * 16 + 16)
                        act.activation(woH[:, u - 2], wo[:, u - 2], ACT.Copy).then_inc(s_oh, 1)

            for half in range(2):
                round_in(0, 0, half)
            with act.Fori(0, NS - 1) as i:
                segment(i, False)
            segment(NS - 1, True)

        @block.vector
        def _(dve):
            def rest_in(n, slot, half):
                dve.wait_ge(s_wh, n * 2 + (half + 1))
                dve.tensor_tensor(wiL[:, slot, half], wi[:, half], wiH[:, slot, half], ALU.subtract).then_inc(s_wl, 1)

            def segment(i, last):
                for u in range(6):
                    j, g = u // NG, u % NG
                    t = slice(GT * g, GT * g + GT)
                    dve.wait_ge(s_silu, i * 6 + (u + 1))
                    dve.wait_ge(s_hl, i * 6 + (u + 1))
                    dve.tensor_tensor(hm[:, u % 2, :], k.bank[2 * (u % 2) + 1][:, 0:GT], sl[:, u % 2, :], ALU.mult).then_inc(s_hm, 1)
                    dve.wait_ge(s_hm, i * 6 + (u + 3))
                    dve.tensor_copy(hH[:, j, t], hm[:, u % 2, :]).then_inc(s_hh, 1)
                    dve.wait_ge(s_hh, i * 6 + (u + 1))
                    dve.tensor_tensor(hL[:, j, t], hm[:, u % 2, :], hH[:, j, t], ALU.subtract).then_inc(s_hl, 1)
                    if g < 2 and not (last and j == 1):
                        rest_in(i * 2 + (j + 1), 1 - j, g)
                    if u in (2, 3):
                        dve.wait_ge(s_oh, i * 2 + (u - 1))
                        dve.tensor_tensor(woL[:, u - 2], wo[:, u - 2], woH[:, u - 2], ALU.subtract).then_inc(s_ol, 1)
                for g in range(NG):
                    for c in range(DK):
                        n = DK * g + c
                        dve.wait_ge(s_yf, i * 24 + (n + 1))
                        add_gated(k, dve, xT, c, g, k.bank[4 + n % 4], 40, tmp, s_x, s_xs, i * 16 + (2 * c + 1))

            for half in range(2):
                rest_in(0, 0, half)
            with dve.Fori(0, NS - 1) as i:
                segment(i, False)
            segment(NS - 1, True)


def store_y(k, yT):
    nc = k.nc
    s_t, s_c, s_o = k.sem("s_y_t"), k.sem("s_y_c"), [k.sem(f"s_y_o{j}") for j in range(2)]
    with ExitStack() as ctx:
        yr = k.sb("yr", [P, 2, D], ctx=ctx)
        block = ctx.enter_context(nc.Block())

        @block.tensor
        def _(pe):
            for f in range(2 * (NTI + 1)):
                ti, half = f // 2, f % 2
                m = P if ti < NTI else B
                if f >= 4:
                    pe.wait_ge(s_c, f - 3)
                for q in range(4):
                    mm = pe.transpose(k.bank[f % 4][0:m, P * q:P * q + P], yT[:, 4 * half + q, P * ti:P * ti + m], k.ident[:, :])
                mm.then_inc(s_t, 1)

        @block.vector
        def _(dve):
            for f in range(2 * (NTI + 1)):
                ti, half = f // 2, f % 2
                m = P if ti < NTI else B
                dve.wait_ge(s_t, f + 1)
                if ti >= 2 and half == 0:
                    dve.wait_ge(s_o[ti % 2], 16 * (ti // 2))
                dve.tensor_copy(yr[0:m, ti % 2, 512 * half:512 * half + 512], k.bank[f % 4][0:m, :]).then_inc(s_c, 1)

        @block.sync
        def _(sp):
            for ti in range(NTI + 1):
                sp.wait_ge(s_c, 2 * ti + 2)
                if ti < NTI:
                    sp.dma_start(k.o["y_prompt"][0, P * ti:P * ti + P, :], yr[:, ti % 2, :]).then_inc(s_o[ti % 2], 16)
                else:
                    sp.dma_start(k.o["y_sample"].rearrange("b o d -> (b o) d"), yr[0:B, ti % 2, :]).then_inc(s_o[ti % 2], 16)
            sp.wait_ge(s_o[0], 16 * 5)
            sp.wait_ge(s_o[1], 16 * 4)


def build(nc, ins, outs):
    k = Core(nc, ins, outs)
    with k.ctx:
        shared_buffers(k)
        k.xT_d = k.dram("xT_d", (P, DK, TT))
        k.uT_d = k.dram("uT_d", (P, DK, TT))
        with ExitStack() as ctx:
            k.pt = k.sb("pt", [1, B * NPAGES], I32, ctx=ctx)
            k.raw = k.sb("raw", [P, 2, 4, STRIDE, P], ctx=ctx)
            k.s_pt = k.lasting_sem("s_pt")
            k.s_page = [[k.lasting_sem(f"s_page{kv}{nt}") for nt in range(4)] for kv in range(2)]
            k.cw1 = k.sb("cw1", [P, 2, 2, 8, CH], ctx=ctx)
            k.cw2 = k.sb("cw2", [P, 2, 2, HD], ctx=ctx)
            k.perow = k.sb("perow", [32, P], ctx=ctx)
            k.cT = k.sb("cT", [P, DK, 9], ctx=ctx)
            k.wada = k.sb("wada", [P, 4, DK, P], ctx=ctx)
            k.s_w1, k.s_w2, k.s_pe = (k.lasting_sem(x) for x in ("s_cw1", "s_cw2", "s_cpe"))
            k.s_ada = [k.lasting_sem(f"s_ada{j}") for j in range(4)]
            setup(k)
            k.stage_done()
            cache_compress(k)
            k.stage_done()
        with ExitStack() as actx:
            k.hbT = k.sb("hbT", [P, MH, TT], ctx=actx)
            k.small = k.sb("small", [P, NTI, 32], ctx=actx)
            k.small_s = k.sb("small_s", [B, 32], ctx=actx)
            k.qTs = k.sb("qTs", [P, 4, B], ctx=actx)
            with ExitStack() as ctx:
                k.uT = k.sb("uT", [P, DK, TT], ctx=ctx)
                k.mw = k.sb("mw", [P, 2, DK, 512], ctx=ctx)
                k.s_mw = [k.lasting_sem(f"s_mw{j}") for j in range(2)]
                with ExitStack() as xctx:
                    xT = k.sb("xT", [P, DK, TT], ctx=xctx)
                    load_x(k, xT)
                    k.stage_done()
                    norm(k, "mix", xT, 0, k.uT, keep=k.xT_d, keep_dst=k.uT_d)
                    k.stage_done()
                k.qbT = k.sb("qbT", [P, MH, TT], ctx=ctx)
                k.kbT = k.sb("kbT", [P, MH, TT], ctx=ctx)
                k.kb = k.sb("kb", [P, NTI, 512], ctx=ctx)
                k.kb_s = k.sb("kb_s", [B, 512], ctx=ctx)
                k.vb = k.sb("vb", [P, NTI, MH, MD + 1], ctx=ctx)
                k.vb_s = k.sb("vb_s", [B, MH, MD + 1], ctx=ctx)
                mlstm_project(k)
                k.stage_done()
                mlstm_scan(k)
                k.stage_done()
                mlstm_decode(k)
                k.stage_done()
            k.oaT = k.sb("oaT", [P, 4, TT], ctx=actx)
            with ExitStack() as dctx:
                k.kcT = k.sb("kcT", [P, B, NPIECE], ctx=dctx)
                k.vc = k.sb("vc", [P, B, 4, P], ctx=dctx)
                k.s_kcv = k.lasting_sem("s_kcv")
                with ExitStack() as ctx:
                    k.qT = k.sb("qT", [P, 4, TT], ctx=ctx)
                    k.kv = k.sb("kv", [P, NTI, 768], ctx=ctx)
                    k.ksT = k.sb("ksT", [P, T], ctx=ctx)
                    k.kwT = k.sb("kwT", [P, T], ctx=ctx)
                    k.kcpT = k.sb("kcpT", [P, T // STRIDE], ctx=ctx)
                    k.vcp = k.sb("vcp", [T // STRIDE, P], ctx=ctx)
                    nsa_project(k)
                    k.stage_done()
                    prompt_compress(k)
                    k.stage_done()
                    prompt_attention(k)
                    k.stage_done()
                decode_attention(k)
                k.stage_done()
            mixT = k.sb("mixT", [P, DK, TT], ctx=actx)
            merge(k, mixT)
            k.stage_done()
            mix_out(k, mixT)
            k.stage_done()
        with ExitStack() as ctx:
            xT = k.sb("xT2", [P, DK, TT], ctx=ctx)
            with ExitStack() as uctx:
                uH = k.sb("u2H", [P, DK, TT], F32R, ctx=uctx)
                uL = k.sb("u2L", [P, DK, TT], F32R, ctx=uctx)
                with ExitStack() as nctx:
                    uT = k.sb("u2T", [P, DK, TT], ctx=nctx)
                    norm(k, "ffn", xT, 1, uT, load=k.xT_d)
                    k.stage_done()
                    split(k, uT, uH, uL)
                    k.stage_done()
                ffn(k, xT, uH, uL)
                k.stage_done()
            uT = k.sb("yT", [P, DK, TT], ctx=ctx)
            norm(k, "final", xT, 2, uT)
            k.stage_done()
            store_y(k, uT)
            k.stage_done()


_INS = ["x_prompt", "x_sample", "c_prompt", "c_sample", "cache_nsa_kv", "cache_nsa_win", "state_mlstm_C",
        "state_mlstm_n", "state_mlstm_m", "page_table", "rel_bias", "w_ada", "b_ada", "norm_mix_g",
        "norm_ffn_g", "w_in", "mlstm_gate_b", "cmp_pe", "cmp_w1", "cmp_w2", "mlstm_norm_g", "w_branch_a",
        "w_branch_b", "w_out", "w_ffn_in", "w_ffn_out", "w_ada_final", "b_ada_final", "norm_final_g"]
_OUTS = [("y_prompt", (1, T, D)), ("y_sample", (B, 1, D)),
         ("kv_prompt", (1, 1, T, 4, G, HD)), ("kv_sample", (1, B, 1, 4, G, HD)),
         ("win_prompt", (1, 1, WIN, 2, G, HD)), ("win_sample", (1, B, WIN, 2, G, HD)),
         ("C_prompt", (1, 1, MH, MD, MD)), ("n_prompt", (1, 1, MH, MD)), ("m_prompt", (1, 1, MH)),
         ("C_sample", (1, B, MH, MD, MD)), ("n_sample", (1, B, MH, MD)), ("m_sample", (1, B, MH))]


def kernel(**inputs):
    import numpy as _np
    import concourse.bacc as _bacc
    from concourse import mybir as _mybir
    from concourse.bass_utils import run_bass_kernel_spmd as _run

    nc = _bacc.Bacc("TRN2", target_bir_lowering=False, num_devices=1)
    arrays, ins, outs = {}, {}, {}
    for name in _INS:
        a = _np.ascontiguousarray(inputs[name])
        arrays[f"in_{name}"] = a
        ins[name] = nc.dram_tensor(f"in_{name}", a.shape, _mybir.dt.from_np(a.dtype), kind="ExternalInput").ap()
    for name, shape in _OUTS:
        outs[name] = nc.dram_tensor(f"out_{name}", shape, F32, kind="ExternalOutput").ap()
    build(nc, ins, outs)
    r = _run(nc, [arrays], core_ids=[0])
    return tuple(r.results[0][f"out_{name}"] for name, _ in _OUTS)
```
